# Optimizing a Trainium2 kernel written in Bass

```python
import math
import jax, jax.numpy as jnp
from jax import lax
import numpy as np

D_MODEL = 1024
BATCH = 1
SEQ = 512
DEPTH = 2

N_EVEN = (DEPTH + 1) // 2
N_ODD = DEPTH // 2
EPS = 1e-6
ROPE_THETA = 10000.0
BLOCK = 128

A_HEADS = 8
A_KV_HEADS = 2
A_GROUP = A_HEADS // A_KV_HEADS
A_HEAD_DIM = D_MODEL // 16
A_WINDOW = 128
A_WIDTH = A_HEADS * A_HEAD_DIM
A_KV_WIDTH = A_KV_HEADS * A_HEAD_DIM
B_WIDTH = D_MODEL // 2
POOL_WINDOWS = (2, 4, 8, 16)
B_GROUPS = len(POOL_WINDOWS)
B_GROUP_DIM = B_WIDTH // B_GROUPS
EVEN_IN = A_WIDTH + 2 * A_KV_WIDTH + B_WIDTH
C_HEADS = 8
C_NOPE = 64
C_ROPE = 32
C_VDIM = 64
C_Q_RANK = D_MODEL // 4
C_KV_RANK = D_MODEL // 8
C_WIDTH = C_HEADS * C_VDIM
D_WIDTH = D_MODEL // 2
D_BLOCKS = 8
D_BLOCK_DIM = D_WIDTH // D_BLOCKS
CONV_WIDTH = 4
LRU_C = 8.0
ODD_IN = C_Q_RANK + C_KV_RANK + C_ROPE + 2 * D_WIDTH
D_FF = 4 * D_MODEL


F32 = jnp.float32

def rmsnorm(x, g):
    xf = x.astype(F32)
    y = xf * lax.rsqrt(jnp.mean(xf * xf, axis=-1, keepdims=True) + EPS)
    return (y * g.astype(F32)).astype(x.dtype)

def rope(x):
    S, d = x.shape[1], x.shape[-1]
    half = d // 2
    inv = ROPE_THETA ** (-jnp.arange(half, dtype=F32) / half)
    ang = jnp.arange(S, dtype=F32)[:, None] * inv[None, :]
    shape = (1, S) + (1,) * (x.ndim - 3) + (half,)
    cos = jnp.cos(ang).reshape(shape)
    sin = jnp.sin(ang).reshape(shape)
    xf = x.astype(F32)
    x1, x2 = xf[..., :half], xf[..., half:]
    return jnp.concatenate([x1 * cos - x2 * sin, x2 * cos + x1 * sin], axis=-1).astype(x.dtype)

def windowed_gqa(q, k, v, sink):
    Bsz, S = q.shape[0], q.shape[1]
    nb = S // BLOCK
    qb = q.reshape(Bsz, nb, BLOCK, A_KV_HEADS, A_GROUP, A_HEAD_DIM)

    def band(t):
        tp = jnp.pad(t, ((0, 0), (BLOCK, BLOCK), (0, 0), (0, 0)))
        tp = tp.reshape(Bsz, nb + 2, BLOCK, A_KV_HEADS, A_HEAD_DIM)
        return jnp.concatenate([tp[:, :-2], tp[:, 1:-1], tp[:, 2:]], axis=2)

    kb, vb = band(k), band(v)
    s = jnp.einsum('bnqhgd,bnjhd->bnhgqj', qb, kb).astype(F32) * (A_HEAD_DIM ** -0.5)
    blk = jnp.arange(nb)[:, None, None]
    qpos = blk * BLOCK + jnp.arange(BLOCK)[None, :, None]
    kpos = (blk - 1) * BLOCK + jnp.arange(3 * BLOCK)[None, None, :]
    valid = (jnp.abs(kpos - qpos) <= A_WINDOW) & (kpos >= 0) & (kpos < S)
    s = jnp.where(valid[None, :, None, None], s, -jnp.inf)
    sk = sink.astype(F32).reshape(1, 1, A_KV_HEADS, A_GROUP, 1, 1)
    m = jnp.maximum(jnp.max(s, axis=-1, keepdims=True), sk)
    p = jnp.exp(s - m)
    p = p / (jnp.sum(p, axis=-1, keepdims=True) + jnp.exp(sk - m))
    out = jnp.einsum('bnhgqj,bnjhd->bnqhgd', p.astype(v.dtype), vb)
    return out.reshape(Bsz, S, A_WIDTH)

def multiscale_pool(u, w_pool, pool_scale):
    Bsz, S = u.shape[0], u.shape[1]
    uf = u.astype(F32).reshape(Bsz, S, B_GROUPS, B_GROUP_DIM)
    cs = jnp.pad(jnp.cumsum(uf, axis=1), ((0, 0), (1, 0), (0, 0), (0, 0)))
    t = jnp.arange(S)
    outs = []
    for g, w in enumerate(POOL_WINDOWS):
        half = w // 2
        lo = jnp.clip(t - half, 0, S)
        hi = jnp.clip(t + half, 0, S)
        win_sum = cs[:, hi, g] - cs[:, lo, g]
        cnt = (hi - lo).astype(F32)[None, :, None]
        outs.append(win_sum / cnt - uf[:, :, g])
    d = jnp.stack(outs, axis=2)
    y = jnp.einsum('bsgi,gij->bsgj', d, w_pool.astype(F32)).reshape(Bsz, S, B_WIDTH)
    return (y * pool_scale.astype(F32)).astype(u.dtype)

def dense_mla(qn, qr, kn, kr, v):
    Bsz, S = qn.shape[0], qn.shape[1]
    nb = S // BLOCK
    scale = (C_NOPE + C_ROPE) ** -0.5

    def blocks(t):
        return jnp.moveaxis(t.reshape((Bsz, nb, BLOCK) + t.shape[2:]), 1, 0)

    def one(args):
        qn_b, qr_b = args
        s = (jnp.einsum('bqhd,bkhd->bhqk', qn_b, kn) + jnp.einsum('bqhr,bkr->bhqk', qr_b, kr)).astype(F32) * scale
        p = jax.nn.softmax(s, axis=-1).astype(v.dtype)
        return jnp.einsum('bhqk,bkhd->bqhd', p, v)

    out = lax.map(one, (blocks(qn), blocks(qr)))
    return jnp.moveaxis(out, 0, 1).reshape(Bsz, S, C_WIDTH)

def _lin_combine(left, right):
    a1, b1 = left
    a2, b2 = right
    return a1 * a2, a2 * b1 + b2

def rglru_block(xr, xg, conv_w, conv_b, wa, ba, wx, bx, lam):
    Bsz, S = xr.shape[0], xr.shape[1]
    left = CONV_WIDTH // 2
    xp = jnp.pad(xr, ((0, 0), (left, CONV_WIDTH - 1 - left), (0, 0)))
    xc = conv_b + conv_w[0] * xp[:, 0:S]
    for j in range(1, CONV_WIDTH):
        xc = xc + conv_w[j] * xp[:, j:j + S]
    xcf = xc.astype(F32)
    xblk = xcf.reshape(Bsz, S, D_BLOCKS, D_BLOCK_DIM)
    hs = []
    for dirn in range(2):
        r = jax.nn.sigmoid(jnp.einsum('bsni,nij->bsnj', xblk, wa[dirn].astype(F32)).reshape(Bsz, S, D_WIDTH) + ba[dirn].astype(F32))
        i = jax.nn.sigmoid(jnp.einsum('bsni,nij->bsnj', xblk, wx[dirn].astype(F32)).reshape(Bsz, S, D_WIDTH) + bx[dirn].astype(F32))
        log_a = -LRU_C * r * jax.nn.softplus(-lam[dirn].astype(F32))
        a = jnp.exp(log_a)
        b = jnp.sqrt(-jnp.expm1(2.0 * log_a)) * (i * xcf)
        _, h = lax.associative_scan(_lin_combine, (a, b), axis=1, reverse=(dirn == 1))
        hs.append(h)
    y = (hs[0] + hs[1]) * jax.nn.gelu(xg.astype(F32))
    return y.astype(xr.dtype)

def even_mixer(h, w_in, sink, w_pool, pool_scale, w_out):
    Bsz, S = h.shape[0], h.shape[1]
    z = h @ w_in
    q, k, v, u = jnp.split(z, [A_WIDTH, A_WIDTH + A_KV_WIDTH, A_WIDTH + 2 * A_KV_WIDTH], axis=-1)
    q = rope(q.reshape(Bsz, S, A_HEADS, A_HEAD_DIM))
    k = rope(k.reshape(Bsz, S, A_KV_HEADS, A_HEAD_DIM))
    v = v.reshape(Bsz, S, A_KV_HEADS, A_HEAD_DIM)
    ya = windowed_gqa(q, k, v, sink)
    yb = multiscale_pool(u, w_pool, pool_scale)
    return jnp.concatenate([ya, yb], axis=-1) @ w_out

def odd_mixer(h, w_in, g_cq, w_uq, g_ckv, w_ukv, conv_w, conv_b, wa, ba, wx, bx, lam, w_out):
    Bsz, S = h.shape[0], h.shape[1]
    z = h @ w_in
    i1 = C_Q_RANK
    i2 = i1 + C_KV_RANK
    i3 = i2 + C_ROPE
    i4 = i3 + D_WIDTH
    cq, ckv, kr, xr, xg = jnp.split(z, [i1, i2, i3, i4], axis=-1)
    q = (rmsnorm(cq, g_cq) @ w_uq).reshape(Bsz, S, C_HEADS, C_NOPE + C_ROPE)
    qn, qr = q[..., :C_NOPE], rope(q[..., C_NOPE:])
    kv = (rmsnorm(ckv, g_ckv) @ w_ukv).reshape(Bsz, S, C_HEADS, C_NOPE + C_VDIM)
    kn, v = kv[..., :C_NOPE], kv[..., C_NOPE:]
    yc = dense_mla(qn, qr, kn, rope(kr), v)
    yd = rglru_block(xr, xg, conv_w, conv_b, wa, ba, wx, bx, lam)
    return jnp.concatenate([yc, yd], axis=-1) @ w_out

def sq_relu_mlp(h, w1, w2):
    u = jax.nn.relu(h @ w1)
    return (u * u) @ w2

def first_inputs(seed: int = 0) -> dict:
    key = jax.random.key(seed)
    ks = iter(jax.random.split(key, 40))

    def nrm(shape, fan_in):
        return jax.random.normal(next(ks), shape, F32) * (fan_in ** -0.5)

    def gain(shape):
        return 1.0 + 0.02 * jax.random.normal(next(ks), shape, F32)

    def bias(shape):
        return 0.01 * jax.random.normal(next(ks), shape, F32)

    x = jax.random.normal(next(ks), (BATCH, SEQ, D_MODEL), F32)
    u = jax.random.uniform(next(ks), (N_ODD, 2, D_WIDTH), F32, 0.9, 0.999)
    a0 = u ** (1.0 / LRU_C)
    lam = jnp.log(a0) - jnp.log1p(-a0)
    return {
        "x": x,
        "e_norm_mix": gain((N_EVEN, D_MODEL)),
        "e_w_in": nrm((N_EVEN, D_MODEL, EVEN_IN), D_MODEL),
        "e_sink": 0.5 * jax.random.normal(next(ks), (N_EVEN, A_HEADS), F32),
        "e_w_pool": nrm((N_EVEN, B_GROUPS, B_GROUP_DIM, B_GROUP_DIM), B_GROUP_DIM),
        "e_pool_scale": gain((N_EVEN, B_WIDTH)),
        "e_w_out": nrm((N_EVEN, D_MODEL, D_MODEL), D_MODEL),
        "o_norm_mix": gain((N_ODD, D_MODEL)),
        "o_w_in": nrm((N_ODD, D_MODEL, ODD_IN), D_MODEL),
        "o_g_cq": gain((N_ODD, C_Q_RANK)),
        "o_w_uq": nrm((N_ODD, C_Q_RANK, C_HEADS * (C_NOPE + C_ROPE)), C_Q_RANK),
        "o_g_ckv": gain((N_ODD, C_KV_RANK)),
        "o_w_ukv": nrm((N_ODD, C_KV_RANK, C_HEADS * (C_NOPE + C_VDIM)), C_KV_RANK),
        "o_conv_w": nrm((N_ODD, CONV_WIDTH, D_WIDTH), CONV_WIDTH),
        "o_conv_b": bias((N_ODD, D_WIDTH)),
        "o_lru_wa": nrm((N_ODD, 2, D_BLOCKS, D_BLOCK_DIM, D_BLOCK_DIM), D_BLOCK_DIM),
        "o_lru_ba": bias((N_ODD, 2, D_WIDTH)),
        "o_lru_wx": nrm((N_ODD, 2, D_BLOCKS, D_BLOCK_DIM, D_BLOCK_DIM), D_BLOCK_DIM),
        "o_lru_bx": bias((N_ODD, 2, D_WIDTH)),
        "o_lru_lambda": lam,
        "o_w_out": nrm((N_ODD, D_MODEL, D_MODEL), D_MODEL),
        "norm_mlp": gain((DEPTH, D_MODEL)),
        "w_mlp1": nrm((DEPTH, D_MODEL, D_FF), D_MODEL),
        "w_mlp2": nrm((DEPTH, D_FF, D_MODEL), D_FF),
        "final_norm": gain((D_MODEL,)),
    }

def first_block(x, e_norm_mix, e_w_in, e_sink, e_w_pool, e_pool_scale, e_w_out,
              o_norm_mix, o_w_in, o_g_cq, o_w_uq, o_g_ckv, o_w_ukv, o_conv_w, o_conv_b,
              o_lru_wa, o_lru_ba, o_lru_wx, o_lru_bx, o_lru_lambda, o_w_out,
              norm_mlp, w_mlp1, w_mlp2, final_norm):
    for layer in range(DEPTH):
        if layer % 2 == 0:
            e = layer // 2
            h = rmsnorm(x, e_norm_mix[e])
            x = x + even_mixer(h, e_w_in[e], e_sink[e], e_w_pool[e], e_pool_scale[e], e_w_out[e])
        else:
            o = layer // 2
            h = rmsnorm(x, o_norm_mix[o])
            x = x + odd_mixer(h, o_w_in[o], o_g_cq[o], o_w_uq[o], o_g_ckv[o], o_w_ukv[o],
                              o_conv_w[o], o_conv_b[o], o_lru_wa[o], o_lru_ba[o], o_lru_wx[o],
                              o_lru_bx[o], o_lru_lambda[o], o_w_out[o])
        x = x + sq_relu_mlp(rmsnorm(x, norm_mlp[layer]), w_mlp1[layer], w_mlp2[layer])
    return rmsnorm(x, final_norm)


DEPTH_2 = 1

PLE_DIM = 256
D_MIX = D_MODEL
HEAD_DIM = 64
RMS_EPS = 1e-6

CONV_W = D_MIX // 4
CONV_K = 3

NSA_HEADS = 6
NSA_KV_HEADS = 2
NSA_GROUP = NSA_HEADS // NSA_KV_HEADS
NSA_W = NSA_HEADS * HEAD_DIM
NSA_KV_W = NSA_KV_HEADS * HEAD_DIM
CMP_BLOCK = 32
CMP_STRIDE = 16
SLC_BLOCK = 64
SLC_TOPK = 16
WIN = 512
Q_BLOCK = 128
FORCE_SCORE = 1e4

DIL_PAIRS = ((128, 1), (512, 4), (2048, 16))
DIL_HEADS_PER_PAIR = 2
DIL_HEADS = DIL_HEADS_PER_PAIR * len(DIL_PAIRS)
DIL_W = DIL_HEADS * HEAD_DIM
DIL_BLOCK = 128

IN_SIZES = ((CONV_W,) * 4
            + (NSA_W,) + (NSA_KV_W,) * 6
            + (NSA_HEADS * 3, NSA_W)
            + (DIL_W,) * 4)
D_IN = sum(IN_SIZES)


def _rmsnorm(x, g):
    x32 = x.astype(jnp.float32)
    y = x32 * lax.rsqrt(jnp.mean(x32 * x32, axis=-1, keepdims=True) + RMS_EPS)
    return (y * g.astype(jnp.float32)).astype(x.dtype)

def _masked_softmax(s, mask):
    s = jnp.where(mask, s.astype(jnp.float32), -jnp.inf)
    m = jnp.max(s, axis=-1, keepdims=True)
    m = jnp.where(jnp.isfinite(m), m, 0.0)
    e = jnp.where(mask, jnp.exp(s - m), 0.0)
    den = jnp.sum(e, axis=-1, keepdims=True)
    return e / jnp.maximum(den, 1e-30), m, den

def _short_conv(u, w, b):
    y = lax.conv_general_dilated(
        u, w[:, None, :].astype(u.dtype), window_strides=(1,), padding=((CONV_K - 1, 0),),
        dimension_numbers=("NWC", "WIO", "NWC"), feature_group_count=u.shape[-1])
    return y + b.astype(u.dtype)

def _nsa(q, kc_raw, vc_raw, ks_raw, vs_raw, kw_raw, vw_raw, gates, pe, w1, w2):
    B, T, G, R, E = q.shape
    scale = E ** -0.5
    n_cmp = (T - CMP_BLOCK) // CMP_STRIDE + 1
    cmp_start = jnp.arange(n_cmp) * CMP_STRIDE
    cmp_idx = cmp_start[:, None] + jnp.arange(CMP_BLOCK)[None, :]

    def compress(a, pe_, w1_, w2_):
        blk = a[:, cmp_idx] + pe_[None, None, :, None, :].astype(a.dtype)
        flat = jnp.moveaxis(blk, 3, 2).reshape(B, n_cmp, G, CMP_BLOCK * E)
        return jax.nn.silu(flat @ w1_) @ w2_

    k_cmp = compress(kc_raw, pe[0], w1[0], w2[0])
    v_cmp = compress(vc_raw, pe[1], w1[1], w2[1])
    cmp_last = cmp_start + CMP_BLOCK - 1
    n_slc = T // SLC_BLOCK
    slc_start = jnp.arange(n_slc) * SLC_BLOCK
    overlap = ((cmp_start[:, None] < slc_start[None, :] + SLC_BLOCK)
               & (cmp_start[:, None] + CMP_BLOCK > slc_start[None, :])).astype(jnp.float32)
    k_slc = ks_raw.reshape(B, n_slc, SLC_BLOCK, G, E).transpose(0, 3, 1, 2, 4)
    v_slc = vs_raw.reshape(B, n_slc, SLC_BLOCK, G, E).transpose(0, 3, 1, 2, 4)
    top = min(SLC_TOPK, n_slc)
    b_ix = jnp.arange(B)[:, None, None, None]
    g_ix = jnp.arange(G)[None, None, :, None]
    k_win = jnp.pad(kw_raw, ((0, 0), (WIN, 0), (0, 0), (0, 0)))
    v_win = jnp.pad(vw_raw, ((0, 0), (WIN, 0), (0, 0), (0, 0)))

    def block(qi):
        q0 = qi * Q_BLOCK
        t = q0 + jnp.arange(Q_BLOCK)
        qb = lax.dynamic_slice_in_dim(q, q0, Q_BLOCK, axis=1)
        gb = lax.dynamic_slice_in_dim(gates, q0, Q_BLOCK, axis=1)
        s_c = jnp.einsum("bqgrd,bngd->bqgrn", qb, k_cmp) * scale
        m_c = (cmp_last[None, :] <= t[:, None])[None, :, None, None, :]
        p_c, _, _ = _masked_softmax(s_c, m_c)
        o_c = jnp.einsum("bqgrn,bngd->bqgrd", p_c.astype(qb.dtype), v_cmp)
        imp = jnp.einsum("bqgrn,ns->bqgs", p_c, overlap)
        blk = jnp.arange(n_slc)[None, :]
        cur = (t // SLC_BLOCK)[:, None]
        forced = (blk == 0) | (blk == cur) | (blk == cur - 1)
        causal = blk * SLC_BLOCK <= t[:, None]
        imp = jnp.where(forced[None, :, None, :], FORCE_SCORE, imp)
        imp = jnp.where(causal[None, :, None, :], imp, -1.0)
        _, sel = lax.top_k(imp, top)
        k_sel = k_slc[b_ix, g_ix, sel]
        v_sel = v_slc[b_ix, g_ix, sel].reshape(B, Q_BLOCK, G, top * SLC_BLOCK, E)
        pos = sel[..., None] * SLC_BLOCK + jnp.arange(SLC_BLOCK)
        m_s = (pos <= t[None, :, None, None, None]).reshape(B, Q_BLOCK, G, 1, top * SLC_BLOCK)
        s_s = jnp.einsum("bqgrd,bqgkld->bqgrkl", qb, k_sel).reshape(
            B, Q_BLOCK, G, R, top * SLC_BLOCK) * scale
        p_s, _, _ = _masked_softmax(s_s, m_s)
        o_s = jnp.einsum("bqgrk,bqgkd->bqgrd", p_s.astype(qb.dtype), v_sel)
        kw = lax.dynamic_slice_in_dim(k_win, q0, WIN + Q_BLOCK, axis=1)
        vw = lax.dynamic_slice_in_dim(v_win, q0, WIN + Q_BLOCK, axis=1)
        kpos = q0 - WIN + jnp.arange(WIN + Q_BLOCK)
        dist = t[:, None] - kpos[None, :]
        m_w = ((dist >= 0) & (dist < WIN) & (kpos[None, :] >= 0))[None, :, None, None, :]
        s_w = jnp.einsum("bqgrd,bkgd->bqgrk", qb, kw) * scale
        p_w, _, _ = _masked_softmax(s_w, m_w)
        o_w = jnp.einsum("bqgrk,bkgd->bqgrd", p_w.astype(qb.dtype), vw)
        return gb[..., 0:1] * o_c + gb[..., 1:2] * o_s + gb[..., 2:3] * o_w

    out = lax.map(block, jnp.arange(T // Q_BLOCK))
    return jnp.moveaxis(out, 0, 1).reshape(B, T, G * R * E)

def _dilated_group(q, k, v, window, dil):
    B, T, H, E = q.shape
    L = T // dil
    Lp = -(-L // DIL_BLOCK) * DIL_BLOCK
    nb = Lp // DIL_BLOCK
    steps = window // dil

    def sub(a):
        a = a.reshape(B, L, dil, H, E).transpose(0, 2, 3, 1, 4)
        a = jnp.pad(a, ((0, 0), (0, 0), (0, 0), (0, Lp - L), (0, 0)))
        return a.reshape(B, dil, H, nb, DIL_BLOCK, E)

    def with_prev(a):
        prev = jnp.concatenate([jnp.zeros_like(a[:, :, :, :1]), a[:, :, :, :-1]], axis=3)
        return jnp.concatenate([prev, a], axis=4)

    qs = sub(q)
    kc = with_prev(sub(k))
    vc = with_prev(sub(v))
    s = jnp.einsum("bdhnqe,bdhnke->bdhnqk", qs, kc) * (E ** -0.5)
    a_i = jnp.arange(DIL_BLOCK)
    c_i = jnp.arange(2 * DIL_BLOCK)
    dist = a_i[:, None] + DIL_BLOCK - c_i[None, :]
    j = jnp.arange(nb)[:, None, None] * DIL_BLOCK - DIL_BLOCK + c_i[None, None, :]
    mask = (dist[None] >= 0) & (dist[None] <= steps) & (j >= 0)
    p, m, den = _masked_softmax(s, mask)
    o = jnp.einsum("bdhnqk,bdhnke->bdhnqe", p.astype(v.dtype), vc)
    lse = (m + jnp.log(den))[..., 0]
    o = o.reshape(B, dil, H, Lp, E)[:, :, :, :L].transpose(0, 3, 1, 2, 4).reshape(B, T, H, E)
    lse = lse.reshape(B, dil, H, Lp)[:, :, :, :L].transpose(0, 3, 1, 2).reshape(B, T, H)
    return o, lse

def _dilated_mixer(q, k, v):
    B, T, _, E = q.shape
    outs, lses = [], []
    for gi, (window, dil) in enumerate(DIL_PAIRS):
        sl = slice(gi * DIL_HEADS_PER_PAIR, (gi + 1) * DIL_HEADS_PER_PAIR)
        o, lse = _dilated_group(q[:, :, sl], k[:, :, sl], v[:, :, sl], window, dil)
        outs.append(o)
        lses.append(lse)
    alpha = jax.nn.softmax(jnp.stack(lses, axis=0), axis=0)
    y = jnp.concatenate([alpha[gi][..., None].astype(outs[gi].dtype) * outs[gi]
                         for gi in range(len(DIL_PAIRS))], axis=2)
    return y.reshape(B, T, DIL_W)

def second_inputs(seed: int = 0) -> dict:
    key = jax.random.key(seed)
    ks = jax.random.split(key, 13)
    f32 = jnp.float32
    x = jax.random.normal(ks[0], (BATCH, SEQ, D_MODEL), f32)
    p = jax.random.normal(ks[1], (DEPTH_2, BATCH, SEQ, PLE_DIM), f32)
    norm_mix = 1.0 + 0.05 * jax.random.normal(ks[2], (DEPTH_2, D_MODEL), f32)
    w_in = jax.random.normal(ks[3], (DEPTH_2, D_MODEL, D_IN), f32) * D_MODEL ** -0.5
    conv_w = jax.random.normal(ks[4], (DEPTH_2, CONV_K, CONV_W), f32) * CONV_K ** -0.5
    conv_b = 0.02 * jax.random.normal(ks[5], (DEPTH_2, CONV_W), f32)
    cmp_pe = 0.5 * jax.random.normal(ks[6], (DEPTH_2, 2, CMP_BLOCK, HEAD_DIM), f32)
    cmp_w1 = jax.random.normal(ks[7], (DEPTH_2, 2, CMP_BLOCK * HEAD_DIM, HEAD_DIM), f32) * (CMP_BLOCK * HEAD_DIM) ** -0.5
    cmp_w2 = jax.random.normal(ks[8], (DEPTH_2, 2, HEAD_DIM, HEAD_DIM), f32) * HEAD_DIM ** -0.5
    w_out = jax.random.normal(ks[9], (DEPTH_2, D_MIX, D_MODEL), f32) * D_MIX ** -0.5
    w_ple_gate = jax.random.normal(ks[10], (DEPTH_2, D_MODEL, D_MODEL), f32) * D_MODEL ** -0.5
    w_ple_proj = jax.random.normal(ks[11], (DEPTH_2, PLE_DIM, D_MODEL), f32) * PLE_DIM ** -0.5
    norm_final = 1.0 + 0.05 * jax.random.normal(ks[12], (D_MODEL,), f32)
    return {"x": x, "p": p, "norm_mix": norm_mix, "w_in": w_in, "conv_w": conv_w,
            "conv_b": conv_b, "cmp_pe": cmp_pe, "cmp_w1": cmp_w1, "cmp_w2": cmp_w2,
            "w_out": w_out, "w_ple_gate": w_ple_gate, "w_ple_proj": w_ple_proj,
            "norm_final": norm_final}

def second_block(x, p, norm_mix, w_in, conv_w, conv_b, cmp_pe, cmp_w1, cmp_w2,
              w_out, w_ple_gate, w_ple_proj, norm_final):
    B, T, _ = x.shape
    E = HEAD_DIM
    split_points = np.cumsum(IN_SIZES)[:-1].tolist()
    h = x
    for i in range(DEPTH_2):
        xn = _rmsnorm(h, norm_mix[i])
        u = xn @ w_in[i]
        (a_b, a_c, a_h, a_z,
         n_q, n_kc, n_vc, n_ks, n_vs, n_kw, n_vw, n_g, n_z,
         d_q, d_k, d_v, d_z) = jnp.split(u, split_points, axis=-1)
        y_a = a_b * _short_conv(a_c * a_h, conv_w[i], conv_b[i]) * jax.nn.silu(a_z)
        kv = lambda a: a.reshape(B, T, NSA_KV_HEADS, E)
        gates = jax.nn.sigmoid(n_g.astype(jnp.float32)).astype(u.dtype).reshape(
            B, T, NSA_KV_HEADS, NSA_GROUP, 3)
        y_b = _nsa(n_q.reshape(B, T, NSA_KV_HEADS, NSA_GROUP, E), kv(n_kc), kv(n_vc),
                   kv(n_ks), kv(n_vs), kv(n_kw), kv(n_vw), gates,
                   cmp_pe[i], cmp_w1[i], cmp_w2[i]) * jax.nn.silu(n_z)
        hd = lambda a: a.reshape(B, T, DIL_HEADS, E)
        y_c = _dilated_mixer(hd(d_q), hd(d_k), hd(d_v)) * jax.nn.silu(d_z)
        h = h + jnp.concatenate([y_a, y_b, y_c], axis=-1) @ w_out[i]
        gate = jax.nn.sigmoid((h @ w_ple_gate[i]).astype(jnp.float32)).astype(h.dtype)
        h = h + gate * (p[i] @ w_ple_proj[i])
    return _rmsnorm(h, norm_final)


def setup_inputs(seed=0):
    out = dict(first_inputs(seed))
    for name, value in second_inputs(seed + 1).items():
        if name != "x":
            out[name + "_2"] = value
    return out


def reference(
    x, e_norm_mix, e_w_in, e_sink, e_w_pool, e_pool_scale, e_w_out, o_norm_mix, o_w_in, o_g_cq,
    o_w_uq, o_g_ckv, o_w_ukv, o_conv_w, o_conv_b, o_lru_wa, o_lru_ba, o_lru_wx, o_lru_bx,
    o_lru_lambda, o_w_out, norm_mlp, w_mlp1, w_mlp2, final_norm, p_2, norm_mix_2, w_in_2,
    conv_w_2, conv_b_2, cmp_pe_2, cmp_w1_2, cmp_w2_2, w_out_2, w_ple_gate_2, w_ple_proj_2,
    norm_final_2,
):
    x = first_block(
        x, e_norm_mix, e_w_in, e_sink, e_w_pool, e_pool_scale, e_w_out, o_norm_mix, o_w_in,
        o_g_cq, o_w_uq, o_g_ckv, o_w_ukv, o_conv_w, o_conv_b, o_lru_wa, o_lru_ba, o_lru_wx,
        o_lru_bx, o_lru_lambda, o_w_out, norm_mlp, w_mlp1, w_mlp2, final_norm,
    )
    return second_block(
        x, p_2, norm_mix_2, w_in_2, conv_w_2, conv_b_2, cmp_pe_2, cmp_w1_2, cmp_w2_2, w_out_2,
        w_ple_gate_2, w_ple_proj_2, norm_final_2,
    )


_drawn_inputs = setup_inputs


def setup_inputs(seed=0):
    import zlib

    import numpy as np

    out = dict(_drawn_inputs(seed))
    spreads = {}
    factors = {'e_norm_mix': 4.451,
     'e_sink': 8.0,
     'e_pool_scale': 4.474,
     'o_norm_mix': 3.407,
     'o_g_cq': 8.0,
     'o_g_ckv': 8.0,
     'o_conv_b': 10.306,
     'o_lru_ba': 64.0,
     'o_lru_bx': 64.0,
     'final_norm': 7.958,
     'conv_b_2': 28.294,
     'norm_mlp': 6.632,
     'norm_mix_2': 5.162,
     'cmp_pe_2': 23.27,
     'p_2': 8.0,
     'w_ple_gate_2': 8.0,
     'w_ple_proj_2': 8.0}
    for name, (base, spread) in spreads.items():
        noise = np.random.default_rng([zlib.crc32(name.encode()), seed]).standard_normal(out[name].shape)
        drawn = base * np.exp(spread * noise) if base else spread * noise
        out[name] = __import__('jax').numpy.asarray(drawn.astype(out[name].dtype))
    for name, factor in factors.items():
        out[name] = (out[name] * factor).astype(out[name].dtype)
    return out
```

```python
from contextlib import ExitStack

import concourse.bass as bass
import numpy as np
from concourse import mybir

F32 = mybir.dt.float32
F32R = mybir.dt.float32r
ALU = mybir.AluOpType
ACT = mybir.ActivationFunctionType
AX = mybir.AxisListType.X

P = 128
SEQ = 512
D = 1024
KT = D // P
TT = SEQ // P
FF = 4 * D
SUBS = 8
RING = 4
EPS = 1e-6
NEG = -1e30
EVEN_HEADS, EVEN_GROUP = 8, 4
LRU_C = 8.0
MLA_HEADS, NOPE, ROPE = 8, 64, 32
NSA_R, HD = 3, 64
CMP_BLOCK, CMP_STRIDE = 32, 16
N_CMP = (SEQ - CMP_BLOCK) // CMP_STRIDE + 1
DILATIONS = (1, 4, 16)

STAGES = [("ein", 10, 8), ("pool", 4, 1), ("eout", 8, 8), ("up0", 32, 8), ("down0", 8, 32),
          ("oin", 12, 8), ("lru", 16, 1), ("uq", 8, 2), ("ukn", 8, 1), ("uv", 4, 1), ("oout", 8, 8),
          ("up1", 32, 8), ("down1", 8, 32), ("zin", 33, 8), ("cmp", 2, 32), ("out2", 8, 8), ("ple", 16, 5)]
TILE0, SUB0, NTILES = {}, {}, {}
_t = _s = 0
for _name, _n, _k in STAGES:
    TILE0[_name], SUB0[_name], NTILES[_name] = _t, _s, _n
    _t += _n
    _s += -(-_n * _k // SUBS) * SUBS
NBLOCKS = _s // SUBS
assert NBLOCKS % RING == 0



def block_ends():
    out, used = [], 0
    for name, tiles, k in STAGES:
        ends, s, t = {}, SUB0[name], TILE0[name]
        if name.startswith("down"):
            ends = {s + tiles * k - tiles + i: t + i + 1 for i in range(tiles)}
        else:
            for i in range(tiles):
                s += k if name != "ple" else (8, 2)[i % 2]
                ends[s - 1] = t + i + 1
        end = SUB0[name] + tiles * k
        for b in range(SUB0[name] // SUBS, -(-end // SUBS)):
            last = min(SUBS * (b + 1), end) - 1
            if last in ends:
                out.append(("tile", ends[last]))
            else:
                used += 1
                out.append(("block", used))
    return out


BLOCK_END = block_ends()
assert len(BLOCK_END) == NBLOCKS

SPLITS = [("even", 8), ("pool", 4), ("pooled", 4), ("eattn", 4), ("mlp0", 8), ("odd", 8), ("xc", 4),
          ("cq", 2), ("ckv", 1), ("lru", 4), ("mattn", 4), ("mlp1", 8), ("mix2", 8), ("cmp", 4),
          ("conv2", 2), ("nsa", 3), ("dil", 3), ("ple", 8)]
SPLIT0 = {}
_t = 0
for _name, _n in SPLITS:
    SPLIT0[_name] = _t
    _t += _n

NORMS = [("even", 8), ("mlp0", 8), ("odd", 8), ("cq", 2), ("ckv", 1), ("mlp1", 8), ("final", 8),
         ("mix2", 8), ("out", 8)]
NORM, SQ0, NORM_TILES = {}, {}, dict(NORMS)
_t = 0
for _i, (_name, _n) in enumerate(NORMS):
    NORM[_name], SQ0[_name] = _i, _t
    _t += _n

PARAM_COLS = [("g_even", 8), ("g_mlp0", 8), ("g_odd", 8), ("g_mlp1", 8), ("g_final", 8), ("g_mix2", 8),
              ("g_out", 8), ("g_cq", 2), ("g_ckv", 1), ("pool_scale", 4), ("conv_w", 16), ("conv_b", 4),
              ("gate_b", 16), ("lam", 8), ("conv2_w", 6), ("conv2_b", 2), ("pe", 64), ("sink", 8),
              ("w2k", 128), ("w2v", 128)]
CONST_COLS = [("causal", 640), ("band", 384), ("near", 256), ("blocks", 128), ("cmpmask", TT * 32),
              ("ident", 128), ("rot_even", 128), ("rot_mla", 128), ("late", 1), ("ones", 1), ("eps", 1)]


def columns(cols):
    at, out = 0, {}
    for name, n in cols:
        out[name] = (at, at + n)
        at += n
    return out, at


PCOL, NPARAM = columns(PARAM_COLS)
CCOL, NCONST = columns(CONST_COLS)


def even_units():
    return [dict(j=j, g=g, qt=qt, lo=max(0, qt - 1), hi=min(TT, qt + 2), group=j)
            for j in range(EVEN_GROUP) for g in range(2) for qt in range(TT)]


def mla_units():
    return [dict(h=h, qt=qt, group=h // 2) for h in range(MLA_HEADS) for qt in range(TT)]


def nsa_units():
    return [dict(r=r, g=g, qt=qt, branch=b, group=r)
            for r in range(NSA_R) for qt in range(TT) for g in range(2) for b in range(3)]


def dilated_units():
    return [dict(gi=gi, tile=t, g=g, group=NSA_R + gi) for gi in range(3) for t in range(TT) for g in range(2)]


EVEN, MLA, LAST = even_units(), mla_units(), nsa_units() + dilated_units()
UNIT0 = {"even": 0, "mla": len(EVEN), "last": len(EVEN) + len(MLA)}


def program(nc, x_t, stream, params, consts, ropes, invcnt, p_t, out_t):
    with ExitStack() as ctx:
        def sb(name, shape, dt=F32):
            return ctx.enter_context(nc.sbuf_tensor(name, shape, dt))

        def sem(name):
            return ctx.enter_context(nc.semaphore(name))

        arena = sb("arena", [P, 49, SEQ])
        base = nc.sbuf_base - 49 * SEQ * 4
        opA = nc.alloc_sbuf_tensor_at("opA", [P, 2, KT, SEQ], F32R, offset=base)
        opC = nc.alloc_sbuf_tensor_at("opC", [P, 2, KT, SEQ], F32R, offset=base + 33 * SEQ * 4)
        x = sb("x", [P, KT, SEQ])
        raw = sb("raw", [P, RING, D])
        w_hi = sb("w_hi", [P, RING, D], F32R)
        w_lo = sb("w_lo", [P, RING, D], F32R)
        mlp_op = sb("mlp_op", [P, 2, 2, SEQ], F32R)
        more = nc.alloc_sbuf_tensor_at("more", [P, 2, SEQ], F32, offset=nc.sbuf_base - 4 * SEQ * 4)
        tmp = sb("tmp", [P, 6, SEQ])
        rms = sb("rms", [P, 3, SEQ])
        rope = sb("rope", [P, 2, SEQ])
        con = sb("con", [P, NCONST])
        par = sb("par", [P, NPARAM])
        negm = sb("negm", [P, 96])
        den = sb("den", [P, 96])
        rden = sb("rden", [P, 96])
        gates = sb("gates", [P, TT * 32])
        small = sb("small", [P, 16, 8])
        std = sb("std", [P, len(NORMS), TT])
        rtok = sb("rtok", [P, len(NORMS), TT])
        hid = sb("hid", [P, 4, 32])
        cmpk = sb("cmpk", [P, 32])
        cmpv = sb("cmpv", [32, P])
        bank = [ctx.enter_context(nc.psum_tensor(f"bank{i}", [P, SEQ], F32)) for i in range(8)]

        raw_in = [sem(f"raw_in{i}") for i in range(RING)]
        hi_made, lo_made, block_used = sem("hi_made"), sem("lo_made"), sem("block_used")
        acc_full, z_ready = sem("acc_full"), sem("z_ready")
        split_hi, split_lo = sem("split_hi"), sem("split_lo")
        sq_ready, sq_used = sem("sq_ready"), sem("sq_used")
        std_ready, rtok_ready, rms_full, rms_ready = sem("std_ready"), sem("rtok_ready"), sem("rms_full"), sem("rms_ready")
        x_in, par_in, con_in, rope_in, inv_in, p_in = (sem(s) for s in ("x_in", "par_in", "con_in", "rope_in", "inv_in", "p_in"))
        rot_full, roped = sem("rot_full"), sem("roped")
        turned, v_tok = sem("turned"), sem("v_tok")
        s_full, masked, sink_put, exp_done = sem("s_full"), sem("masked"), sem("sink_put"), sem("exp_done")
        p_ready, pt_full, pt_ready, pv_done = sem("p_ready"), sem("pt_full"), sem("pt_ready"), sem("pv_done")
        o_out = sem("o_out")
        relu_made, mlp_hi, mlp_lo = sem("relu_made"), sem("mlp_hi"), sem("mlp_lo")
        src_ready = sem("src_ready")
        key_rope = sem("key_rope")
        gate_sig, decay_made, beta_sq, beta_made, gelu_made = (sem(s) for s in ("gate_sig", "decay_made", "beta_sq", "beta_made", "gelu_made"))
        lam_act, sp_made = sem("lam_act"), sem("sp_made")
        silu_made, hid_sig, hid_made, cmp_full, cmp_ready = (sem(s) for s in ("silu_made", "hid_sig", "hid_made", "cmp_full", "cmp_ready"))
        gates_turned, gates_ready = sem("gates_turned"), sem("gates_ready")
        log_den, lse_ready, lse_full, lse_exp = sem("log_den"), sem("lse_ready"), sem("lse_full"), sem("lse_exp")
        ls_max, ple_sig = sem("ls_max"), sem("ple_sig")
        vstep, y_ready, stored = sem("vstep"), sem("y_ready"), sem("stored")

        def c(name, lo=0, hi=None):
            a, b = CCOL[name]
            return con[:, a + lo:(b if hi is None else a + hi)]

        def g(name, i=0, n=1):
            return par[:, PCOL[name][0] + i:PCOL[name][0] + i + n]

        ident = c("ident")

        def z(i, layer):
            return arena[:, i + 16 * (layer % 2), :]

        def Z(layer):
            return lambda i: z(i, layer)

        z0, z1, z2 = Z(0), Z(1), Z(2)
        splits = {}

        def place(name, op, first, n):
            for i in range(n):
                splits[name, i] = (op[:, 0, first + i, :], op[:, 1, first + i, :])

        for name, op, first, n in (
                ("even", opC, 0, 8), ("pool", opC, 0, 4), ("pooled", opC, 4, 4), ("eattn", opC, 0, 4),
                ("mlp0", opA, 0, 8), ("odd", opA, 0, 8), ("xc", opA, 0, 4), ("cq", opA, 4, 2), ("ckv", opA, 6, 1),
                ("lru", opA, 4, 4), ("mattn", opA, 0, 4), ("mlp1", opC, 0, 8), ("mix2", opC, 0, 8),
                ("conv2", opC, 0, 2), ("nsa", opC, 2, 3), ("dil", opC, 5, 3), ("ple", opA, 0, 8)):
            place(name, op, first, n)
        cmp_half = SEQ + CMP_STRIDE
        for kv in range(2):
            for half in range(2):
                splits["cmp", 2 * kv + half] = tuple(
                    opC[:, s, :, :].rearrange("p a b -> p (a b)")[:, (2 * kv + half) * 2 * SEQ:][:, 0:cmp_half]
                    for s in range(2))

        def tmp_flat(i):
            return tmp[:, 2 * (i % 2):2 * (i % 2) + 2, :].rearrange("p a b -> p (a b)")[:, 0:cmp_half]

        def dilate(ap, r):
            return ap.rearrange("p (a r) -> p r a", r=r)

        def residues(ap, r):
            return ap.rearrange("p (r a) -> p r a", r=r)

        def unit(u, family):
            if family == "even":
                lo, hi, b = u["lo"], u["hi"], slice(64 * u["g"], 64 * u["g"] + 64)
                off = P * (lo - u["qt"] + 1)
                return dict(q=z0(u["j"])[b, P * u["qt"]:P * (u["qt"] + 1)], k=z0(4)[b, P * lo:P * hi], n=P * (hi - lo),
                            mask=c("band", off, off + P * (hi - lo)), scale=HD ** -0.5, sink=4 * u["g"] + u["j"],
                            v=[z0(5)[:, P * t + 64 * u["g"]:P * t + 64 * u["g"] + 64] for t in range(lo, hi)],
                            out=(64 * u["g"], P * u["qt"]), gate=None)
            if family == "mla":
                h, qt = u["h"], u["qt"]
                at = 64 * (h % 2)
                return dict(q=z1(12 + h)[0:96, P * qt:P * (qt + 1)], k=z1(20 + h)[0:96, :], n=SEQ,
                            mask=c("causal", 0, SEQ), scale=(NOPE + ROPE) ** -0.5, sink=None,
                            v=[z1(28 + h // 2)[:, P * t + at:P * t + at + 64] for t in range(TT)],
                            out=(at, P * qt), gate=None)
            b = slice(64 * u["g"], 64 * u["g"] + 64)
            if "r" in u:
                qt, br = u["qt"], u["branch"]
                n = N_CMP if br == 0 else P * (qt + 1)
                col = 32 * qt + 9 * u["g"] + 3 * u["r"] + br
                return dict(q=z2(8 + u["r"])[b, P * qt:P * (qt + 1)], n=n,
                            k=cmpk[b, 0:N_CMP] if br == 0 else z2(11 + 2 * br)[b, 0:n],
                            mask=c("cmpmask", 32 * qt, 32 * qt + N_CMP) if br == 0 else c("causal", 640 - n, 640),
                            scale=HD ** -0.5, sink=None,
                            v=[cmpv[0:N_CMP, b]] if br == 0 else
                              [z2(12 + 2 * br)[:, P * t + b.start:P * t + b.stop] for t in range(qt + 1)],
                            out=(b.start, P * qt), gate=gates[:, col:col + 1], first=br == 0, last=br == 2)
            gi, t = u["gi"], u["tile"]
            lo = t - 1 if gi == 0 and t else t
            mask = [c("near", 0 if t else P, 2 * P), c("causal", 512, 640), c("blocks")][gi]
            return dict(q=z2(21 + gi)[b, P * t:P * (t + 1)], k=z2(24 + gi)[b, P * lo:P * (t + 1)], n=P * (t + 1 - lo),
                        mask=mask, scale=HD ** -0.5, sink=None,
                        v=[z2(27 + gi)[:, P * s + b.start:P * s + b.stop] for s in range(lo, t + 1)],
                        out=(b.start, P * t), gate=None)

        FAMILY = {"even": [unit(u, "even") | {"group": u["group"]} for u in EVEN],
                  "mla": [unit(u, "mla") | {"group": u["group"]} for u in MLA],
                  "last": [unit(u, "last") | {"group": u["group"]} for u in LAST]}
        GROUP0 = {"even": 0, "mla": 4, "last": 8}

        def last_of(family, group):
            return max(i for i, u in enumerate(FAMILY[family]) if u["group"] == group)

        NORM_LAG, TURN_LAG, VALUE_LAG = 2, 3, 4

        def probs(i, n):
            return more[:, i % 4 - 2, 0:n] if i % 4 >= 2 else tmp[:, 2 + i % 4, 0:n]

        def groups_after(family, step):
            n = max(u["group"] for u in FAMILY[family]) + 1
            return [k for k in range(n) if last_of(family, k) + VALUE_LAG + 1 == step]

        block = ctx.enter_context(nc.Block())

        @block.sync
        def _(sp):
            for n in range(RING):
                sp.dma_start(raw[:, n, :], stream[n]).then_inc(raw_in[n], 16)
            with sp.Fori(1, NBLOCKS // RING) as i:
                for j in range(RING):
                    sp.wait_ge(lo_made, RING * i + (j + 1 - RING))
                    sp.dma_start(raw[:, j, :], stream[RING * i + j]).then_inc(raw_in[j], 16)
            for m in range(KT):
                sp.wait_ge(y_ready, m + 1)
                sp.dma_start(out_t[P * m:P * (m + 1), :], arena[:, m, :]).then_inc(stored, 16)
            sp.wait_ge(stored, 16 * KT)

        @block.gpsimd
        def _(pool):
            with pool.Fori(0, NBLOCKS // RING) as i:
                for j in range(RING):
                    pool.wait_ge(hi_made, RING * i + (j + 1))
                    pool.tensor_tensor(w_lo[:, j, :], raw[:, j, :], w_hi[:, j, :].bitcast(F32),
                                       ALU.subtract).then_inc(lo_made, 1)

        @block.tensor
        def _(pe):
            seen = {"split": 0}

            def need_split(name, i):
                n = SPLIT0[name] + i + 1
                if n > seen["split"]:
                    pe.wait_ge(split_lo, n)
                    seen["split"] = n

            def product(out, slot, k, hi, lo, first, last):
                wh, wl = w_hi[:, slot, P * k:P * (k + 1)], w_lo[:, slot, P * k:P * (k + 1)]
                pe.matmul(out, wh, hi, start=first, stop=False)
                pe.matmul(out, wh, lo, start=False, stop=False)
                return pe.matmul(out, wl, hi, start=False, stop=last)

            def linear(name, operand, n=SEQ, subs=None, after=None):
                t0, s, ntiles = TILE0[name], SUB0[name], NTILES[name]
                nsub = {a: k for a, _, k in STAGES}[name]
                count = subs or (lambda i: nsub)
                end = s + sum(count(i) for i in range(ntiles))
                for i in range(ntiles):
                    t = t0 + i
                    if t >= 2:
                        pe.wait_ge(z_ready, t - 1)
                    for k in range(count(i)):
                        if s % SUBS == 0:
                            pe.wait_ge(lo_made, s // SUBS + 1)
                        hi, lo = operand(i, k)
                        mm = product(bank[6 + t % 2][:, 0:n], s // SUBS % RING, s % SUBS, hi, lo, k == 0, k == count(i) - 1)
                        s += 1
                        if (s % SUBS == 0 or s == end) and k < count(i) - 1:
                            mm.then_inc(block_used, 1)
                    mm.then_inc(acc_full, 1)
                    if after:
                        after(i)

            def split_operand(name):
                def operand(i, k):
                    need_split(name, k)
                    return splits[name, k]
                return operand

            def norm_sums(name, tiles=None):
                for m in tiles or range(NORM_TILES[name]):
                    pe.wait_ge(sq_ready, SQ0[name] + m + 1)
                    for t in range(TT):
                        mm = pe.matmul(bank[0][:, t:t + 1], tmp[:, 4 + (SQ0[name] + m) % 2, P * t:P * (t + 1)], c("ones"),
                                       start=(m == 0 and t == 0), stop=(m == NORM_TILES[name] - 1), skip_group_check=True)
                    mm.then_inc(sq_used, 1)

            def norm_spread(name):
                pe.wait_ge(rtok_ready, NORM[name] + 1)
                for t in range(TT):
                    mm = pe.matmul(bank[1][:, P * t:P * (t + 1)], rtok[:, NORM[name], t:t + 1].broadcast_to([P, P]), ident,
                                   start=True, stop=True)
                mm.then_inc(rms_full, 1)

            def behind(name):
                return lambda i: norm_sums(name, [i - 2]) if i >= 2 else None

            turn_count = [0]

            def rotate(first, tiles, rot, m):
                for i, (tile, ready) in enumerate(tiles):
                    pe.wait_ge(z_ready, ready)
                    if i >= 2:
                        pe.wait_ge(roped, first + i - 1)
                    pe.matmul(bank[2 + i % 2][0:m, :], rot[0:m, 0:m], tile[0:m, :], start=True, stop=True).then_inc(rot_full, 1)

            def turn_values(tiles):
                for i, (tile, ready) in enumerate(tiles):
                    pe.wait_ge(z_ready, ready)
                    if i >= 2:
                        pe.wait_ge(v_tok, turn_count[0] - 1)
                    for t in range(TT):
                        mm = pe.transpose(bank[4 + i % 2][:, P * t:P * (t + 1)], tile[:, P * t:P * (t + 1)], ident)
                    mm.then_inc(turned, 1)
                    turn_count[0] += 1

            def attention(family):
                units, u0 = FAMILY[family], UNIT0[family]
                n = len(units)
                for step in range(n + VALUE_LAG):
                    if step < n:
                        u, gu = units[step], u0 + step
                        if step >= 2:
                            pe.wait_ge(masked, gu - 1)
                        pe.matmul(bank[2 + step % 2][:, 0:u["n"]], u["q"], u["k"], start=True, stop=True).then_inc(s_full, 1)
                    i = step - TURN_LAG
                    if 0 <= i < n:
                        u, gu = units[i], u0 + i
                        pe.wait_ge(p_ready, gu + 1)
                        if i >= 2:
                            pe.wait_ge(pt_ready, gu - 1)
                        for a in range(0, u["n"], P):
                            w = min(P, u["n"] - a)
                            mm = pe.transpose(bank[4 + i % 2][0:w, a:a + P], probs(i, SEQ)[:, a:a + w], ident)
                        mm.then_inc(pt_full, 1)
                    i = step - VALUE_LAG
                    if i >= 0:
                        u, gu = units[i], u0 + i
                        pe.wait_ge(pt_ready, gu + 1)
                        grp = GROUP0[family] + u["group"]
                        if u["group"] >= 2 and units[i - 1]["group"] != u["group"]:
                            if family == "last":
                                pe.wait_ge(o_out, u["group"] - 1)
                            else:
                                pe.wait_ge(split_lo, SPLIT0["eattn" if family == "even" else "mattn"] + u["group"] - 1)
                        at, col = u["out"]
                        for b, v in enumerate(u["v"]):
                            kw = v.shape[0]
                            mm = pe.matmul(bank[grp % 2][at:at + 64, col:col + P], v,
                                           tmp[0:kw, 4 + i % 2, P * b:P * (b + 1)],
                                           start=(b == 0 and u.get("first", True)),
                                           stop=(b == len(u["v"]) - 1 and u.get("last", True)))
                        mm.then_inc(pv_done, 1)

            def mlp(layer):
                op, arena0 = f"mlp{layer}", 16 * ((layer + 1) % 2)
                t0, b0 = TILE0[f"up{layer}"], SUB0[f"up{layer}"] // SUBS
                need_split(op, KT - 1)

                def up(i, j):
                    t = RING * i + (t0 + j)
                    pe.wait_ge(z_ready, t - 1)
                    pe.wait_ge(lo_made, RING * i + (b0 + j + 1))
                    for k in range(KT):
                        mm = product(bank[6 + (t0 + j) % 2][:, :], (b0 + j) % RING, k, *splits[op, k], k == 0, k == KT - 1)
                    mm.then_inc(acc_full, 1)

                with pe.Fori(0, FF // P // RING) as i:
                    for j in range(RING):
                        up(i, j)

                b1 = b0 + FF // P
                t1 = t0 + FF // P

                def down(i, j, first, last):
                    pe.wait_ge(lo_made, RING * i + (b1 + j + 1))
                    pe.wait_ge(mlp_lo, RING * i + (layer * FF // P + j + 1))
                    for m in range(KT):
                        if first and m == 6:
                            pe.wait_ge(z_ready, t1)
                        mm = product(bank[m][:, :], (b1 + j) % RING, m, mlp_op[:, 0, j % 2, :], mlp_op[:, 1, j % 2, :], first, last)
                        if last:
                            mm.then_inc(acc_full, 1)
                    if not last:
                        mm.then_inc(block_used, 1)

                for j in range(RING):
                    down(0, j, j == 0, False)
                with pe.Fori(1, FF // P // RING - 1) as i:
                    for j in range(RING):
                        down(i, j, False, False)
                for j in range(RING):
                    down(FF // P // RING - 1, j, False, j == RING - 1)

            pe.wait_ge(con_in, 16)
            norm_sums("even")
            norm_spread("even")
            linear("ein", split_operand("even"))
            rotate(0, [(z0(i), TILE0["ein"] + i + 1) for i in range(5)], c("rot_even"), P)
            turn_values([(z0(5), TILE0["ein"] + 6)])
            linear("pool", lambda i, k: (need_split("pool", i), splits["pool", i])[1])
            pe.wait_ge(roped, 5)
            pe.wait_ge(v_tok, 1)
            attention("even")
            linear("eout", lambda i, k: (need_split("pooled" if k >= 4 else "eattn", k % 4),
                                         splits["pooled" if k >= 4 else "eattn", k % 4])[1],
                   after=behind("mlp0"))
            norm_sums("mlp0", [KT - 2, KT - 1])
            norm_spread("mlp0")
            mlp(0)

            norm_sums("odd")
            norm_spread("odd")
            linear("oin", split_operand("odd"))
            linear("lru", lambda i, k: (need_split("xc", i % 4), splits["xc", i % 4])[1])
            norm_sums("cq")
            norm_spread("cq")
            norm_sums("ckv")
            norm_spread("ckv")
            linear("uq", split_operand("cq"))
            linear("ukn", split_operand("ckv"))
            linear("uv", split_operand("ckv"))
            rotate(5, [(z1(3), TILE0["oin"] + 4)] + [(z1(12 + h), TILE0["uq"] + h + 1) for h in range(MLA_HEADS)],
                   c("rot_mla"), 96)
            turn_values([(z1(28 + i), TILE0["uv"] + i + 1) for i in range(4)])
            pe.wait_ge(roped, 14)
            pe.wait_ge(key_rope, MLA_HEADS)
            pe.wait_ge(v_tok, 5)
            attention("mla")
            linear("oout", lambda i, k: (need_split("lru" if k >= 4 else "mattn", k % 4),
                                         splits["lru" if k >= 4 else "mattn", k % 4])[1],
                   after=behind("mlp1"))
            norm_sums("mlp1", [KT - 2, KT - 1])
            norm_spread("mlp1")
            mlp(1)

            norm_sums("final")
            norm_spread("final")
            norm_sums("mix2")
            norm_spread("mix2")
            linear("zin", split_operand("mix2"))
            pe.wait_ge(silu_made, 1)
            for t in range(TT):
                mm = pe.transpose(bank[2][:, 32 * t:32 * (t + 1)], z2(17)[0:32, P * t:P * (t + 1)], ident[0:32, 0:32])
            mm.then_inc(gates_turned, 1)

            def cmp_operand(i, k):
                need_split("cmp", 2 * i + k // CMP_STRIDE)
                at = k if k < CMP_STRIDE else CMP_STRIDE + k % CMP_STRIDE
                return tuple(ap[:, at:at + 31 * CMP_STRIDE + 1:CMP_STRIDE] for ap in splits["cmp", 2 * i + k // CMP_STRIDE])

            turn_values([(z2(i), TILE0["zin"] + i + 1) for i in (14, 16, 27, 28, 29)])
            linear("cmp", cmp_operand, n=32)
            pe.wait_ge(hid_made, 1)
            pe.wait_ge(gates_ready, 1)
            pe.matmul(bank[2][:, 0:32], g("w2k", 0, P), hid[:, 0, :], start=True, stop=True).then_inc(cmp_full, 1)
            pe.wait_ge(hid_made, 2)
            pe.matmul(bank[3][0:32, 0:P], hid[:, 1, :], g("w2v", 0, P), start=True, stop=True).then_inc(cmp_full, 1)
            pe.wait_ge(cmp_ready, 2)
            pe.wait_ge(v_tok, 10)
            attention("last")
            pe.wait_ge(lse_ready, 1)
            for gi in range(3):
                for t in range(TT):
                    mm = pe.matmul(bank[2 + gi][:, P * t:P * (t + 1)],
                                   tmp[:, gi, P * t:P * (t + 1)], ident, start=True, stop=True)
                mm.then_inc(lse_full, 1)

            def out2_operand(i, k):
                name, j = ("conv2", k) if k < 2 else ("nsa", k - 2) if k < 5 else ("dil", k - 5)
                need_split(name, j)
                return splits[name, j]

            linear("out2", out2_operand)

            def ple_operand(i, k):
                if i % 2 == 0:
                    need_split("ple", k)
                    return splits["ple", k]
                pe.wait_ge(mlp_lo, 2 * FF // P + 2) if i == 1 and k == 0 else None
                return mlp_op[:, 0, k, :], mlp_op[:, 1, k, :]

            linear("ple", ple_operand, subs=lambda i: 2 if i % 2 else 8,
                   after=lambda i: norm_sums("out", [i // 2 - 1]) if i % 2 and i > 1 else None)
            norm_sums("out", [KT - 1])
            norm_spread("out")

        @block.scalar
        def _(act):
            prepared = [0]

            def prepare(n):
                while prepared[0] <= min(n, NBLOCKS - 1):
                    b = prepared[0]
                    act.wait_ge(raw_in[b % RING], 16 * (b // RING + 1))
                    if b >= RING:
                        what, count = BLOCK_END[b - RING]
                        act.wait_ge(acc_full if what == "tile" else block_used, count)
                    nc.scalar.activation(w_hi[:, b % RING, :], raw[:, b % RING, :], ACT.Copy).then_inc(hi_made, 1)
                    prepared[0] += 1

            def prepare_stage(name):
                i = [s[0] for s in STAGES].index(name)
                end = SUB0[STAGES[i + 1][0]] if i + 1 < len(STAGES) else NBLOCKS * SUBS
                prepare(end // SUBS - 1 + RING - 1)

            def hi_of(name, i, src, scale=1.0):
                nc.scalar.activation(splits[name, i][0], src, ACT.Copy, scale=scale).then_inc(split_hi, 1)

            def square(name, m, src):
                q = SQ0[name] + m
                if q >= 2:
                    act.wait_ge(sq_used, q - 1)
                nc.scalar.activation(tmp[:, 4 + q % 2, :], src, ACT.Square).then_inc(sq_ready, 1)

            def root(name, n):
                act.wait_ge(sq_used, SQ0[name] + NORM_TILES[name])
                nc.scalar.activation(std[:, NORM[name], :], bank[0][:, 0:TT], ACT.Sqrt, bias=c("eps"),
                                     scale=1.0 / n).then_inc(std_ready, 1)

            def norm(name, gain, ready, stage=None):
                for m in range(KT):
                    if stage:
                        prepare(SUB0[stage] // SUBS + m + RING - 1)
                    ready(m)
                    square(name, m, x[:, m, :])
                    if gain:
                        hi_of(name, m, x[:, m, :], g(gain, m))
                root(name, D)

            def rows(stage):
                return lambda m: act.wait_ge(z_ready, TILE0[stage] + m + 1)

            def attention(family, evacuate):
                units, u0 = FAMILY[family], UNIT0[family]
                n = len(units)
                for step in range(n + VALUE_LAG + 1):
                    if step < n:
                        u, gu = units[step], u0 + step
                        act.wait_ge(masked, gu + 1)
                        if u["sink"] is not None:
                            act.wait_ge(sink_put, gu + 1)
                        if step >= 4:
                            act.wait_ge(pt_full, gu - 3)
                        w = u["n"] + (u["sink"] is not None)
                        nc.scalar.activation(probs(step, w), tmp[:, step % 2, 0:w], ACT.Exp,
                                             bias=negm[:, step:step + 1], scale=-1.0,
                                             accum_out=den[:, step:step + 1]).then_inc(exp_done, 1)
                    i = step - TURN_LAG
                    if 0 <= i < n:
                        u, gu = units[i], u0 + i
                        act.wait_ge(pt_full, gu + 1)
                        if i >= 2:
                            act.wait_ge(pv_done, gu - 1)
                        w, m = (u["n"] + P - 1) // P * P, min(P, u["n"])
                        nc.scalar.activation(tmp[0:m, 4 + i % 2, 0:w], bank[4 + i % 2][0:m, 0:w],
                                             ACT.Copy).then_inc(pt_ready, 1)
                    for k in groups_after(family, step):
                        evacuate(k)

            def group_done(family, k):
                act.wait_ge(pv_done, UNIT0[family] + last_of(family, k) + 1)

            def mlp(layer):
                t0, b0 = TILE0[f"up{layer}"], SUB0[f"up{layer}"] // SUBS
                arena0 = 16 * ((layer + 1) % 2)
                used0 = BLOCK_END[b0 + FF // P][1] - 1
                prepare(b0 + RING - 2)

                def ahead(i, j, base, first=False):
                    b = base + j + RING - 1
                    act.wait_ge(raw_in[b % RING], 16 * i + 16 * (b // RING + 1))
                    if base == b0 or first:
                        act.wait_ge(acc_full, RING * i + (TILE0[f"up{layer}"] + base - b0 + j))
                    else:
                        act.wait_ge(block_used, RING * i + (used0 + j))
                    nc.scalar.activation(w_hi[:, b % RING, :], raw[:, b % RING, :], ACT.Copy).then_inc(hi_made, 1)

                with act.Fori(0, FF // P // RING) as i:
                    for j in range(RING):
                        ahead(i, j, b0)
                        t = RING * i + (t0 + j)
                        act.wait_ge(acc_full, t + 1)
                        act.wait_ge(z_ready, t - 1)
                        nc.scalar.activation(tmp[:, j % 2, :], bank[6 + (t0 + j) % 2][:, :], ACT.Relu).then_inc(relu_made, 1)

                b1, t1, k0 = b0 + FF // P, t0 + FF // P, layer * FF // P
                src = arena[:, arena0:arena0 + FF // P, :].rearrange("p a b -> p (a b)")
                for k in range(2):
                    act.wait_ge(z_ready, t0 + k + 1)
                    nc.scalar.activation(mlp_op[:, 0, k, :], src[:, SEQ * k:SEQ * (k + 1)], ACT.Copy).then_inc(mlp_hi, 1)

                def down(i, j):
                    ahead(i, j, b1)
                    act.wait_ge(z_ready, t1)
                    nc.scalar.activation(mlp_op[:, 0, (j + 1) % 2, :], src[:, bass.ds(SEQ * RING * i + SEQ * (j + 1), SEQ)],
                                         ACT.Copy).then_inc(mlp_hi, 1)

                for j in range(RING):
                    if j == 0:
                        ahead(0, 0, b1, True)
                    else:
                        down(0, j)
                with act.Fori(1, FF // P // RING - 1) as i:
                    for j in range(RING):
                        down(i, j)
                for j in range(RING):
                    if j < RING - 1:
                        down(FF // P // RING - 1, j)
                    else:
                        ahead(FF // P // RING - 1, j, b1)
                prepared[0] = b1 + FF // P + RING - 1

            act.dma_start(x[:, :, :], x_t.rearrange("(m p) n -> p m n", p=P)).then_inc(x_in, 16)
            act.dma_start(par[:, :], params).then_inc(par_in, 16)
            act.dma_start(con[:, :], consts).then_inc(con_in, 16)
            act.dma_start(rope[:, :, :], ropes[0]).then_inc(rope_in, 16)
            act.dma_start(arena[:, 29:33, :], invcnt).then_inc(inv_in, 16)
            act.wait_ge(par_in, 16)
            act.wait_ge(con_in, 16)
            nc.scalar.activation(small[:, 0, :], g("lam", 0, 8), ACT.Abs).then_inc(lam_act, 1)
            act.wait_ge(lam_act, 1)
            nc.scalar.activation(small[:, 1, :], small[:, 0, :], ACT.Exp, scale=-1.0).then_inc(lam_act, 1)
            act.wait_ge(x_in, 16)

            norm("even", "g_even", lambda m: None)
            prepare_stage("ein")
            for i in range(4):
                act.wait_ge(src_ready, i + 1)
                act.wait_ge(acc_full, TILE0["ein"] + 10)
                hi_of("pool", i, z0(14 + i))
            prepare_stage("pool")
            for i in range(4):
                act.wait_ge(z_ready, TILE0["pool"] + i + 1)
                hi_of("pooled", i, z0(10 + i))

            def even_out(k):
                if k == 0:
                    act.wait_ge(acc_full, TILE0["pool"] + 4)
                group_done("even", k)
                hi_of("eattn", k, bank[(GROUP0["even"] + k) % 2][:, :])

            attention("even", even_out)
            act.dma_start(rope[:, :, :], ropes[1]).then_inc(rope_in, 16)
            norm("mlp0", "g_mlp0", rows("eout"), "eout")
            mlp(0)

            norm("odd", "g_odd", rows("down0"))
            prepare_stage("oin")
            for i in range(4):
                act.wait_ge(src_ready, 4 + i + 1)
                act.wait_ge(acc_full, TILE0["oin"] + 12)
                hi_of("xc", i, z1(28 + i))
            prepare_stage("lru")
            for i in range(16):
                act.wait_ge(z_ready, TILE0["lru"] + i + 1)
                nc.scalar.activation(z1(12 + i), z1(12 + i), ACT.Sigmoid).then_inc(gate_sig, 1)
            act.wait_ge(sp_made, 2)

            def decay_tmp(u):
                return z1(4 + u) if u < 4 else tmp[:, u - 4, :]

            def gate_tile(kind, u):
                return z1(12 + 8 * (u // 4) + 4 * kind + u % 4)

            for u in range(8):
                act.wait_ge(gate_sig, 8 * (u // 4) + u % 4 + 1)
                nc.scalar.activation(decay_tmp(u), gate_tile(0, u), ACT.Exp, scale=small[:, 14, u:u + 1]).then_inc(decay_made, 1)
                nc.scalar.activation(gate_tile(0, u), gate_tile(0, u), ACT.Tanh, scale=small[:, 15, u:u + 1]).then_inc(decay_made, 1)
            for u in range(8):
                act.wait_ge(beta_sq, u + 1)
                nc.scalar.activation(decay_tmp(u), decay_tmp(u), ACT.Sqrt, scale=-1.0).then_inc(beta_made, 1)
            for j in range(4):
                nc.scalar.activation(z1(8 + j), z1(8 + j), ACT.Gelu_apprx_tanh).then_inc(gelu_made, 1)
            act.wait_ge(src_ready, 12)
            for m in range(2):
                square("cq", m, z1(m))
                hi_of("cq", m, z1(m), g("g_cq", m))
            root("cq", 2 * P)
            square("ckv", 0, z1(2))
            hi_of("ckv", 0, z1(2), g("g_ckv"))
            root("ckv", P)
            prepare_stage("uq")
            prepare_stage("ukn")
            prepare_stage("uv")
            act.wait_ge(roped, 6)
            for h in range(MLA_HEADS):
                act.wait_ge(z_ready, TILE0["ukn"] + h + 1)
                nc.scalar.activation(z1(20 + h)[64:96, :], z1(3)[64:96, :], ACT.Copy).then_inc(key_rope, 1)
            for i in range(4):
                act.wait_ge(acc_full, TILE0["uv"] + 4)
                hi_of("lru", i, z1(8 + i))

            def mla_out(k):
                group_done("mla", k)
                hi_of("mattn", k, bank[(GROUP0["mla"] + k) % 2][:, :])

            attention("mla", mla_out)
            norm("mlp1", "g_mlp1", rows("oout"), "oout")
            mlp(1)

            norm("final", None, rows("down1"))
            norm("mix2", "g_mix2", lambda m: act.wait_ge(src_ready, 12 + m + 1))
            prepare_stage("zin")
            act.wait_ge(z_ready, TILE0["zin"] + 33)
            nc.scalar.activation(z2(17)[0:32, :], z2(17)[0:32, :], ACT.Sigmoid).then_inc(silu_made, 1)
            for i in (6, 7, 18, 19, 20, 30, 31, 32):
                nc.scalar.activation(z2(i), z2(i), ACT.Silu).then_inc(silu_made, 1)
            for i in range(4):
                act.wait_ge(src_ready, 20 + i + 1)
                act.wait_ge(acc_full, TILE0["zin"] + 33)
                nc.scalar.activation(splits["cmp", i][0], tmp_flat(i), ACT.Copy).then_inc(split_hi, 1)
            prepare_stage("cmp")
            for i in range(2):
                act.wait_ge(z_ready, TILE0["cmp"] + i + 1)
                nc.scalar.activation(hid[:, 2 + i, :], hid[:, i, :], ACT.Sigmoid).then_inc(hid_sig, 1)
            for i in range(2):
                act.wait_ge(src_ready, 24 + i + 1)
                act.wait_ge(acc_full, TILE0["cmp"] + 2)
                hi_of("conv2", i, z2(4 + i))

            def last_out(k):
                if k < NSA_R:
                    act.wait_ge(o_out, k + 1)
                    hi_of("nsa", k, z2(18 + k))

            attention("last", last_out)
            first = 3 * TT * 2 * NSA_R
            nc.scalar.activation(rden[:, 0:24], den[:, first:first + 24], ACT.Ln).then_inc(log_den, 1)
            for gi in range(3):
                act.wait_ge(ls_max, gi + 1)
                nc.scalar.activation(z2(24 + gi), z2(24 + gi), ACT.Exp).then_inc(lse_exp, 1)
            for gi in range(3):
                act.wait_ge(src_ready, 26 + gi + 1)
                hi_of("dil", gi, z2(30 + gi))
            act.dma_start(arena[:, 24:26, :], p_t.rearrange("(m p) n -> p m n", p=P)).then_inc(p_in, 16)
            act.wait_ge(p_in, 16)
            for k in range(2):
                nc.scalar.activation(mlp_op[:, 0, k, :], arena[:, 24 + k, :], ACT.Copy).then_inc(mlp_hi, 1)
            for m in range(KT):
                prepare(SUB0["out2"] // SUBS + m + RING - 1)
                act.wait_ge(z_ready, TILE0["out2"] + m + 1)
                hi_of("ple", m, x[:, m, :])
            for m in range(KT):
                prepare((SUB0["ple"] + 10 * m + 9) // SUBS + RING - 1)
                act.wait_ge(z_ready, TILE0["ple"] + 2 * m + 1)
                nc.scalar.activation(tmp[:, m % 2, :], tmp[:, m % 2, :], ACT.Sigmoid).then_inc(ple_sig, 1)
                act.wait_ge(z_ready, TILE0["ple"] + 2 * m + 2)
                square("out", m, x[:, m, :])
            root("out", D)

        @block.vector
        def _(dve):
            steps = [0]

            def mark(ins):
                ins.then_inc(vstep, 1)
                steps[0] += 1
                return steps[0]

            def step(ins):
                dve.wait_ge(vstep, mark(ins))

            TTn, TS, STT = nc.vector.tensor_tensor, nc.vector.tensor_scalar, nc.vector.scalar_tensor_tensor

            def lo_of(name, i, src, scale=None):
                e = SPLIT0[name] + i
                dve.wait_ge(split_hi, e + 1)
                hi, lo = splits[name, i]
                if scale is None:
                    return TTn(lo, src, hi.bitcast(F32), ALU.subtract).then_inc(split_lo, 1)
                return STT(lo, src, scale, hi.bitcast(F32), ALU.mult, ALU.subtract).then_inc(split_lo, 1)

            def spread(name, slot=0):
                k = NORM[name]
                dve.wait_ge(std_ready, k + 1)
                nc.vector.reciprocal(rtok[:, k, :], std[:, k, :]).then_inc(rtok_ready, 1)
                dve.wait_ge(rms_full, k + 1)
                nc.vector.tensor_copy(rms[:, slot, :], bank[1][:, :]).then_inc(rms_ready, 1)
                dve.wait_ge(rms_ready, k + 1)

            def norm(name, gain):
                for m in range(KT):
                    lo_of(name, m, x[:, m, :], g(gain, m))
                spread(name)

            def taken(name, i):
                t = TILE0[name] + i
                dve.wait_ge(acc_full, t + 1)
                return bank[6 + t % 2]

            def scaled(name, i, out, slot=0, m=P):
                src = taken(name, i)
                TTn(out[0:m, :], src[0:m, :], rms[0:m, slot, :], ALU.mult).then_inc(z_ready, 1)

            def residual(name):
                for m in range(KT):
                    src = taken(name, m)
                    TTn(x[:, m, :], src[:, :], x[:, m, :], ALU.add).then_inc(z_ready, 1)

            def rotate(first, tiles, m):
                for i, tile in enumerate(tiles):
                    dve.wait_ge(rot_full, first + i + 1)
                    if i >= 2:
                        dve.wait_ge(roped, first + i - 1)
                    a, b = tmp[0:m, 2 * (i % 2), :], tmp[0:m, 2 * (i % 2) + 1, :]
                    mark(TTn(a, tile[0:m, :], rope[0:m, 0, :], ALU.mult))
                    step(TTn(b, bank[2 + i % 2][0:m, :], rope[0:m, 1, :], ALU.mult))
                    TTn(tile[0:m, :], a, b, ALU.add).then_inc(roped, 1)

            values = [0]

            def turn_values(tiles):
                for i, tile in enumerate(tiles):
                    values[0] += 1
                    dve.wait_ge(turned, values[0])
                    nc.vector.tensor_copy(tile, bank[4 + i % 2][:, :]).then_inc(v_tok, 1)

            def attention(family, evacuate):
                units, u0 = FAMILY[family], UNIT0[family]
                n = len(units)
                for s in range(n + VALUE_LAG + 1):
                    i = s - NORM_LAG
                    if 0 <= i < n:
                        dve.wait_ge(exp_done, u0 + i + 1)
                        inverted = mark(nc.vector.reciprocal(rden[:, i:i + 1], den[:, i:i + 1]))
                    if s < n:
                        u, gu = units[s], u0 + s
                        if s >= 2:
                            dve.wait_ge(exp_done, gu - 1)
                        if u["sink"] is not None:
                            col = small[:, 13, u["sink"]:u["sink"] + 1]
                            nc.vector.tensor_copy(tmp[:, s % 2, u["n"]:u["n"] + 1], col).then_inc(sink_put, 1)
                        dve.wait_ge(s_full, gu + 1)
                        nc.vector.tensor_tensor_reduce(
                            tmp[:, s % 2, 0:u["n"]], bank[2 + s % 2][:, 0:u["n"]], u["mask"], -u["scale"],
                            3e38 if u["sink"] is None else col, ALU.add, ALU.min, negm[:, s:s + 1]).then_inc(masked, 1)
                    if 0 <= i < n:
                        u = units[i]
                        dve.wait_ge(vstep, inverted)
                        pr = probs(i, u["n"])
                        if u["gate"] is None:
                            TS(pr, pr, rden[:, i:i + 1], None, ALU.mult).then_inc(p_ready, 1)
                        else:
                            TS(pr, pr, rden[:, i:i + 1], u["gate"], ALU.mult, ALU.mult).then_inc(p_ready, 1)
                    for k in groups_after(family, s):
                        evacuate(k)

            def group_bank(family, k):
                dve.wait_ge(pv_done, UNIT0[family] + last_of(family, k) + 1)
                return bank[(GROUP0[family] + k) % 2]

            def mlp(layer):
                t0 = TILE0[f"up{layer}"]
                arena0 = 16 * ((layer + 1) % 2)
                u = arena[:, arena0:arena0 + FF // P, :].rearrange("p a b -> p (a b)")
                step(TTn(rms[:, 1, :], rms[:, 0, :], rms[:, 0, :], ALU.mult))
                v0 = steps[0]
                with dve.Fori(0, FF // P // RING) as i:
                    for j in range(RING):
                        t = RING * i + (t0 + j)
                        dve.wait_ge(relu_made, RING * i + (layer * FF // P + j + 1))
                        TTn(tmp[:, j % 2, :], tmp[:, j % 2, :], rms[:, 1, :], ALU.mult).then_inc(vstep, 1)
                        dve.wait_ge(vstep, RING * i + (v0 + j + 1))
                        TTn(u[:, bass.ds(SEQ * RING * i + SEQ * j, SEQ)], bank[6 + (t0 + j) % 2][:, :], tmp[:, j % 2, :],
                            ALU.mult).then_inc(z_ready, 1)
                steps[0] += FF // P
                with dve.Fori(0, FF // P // RING) as i:
                    for j in range(RING):
                        dve.wait_ge(mlp_hi, RING * i + (layer * FF // P + j + 1))
                        TTn(mlp_op[:, 1, j % 2, :], u[:, bass.ds(SEQ * RING * i + SEQ * j, SEQ)],
                            mlp_op[:, 0, j % 2, :].bitcast(F32), ALU.subtract).then_inc(mlp_lo, 1)
                for m in range(KT):
                    dve.wait_ge(acc_full, TILE0[f"down{layer}"] + m + 1)
                    TTn(x[:, m, :], bank[m][:, :], x[:, m, :], ALU.add).then_inc(z_ready, 1)

            def cut_conv(out, src, taps, w, bias, done=None):
                at = [i for i, s in enumerate(taps) if s == 0][0]
                step(TS(out, src, w(at), bias, ALU.mult, ALU.add))
                others = [i for i, s in enumerate(taps) if s]
                for i in others:
                    a, b = max(0, -taps[i]), SEQ - max(0, taps[i])
                    ins = STT(out[:, a:b], src[:, a + taps[i]:b + taps[i]], w(i), out[:, a:b], ALU.mult, ALU.add)
                    if done is not None and i == others[-1]:
                        ins.then_inc(done, 1)
                    else:
                        step(ins)

            dve.wait_ge(par_in, 16)
            dve.wait_ge(con_in, 16)
            TS(small[:, 13, :], g("sink", 0, 8), -1.0, None, ALU.mult)
            dve.wait_ge(lam_act, 2)
            step(TS(small[:, 2, :], small[:, 1, :], 2.0, None, ALU.add))
            step(nc.vector.reciprocal(small[:, 3, :], small[:, 2, :]))
            step(TTn(small[:, 4, :], small[:, 3, :], small[:, 1, :], ALU.mult))
            step(TTn(small[:, 5, :], small[:, 4, :], small[:, 4, :], ALU.mult))
            terms = 10
            step(TS(small[:, 6, :], small[:, 5, :], 1.0 / (2 * terms + 1), 1.0 / (2 * terms - 1), ALU.mult, ALU.add))
            for k in range(terms - 2, -1, -1):
                step(TTn(small[:, 6, :], small[:, 6, :], small[:, 5, :], ALU.mult))
                step(TS(small[:, 6, :], small[:, 6, :], 1.0 / (2 * k + 1), None, ALU.add))
            step(TTn(small[:, 7, :], small[:, 6, :], small[:, 4, :], ALU.mult))
            step(TS(small[:, 8, :], g("lam", 0, 8), -1.0, 0.0, ALU.mult, ALU.max))
            step(STT(small[:, 9, :], small[:, 7, :], 2.0, small[:, 8, :], ALU.mult, ALU.add))
            TS(small[:, 14, :], small[:, 9, :], -LRU_C, None, ALU.mult).then_inc(sp_made, 1)
            TS(small[:, 15, :], small[:, 9, :], -LRU_C / 2, None, ALU.mult).then_inc(sp_made, 1)

            dve.wait_ge(x_in, 16)
            norm("even", "g_even")
            for i in range(10):
                scaled("ein", i, z0(i))
            dve.wait_ge(rope_in, 16)
            rotate(0, [z0(i) for i in range(5)], P)
            turn_values([z0(5)])
            dve.wait_ge(inv_in, 16)
            wide = [tmp[:, 2 * i:2 * i + 2, :].rearrange("p a b -> p (a b)") for i in range(2)]
            for grp in range(4):
                u = z0(6 + grp)
                dve.wait_ge(z_ready, TILE0["ein"] + 6 + grp + 1)
                if grp:
                    dve.wait_ge(src_ready, grp)
                else:
                    dve.wait_ge(roped, 5)
                step(nc.vector.memset(wide[0][:, 0:8], 0.0))
                step(nc.vector.memset(wide[0][:, SEQ + 8:SEQ + 16], 0.0))
                step(nc.vector.tensor_copy(wide[0][:, 8:SEQ + 8], u))
                step(TTn(wide[1][:, 1:SEQ + 16], wide[0][:, 0:SEQ + 15], wide[0][:, 1:SEQ + 16], ALU.add))
                a, lo, hi = 1, 1, SEQ + 16
                for k in range(grp):
                    h = 1 << k
                    lo, hi = lo + h, hi - h
                    step(TTn(wide[1 - a][:, lo:hi], wide[a][:, lo - h:hi - h], wide[a][:, lo + h:hi + h], ALU.add))
                    a = 1 - a
                total = wide[a][:, 8:SEQ + 8]
                step(TTn(total, total, arena[:, 29 + grp, :], ALU.mult))
                TTn(z0(14 + grp), total, u, ALU.subtract).then_inc(src_ready, 1)
            for i in range(4):
                lo_of("pool", i, z0(14 + i))
            for i in range(4):
                src = taken("pool", i)
                TS(z0(10 + i), src[:, :], g("pool_scale", i), None, ALU.mult).then_inc(z_ready, 1)
            for i in range(4):
                lo_of("pooled", i, z0(10 + i))

            def even_out(k):
                src = group_bank("even", k)
                lo_of("eattn", k, src[:, :])

            dve.wait_ge(src_ready, 4)
            attention("even", even_out)
            residual("eout")
            norm("mlp0", "g_mlp0")
            mlp(0)

            norm("odd", "g_odd")
            for i in range(12):
                scaled("oin", i, z1(i))
            for j in range(4):
                dve.wait_ge(z_ready, TILE0["oin"] + 4 + j + 1)
                cut_conv(z1(28 + j), z1(4 + j), (-2, -1, 0, 1), lambda i, j=j: g("conv_w", 4 * i + j), g("conv_b", j),
                         src_ready)
            for j in range(4):
                lo_of("xc", j, z1(28 + j))
            for i in range(16):
                src = taken("lru", i)
                TS(z1(12 + i), src[:, :], g("gate_b", i), None, ALU.add).then_inc(z_ready, 1)

            def decay_tmp(u):
                return z1(4 + u) if u < 4 else tmp[:, u - 4, :]

            def gate_tile(kind, u):
                return z1(12 + 8 * (u // 4) + 4 * kind + u % 4)

            for u in range(8):
                dve.wait_ge(decay_made, 2 * u + 2)
                e, r = decay_tmp(u), gate_tile(0, u)
                step(STT(e, e, 1.0, r, ALU.add, ALU.mult))
                step(TS(r, e, 1.0, None, ALU.add))
                STT(e, r, 1.0, e, ALU.add, ALU.mult).then_inc(beta_sq, 1)
            for u in range(8):
                dve.wait_ge(gate_sig, 8 * (u // 4) + 4 + u % 4 + 1)
                ig = gate_tile(1, u)
                step(TTn(ig, ig, z1(28 + u % 4), ALU.mult))
                dve.wait_ge(beta_made, u + 1)
                step(TTn(ig, ig, decay_tmp(u), ALU.mult))
                back = slice(None, None, -1) if u >= 4 else slice(None)
                ins = nc.vector.tensor_tensor_scan(decay_tmp(u)[:, back], gate_tile(0, u)[:, back], ig[:, back], 0.0,
                                                   ALU.mult, ALU.add)
                step(ins)
                if u >= 4:
                    j = u - 4
                    step(TTn(decay_tmp(j), decay_tmp(j), decay_tmp(u), ALU.add))
                    dve.wait_ge(gelu_made, j + 1)
                    TTn(z1(8 + j), z1(8 + j), decay_tmp(j), ALU.mult).then_inc(src_ready, 1)
            for m in range(2):
                lo_of("cq", m, z1(m), g("g_cq", m))
            spread("cq", 1)
            lo_of("ckv", 0, z1(2), g("g_ckv"))
            spread("ckv", 2)
            for h in range(MLA_HEADS):
                scaled("uq", h, z1(12 + h), 1, 96)
            for h in range(MLA_HEADS):
                scaled("ukn", h, z1(20 + h), 2, 64)
            for i in range(4):
                scaled("uv", i, z1(28 + i), 2)
            dve.wait_ge(rope_in, 32)
            rotate(5, [z1(3)] + [z1(12 + h) for h in range(MLA_HEADS)], 96)
            turn_values([z1(28 + i) for i in range(4)])
            for i in range(4):
                lo_of("lru", i, z1(8 + i))

            def mla_out(k):
                src = group_bank("mla", k)
                lo_of("mattn", k, src[:, :])

            attention("mla", mla_out)
            residual("oout")
            norm("mlp1", "g_mlp1")
            mlp(1)

            spread("final")
            for m in range(KT):
                STT(x[:, m, :], x[:, m, :], g("g_final", m), rms[:, 0, :], ALU.mult, ALU.mult).then_inc(src_ready, 1)
            norm("mix2", "g_mix2")
            for i in range(33):
                gi = (i - 21) % 3
                if 21 <= i < 30 and gi:
                    src = taken("zin", i)
                    r = DILATIONS[gi]
                    TTn(residues(z2(i), r), dilate(src[:, :], r), dilate(rms[:, 0, :], r), ALU.mult).then_inc(z_ready, 1)
                else:
                    scaled("zin", i, z2(i))
            dve.wait_ge(gates_turned, 1)
            step(nc.vector.tensor_copy(gates[:, :], bank[2][:, 0:TT * 32]))
            TS(gates[:, 0:18:3], gates[:, 0:18:3], c("late"), None, ALU.mult).then_inc(gates_ready, 1)
            turn_values([z2(i) for i in (14, 16, 27, 28, 29)])
            for i in range(4):
                kv, half = i // 2, i % 2
                row = tmp_flat(i)
                if i >= 2:
                    dve.wait_ge(split_lo, SPLIT0["cmp"] + i - 1)
                step(nc.vector.memset(row[:, SEQ:cmp_half], 0.0))
                pe_row = g("pe", CMP_BLOCK * kv + CMP_STRIDE * half, CMP_STRIDE).rearrange("p (o i) -> p o i", o=1)
                TTn(row[:, 0:SEQ].rearrange("p (n i) -> p n i", i=CMP_STRIDE),
                    z2(11 + kv).rearrange("p (n i) -> p n i", i=CMP_STRIDE),
                    pe_row.broadcast_to([P, SEQ // CMP_STRIDE, CMP_STRIDE]), ALU.add).then_inc(src_ready, 1)
                dve.wait_ge(split_hi, SPLIT0["cmp"] + i + 1)
                hi, lo = splits["cmp", i]
                TTn(lo, row, hi.bitcast(F32), ALU.subtract).then_inc(split_lo, 1)
            for i in range(2):
                src = taken("cmp", i)
                nc.vector.tensor_copy(hid[:, i, :], src[:, 0:32]).then_inc(z_ready, 1)
            for i in range(2):
                dve.wait_ge(hid_sig, i + 1)
                TTn(hid[:, i, :], hid[:, i, :], hid[:, 2 + i, :], ALU.mult).then_inc(hid_made, 1)
            dve.wait_ge(cmp_full, 1)
            nc.vector.tensor_copy(cmpk[:, :], bank[2][:, 0:32]).then_inc(cmp_ready, 1)
            dve.wait_ge(cmp_full, 2)
            nc.vector.tensor_copy(cmpv[:, :], bank[3][0:32, 0:P]).then_inc(cmp_ready, 1)
            for j in range(2):
                step(TTn(z2(2 + j), z2(2 + j), z2(4 + j), ALU.mult))
                cut_conv(z2(4 + j), z2(2 + j), (-2, -1, 0), lambda i, j=j: g("conv2_w", 2 * i + j), g("conv2_b", j))
                step(TTn(z2(4 + j), z2(4 + j), z2(j), ALU.mult))
                dve.wait_ge(silu_made, 2 + j)
                TTn(z2(4 + j), z2(4 + j), z2(6 + j), ALU.mult).then_inc(src_ready, 1)
            for j in range(2):
                lo_of("conv2", j, z2(4 + j))
            dve.wait_ge(silu_made, 9)

            def last_out(k):
                src = group_bank("last", k)
                if k < NSA_R:
                    TTn(z2(18 + k), src[:, :], z2(18 + k), ALU.mult).then_inc(o_out, 1)
                    lo_of("nsa", k, z2(18 + k))
                else:
                    r = DILATIONS[k - NSA_R]
                    nc.vector.tensor_copy(dilate(z2(21 + k - NSA_R), r), residues(src[:, :], r)).then_inc(o_out, 1)

            attention("last", last_out)
            dve.wait_ge(log_den, 1)
            first = 3 * TT * 2 * NSA_R
            step(TTn(rden[:, 24:48], rden[:, 0:24], negm[:, first:first + 24], ALU.subtract))
            nc.vector.tensor_copy(tmp[:, 0:3, :].rearrange("p a (b e) -> p (a b) e", e=64),
                                  rden[:, 24:48].rearrange("p (n o) -> p n o", o=1).broadcast_to([P, 24, 64])).then_inc(lse_ready, 1)
            for gi in range(3):
                r = DILATIONS[gi]
                dve.wait_ge(lse_full, gi + 1)
                step(nc.vector.tensor_copy(dilate(z2(24 + gi), r), residues(bank[2 + gi][:, :], r)))
            step(TTn(tmp[:, 3, :], z2(24), z2(25), ALU.max))
            step(TTn(tmp[:, 3, :], tmp[:, 3, :], z2(26), ALU.max))
            for gi in range(3):
                TTn(z2(24 + gi), z2(24 + gi), tmp[:, 3, :], ALU.subtract).then_inc(ls_max, 1)
            dve.wait_ge(lse_exp, 3)
            step(TTn(tmp[:, 4, :], z2(24), z2(25), ALU.add))
            step(TTn(tmp[:, 4, :], tmp[:, 4, :], z2(26), ALU.add))
            step(nc.vector.reciprocal(tmp[:, 5, :], tmp[:, 4, :]))
            for gi in range(3):
                step(TTn(z2(24 + gi), z2(24 + gi), tmp[:, 5, :], ALU.mult))
                step(TTn(z2(24 + gi), z2(24 + gi), z2(21 + gi), ALU.mult))
                TTn(z2(30 + gi), z2(30 + gi), z2(24 + gi), ALU.mult).then_inc(src_ready, 1)
            for gi in range(3):
                lo_of("dil", gi, z2(30 + gi))
            for k in range(2):
                dve.wait_ge(mlp_hi, 2 * FF // P + k + 1)
                TTn(mlp_op[:, 1, k, :], arena[:, 24 + k, :], mlp_op[:, 0, k, :].bitcast(F32), ALU.subtract).then_inc(mlp_lo, 1)
            residual("out2")
            for m in range(KT):
                lo_of("ple", m, x[:, m, :])
            for m in range(KT):
                src = taken("ple", 2 * m)
                nc.vector.tensor_copy(tmp[:, m % 2, :], src[:, :]).then_inc(z_ready, 1)
                src = taken("ple", 2 * m + 1)
                dve.wait_ge(ple_sig, m + 1)
                step(TTn(tmp[:, 2, :], src[:, :], tmp[:, m % 2, :], ALU.mult))
                TTn(x[:, m, :], x[:, m, :], tmp[:, 2, :], ALU.add).then_inc(z_ready, 1)
            spread("out")
            for m in range(KT):
                STT(arena[:, m, :], x[:, m, :], g("g_out", m), rms[:, 0, :], ALU.mult, ALU.mult).then_inc(y_ready, 1)


def sub_blocks(w, cols=None):
    k, _ = w.shape
    if cols is not None:
        wide = np.zeros((k, len(cols)), w.dtype)
        there = np.asarray(cols) >= 0
        wide[:, there] = w[:, np.asarray(cols)[there]]
        w = wide
    m = w.shape[1]
    if m % P:
        w = np.concatenate([w, np.zeros((k, P - m % P), w.dtype)], axis=1)
    return w.reshape(k // P, P, -1, P).transpose(2, 0, 1, 3)


def pair_diagonal(w):
    n, a, b = w.shape
    out = np.zeros((n, 2 * a, 2 * b), w.dtype)
    out[:, :a, :b] = w
    out[:, a:, b:] = w
    return out


def padded(blocks):
    blocks = blocks.reshape(-1, P, P)
    short = -len(blocks) % SUBS
    return np.concatenate([blocks, np.zeros((short, P, P), blocks.dtype)]) if short else blocks


def heads(n_pairs, stride, offset=0, dh=64):
    return [offset + dh * (j + stride * s) + i for j in range(n_pairs) for s in range(2) for i in range(dh)]


def weight_stream(a):
    span = lambda lo, n: list(range(lo, lo + n))
    out = []
    ein = heads(4, 4) + span(512, 768)
    out.append(padded(sub_blocks(a["e_w_in"][0], ein)))
    out.append(padded(a["e_w_pool"][0]))
    rows = heads(4, 4) + span(512, 512)
    out.append(padded(sub_blocks(a["e_w_out"][0][rows])))

    def mlp(layer):
        out.append(padded(sub_blocks(a["w_mlp1"][layer])))
        out.append(padded(sub_blocks(a["w_mlp2"][layer]).transpose(1, 0, 2, 3)))

    mlp(0)
    oin = span(0, 384) + [-1] * 64 + span(384, 32) + [-1] * 32 + span(416, 1024)
    out.append(padded(sub_blocks(a["o_w_in"][0], oin)))
    gates = np.stack([a["o_lru_wa"][0], a["o_lru_wx"][0]], axis=1)
    lru = np.zeros((2, 2, 4, P, P), gates.dtype)
    lru[:, :, :, :64, :64] = gates[:, :, 0::2]
    lru[:, :, :, 64:, 64:] = gates[:, :, 1::2]
    out.append(padded(lru))
    uq = [96 * h + i if i < 96 else -1 for h in range(MLA_HEADS) for i in range(P)]
    out.append(padded(sub_blocks(a["o_w_uq"][0], uq)))
    ukn = [P * h + i if i < 64 else -1 for h in range(MLA_HEADS) for i in range(P)]
    out.append(padded(sub_blocks(a["o_w_ukv"][0], ukn)))
    uv = [P * h + 64 + i for h in range(MLA_HEADS) for i in range(64)]
    out.append(padded(sub_blocks(a["o_w_ukv"][0], uv)))
    out.append(padded(sub_blocks(a["o_w_out"][0])))
    mlp(1)
    q0 = 1024
    g0 = q0 + 384 + 6 * 128
    zin = (span(0, 1024) + heads(3, 3, q0) + span(q0 + 384, 768) + span(g0, 18) + [-1] * 110
           + heads(3, 3, g0 + 18) + span(g0 + 18 + 384, 4 * 384))
    out.append(padded(sub_blocks(a["w_in_2"][0], zin)))
    for kv in range(2):
        out.append(padded(pair_diagonal(a["cmp_w1_2"][0, kv].reshape(CMP_BLOCK, HD, HD))))
    rows = span(0, 256) + heads(3, 3, 256) + span(640, 384)
    out.append(padded(sub_blocks(a["w_out_2"][0][rows])))
    gate, proj = sub_blocks(a["w_ple_gate_2"][0]), sub_blocks(a["w_ple_proj_2"][0])
    out.append(padded(np.concatenate([gate, proj], axis=1)))
    stream = np.concatenate(out)
    assert len(stream) == NBLOCKS * SUBS
    return np.ascontiguousarray(stream.reshape(NBLOCKS, SUBS, P, P).transpose(0, 2, 1, 3)).reshape(NBLOCKS, P, D)


def small_params(a):
    tiles = lambda v: v.reshape(-1, P).T
    pe = a["cmp_pe_2"][0].transpose(2, 0, 1).reshape(HD, 2 * CMP_BLOCK)
    w2 = pair_diagonal(a["cmp_w2_2"][0])
    bias = np.stack([a["o_lru_ba"][0], a["o_lru_bx"][0]], axis=1)
    parts = dict(g_even=tiles(a["e_norm_mix"][0]), g_mlp0=tiles(a["norm_mlp"][0]), g_odd=tiles(a["o_norm_mix"][0]),
                 g_mlp1=tiles(a["norm_mlp"][1]), g_final=tiles(a["final_norm"]), g_mix2=tiles(a["norm_mix_2"][0]),
                 g_out=tiles(a["norm_final_2"]), g_cq=tiles(a["o_g_cq"][0]), g_ckv=tiles(a["o_g_ckv"][0]),
                 pool_scale=tiles(a["e_pool_scale"][0]), conv_w=tiles(a["o_conv_w"][0]), conv_b=tiles(a["o_conv_b"][0]),
                 gate_b=tiles(bias), lam=tiles(a["o_lru_lambda"][0]), conv2_w=tiles(a["conv_w_2"][0]),
                 conv2_b=tiles(a["conv_b_2"][0]), pe=np.concatenate([pe, pe]),
                 sink=np.broadcast_to(a["e_sink"][0], (P, 8)), w2k=w2[0], w2v=w2[1])
    return np.ascontiguousarray(np.concatenate([parts[n].reshape(P, w) for n, w in PARAM_COLS], axis=1))


def small_consts():
    p = np.arange(P)[:, None]
    mask = lambda ok: np.where(ok, 0.0, NEG)
    c = np.arange(640)[None]
    band = np.arange(384)[None]
    near = np.arange(256)[None]
    b = np.arange(P)[None]
    tok = (np.arange(TT) * P)[None, :, None] + p[:, :, None]
    n = np.arange(32)[None, None, :]
    rot = np.zeros((2, P, P))
    for first, half, which in ((0, 32, 0), (64, 32, 0), (64, 16, 1)):
        for i in range(half):
            rot[which, first + half + i, first + i] = -1.0
            rot[which, first + i, first + half + i] = 1.0
    parts = dict(causal=mask(c - 512 <= p), band=mask(np.abs(band - P - p) <= 128),
                 near=mask((p + P - near >= 0) & (p + P - near <= 128)),
                 blocks=mask((p // 32 == b // 32) & (b <= p)),
                 cmpmask=mask(CMP_STRIDE * n + CMP_BLOCK - 1 <= tok).reshape(P, TT * 32),
                 ident=np.eye(P), rot_even=rot[0], rot_mla=rot[1], late=(p >= CMP_BLOCK - 1) * 1.0,
                 ones=np.ones((P, 1)), eps=np.full((P, 1), EPS))
    return np.concatenate([parts[k].reshape(P, w) for k, w in CONST_COLS], axis=1).astype(np.float32)


def rope_tables():
    out = np.zeros((2, P, 2, SEQ), np.float32)
    out[1, :64, 0] = 1.0
    for layer, first, half, n in ((0, 0, 32, 4), (1, 64, 16, 2)):
        inv = np.float32(10000.0) ** (-np.arange(half, dtype=np.float32) / np.float32(half))
        ang = np.arange(SEQ, dtype=np.float32)[None] * inv[:, None]
        for j in range(n):
            out[layer, first + half * j:first + half * (j + 1), 0] = np.cos(ang)
            out[layer, first + half * j:first + half * (j + 1), 1] = np.sin(ang)
    return out


def window_counts():
    t = np.arange(SEQ)
    rows = [1.0 / (np.clip(t + w // 2, 0, SEQ) - np.clip(t - w // 2, 0, SEQ)) for w in (2, 4, 8, 16)]
    return np.ascontiguousarray(np.broadcast_to(np.stack(rows)[None], (P, 4, SEQ))).astype(np.float32)


def kernel(**inputs):
    import concourse.bacc as bacc
    from concourse.bass_utils import run_bass_kernel_spmd

    a = {k: np.asarray(v) for k, v in inputs.items()}
    arrays = dict(x_t=np.ascontiguousarray(a["x"][0].T), stream=weight_stream(a), params=small_params(a),
                  consts=small_consts(), ropes=rope_tables(), invcnt=window_counts(),
                  p_t=np.ascontiguousarray(a["p_2"][0, 0].T))
    nc = bacc.Bacc("TRN2", target_bir_lowering=False, num_devices=1)
    args = {n: nc.dram_tensor(n + "_dram", v.shape, mybir.dt.from_np(v.dtype), kind="ExternalInput").ap()
            for n, v in arrays.items()}
    out = nc.dram_tensor("out_t_dram", (D, SEQ), F32, kind="ExternalOutput").ap()
    program(nc, out_t=out, **args)
    r = run_bass_kernel_spmd(nc, [{n + "_dram": v for n, v in arrays.items()}], core_ids=[0])
    return np.ascontiguousarray(r.results[0]["out_t_dram"].T)[None]
```

```python
from contextlib import ExitStack

import concourse.bass as bass
import numpy as np
from concourse import mybir

F32 = mybir.dt.float32
F32R = mybir.dt.float32r
ALU = mybir.AluOpType
ACT = mybir.ActivationFunctionType
AX = mybir.AxisListType.X

P = 128
SEQ = 512
D = 1024
KT = D // P
TT = SEQ // P
FF = 4 * D
SUBS = 8
RING = 4
EPS = 1e-6
NEG = -1e30
EVEN_HEADS, EVEN_GROUP = 8, 4
LRU_C = 8.0
MLA_HEADS, NOPE, ROPE = 8, 64, 32
NSA_R, HD = 3, 64
CMP_BLOCK, CMP_STRIDE = 32, 16
N_CMP = (SEQ - CMP_BLOCK) // CMP_STRIDE + 1
DILATIONS = (1, 4, 16)

STAGES = [("ein", 10, 8), ("pool", 4, 1), ("eout", 8, 8), ("up0", 32, 8), ("down0", 8, 32),
          ("oin", 12, 8), ("lru", 16, 1), ("uq", 8, 2), ("ukn", 8, 1), ("uv", 4, 1), ("oout", 8, 8),
          ("up1", 32, 8), ("down1", 8, 32), ("zin", 6, 8),
          *((f"{kind}{i}", n, 8) for i in range(8) for kind, n in (("zin_by", 1), ("cmp", 0))),
          ("zin_rest", 19, 8), ("out2", 8, 8), ("ple", 16, 5)]
ZIN = [11, 12, 13, 14, 16, 17, 27, 28, 29, 15, 2, 4, 3, 5, 0, 1, 6, 7, 18, 19, 20, 30, 31, 32, 8, 9, 10,
       21, 22, 23, 24, 25, 26]
assert sorted(ZIN) == list(range(33))
TILE0, SUB0, NTILES = {}, {}, {}
_t = _s = 0
for _name, _n, _k in STAGES:
    TILE0[_name], SUB0[_name], NTILES[_name] = _t, _s, _n
    _t += _n
    _s += -(-max(_n, 1) * _k // SUBS) * SUBS
NBLOCKS = _s // SUBS
assert NBLOCKS % RING == 0



def block_ends():
    out, used = [], 0
    for name, tiles, k in STAGES:
        ends, s, t = {}, SUB0[name], TILE0[name]
        if name.startswith("down"):
            ends = {s + tiles * k - tiles + i: t + i + 1 for i in range(tiles)}
        else:
            for i in range(tiles):
                s += k if name != "ple" else (8, 2)[i % 2]
                ends[s - 1] = t + i + 1
        end = SUB0[name] + max(tiles, 1) * k
        for b in range(SUB0[name] // SUBS, -(-end // SUBS)):
            last = min(SUBS * (b + 1), end) - 1
            if last in ends:
                out.append(("tile", ends[last]))
            else:
                used += 1
                out.append(("block", used))
    return out


BLOCK_END = block_ends()
assert len(BLOCK_END) == NBLOCKS

SPLITS = [("even", 8), ("pool", 4), ("pooled", 4), ("eattn", 4), ("mlp0", 8), ("odd", 8), ("xc", 4),
          ("cq", 2), ("ckv", 1), ("lru", 4), ("mattn", 4), ("mlp1", 8), ("mix2", 8), ("cmp", 4),
          ("conv2", 2), ("nsa", 3), ("dil", 3), ("ple", 8)]
HEAD = 3
SPLIT0 = {}
_t = 0
for _name, _n in SPLITS:
    SPLIT0[_name] = _t
    _t += _n

NORMS = [("even", 8), ("mlp0", 8), ("odd", 8), ("cq", 2), ("ckv", 1), ("mlp1", 8), ("final", 16),
         ("mix2", 0), ("out", 8)]
NORM, SQ0, NORM_TILES = {}, {}, dict(NORMS)
_t = 0
for _i, (_name, _n) in enumerate(NORMS):
    NORM[_name], SQ0[_name] = _i, _t
    _t += _n

PARAM_COLS = [("g_even", 8), ("g_mlp0", 8), ("g_odd", 8), ("g_mlp1", 8), ("g_final", 8), ("g_mix2", 8),
              ("g_out", 8), ("g_cq", 2), ("g_ckv", 1), ("pool_scale", 4), ("conv_w", 16), ("conv_b", 4),
              ("gate_b", 16), ("lam", 8), ("conv2_w", 6), ("conv2_b", 2), ("pe", 64), ("sink", 8),
              ("w2k", 128), ("w2v", 128)]
CONST_COLS = [("causal", 640), ("band", 384), ("near", 256), ("blocks", 128), ("cmpmask", TT * 32),
              ("ident", 128), ("rot_even", 128), ("rot_mla", 128), ("late", 1), ("ones", 1), ("eps", 1)]


def columns(cols):
    at, out = 0, {}
    for name, n in cols:
        out[name] = (at, at + n)
        at += n
    return out, at


PCOL, NPARAM = columns(PARAM_COLS)
CCOL, NCONST = columns(CONST_COLS)


def even_units():
    return [dict(j=j, g=g, qt=qt, lo=max(0, qt - 1), hi=min(TT, qt + 2), group=j)
            for j in range(EVEN_GROUP) for g in range(2) for qt in range(TT)]


def mla_units():
    return [dict(h=h, qt=qt, group=h // 2) for h in range(MLA_HEADS) for qt in range(TT)]


def nsa_units():
    return [dict(r=r, g=g, qt=qt, branch=b, group=r)
            for r in range(NSA_R) for qt in range(TT) for g in range(2) for b in range(3)]


def dilated_units():
    return [dict(gi=gi, tile=t, g=g, group=NSA_R + gi) for gi in range(3) for t in range(TT) for g in range(2)]


EVEN, MLA, LAST = even_units(), mla_units(), nsa_units() + dilated_units()
UNIT0 = {"even": 0, "mla": len(EVEN), "last": len(EVEN) + len(MLA)}


def program(nc, x_t, stream, params, consts, ropes, invcnt, p_t, out_t):
    with ExitStack() as ctx:
        def sb(name, shape, dt=F32):
            return ctx.enter_context(nc.sbuf_tensor(name, shape, dt))

        def sem(name):
            return ctx.enter_context(nc.semaphore(name))

        arena = sb("arena", [P, 49, SEQ])
        base = nc.sbuf_base - 49 * SEQ * 4
        opA = nc.alloc_sbuf_tensor_at("opA", [P, 2, KT, SEQ], F32R, offset=base)
        opC = nc.alloc_sbuf_tensor_at("opC", [P, 2, KT, SEQ], F32R, offset=base + 33 * SEQ * 4)
        x = sb("x", [P, KT, SEQ])
        raw = sb("raw", [P, RING, D])
        w_hi = sb("w_hi", [P, RING, D], F32R)
        w_lo = sb("w_lo", [P, RING, D], F32R)
        mlp_op = sb("mlp_op", [P, 2, 2, SEQ], F32R)
        more = nc.alloc_sbuf_tensor_at("more", [P, 2, SEQ], F32, offset=nc.sbuf_base - 4 * SEQ * 4)
        tmp = sb("tmp", [P, 6, SEQ])
        rms = sb("rms", [P, 3, SEQ])
        rope = sb("rope", [P, 2, SEQ])
        con = sb("con", [P, NCONST])
        par = sb("par", [P, NPARAM])
        negm = sb("negm", [P, 96])
        den = sb("den", [P, 96])
        rden = sb("rden", [P, 96])
        gates = sb("gates", [P, TT * 32])
        small = sb("small", [P, 16, 8])
        std = sb("std", [P, len(NORMS), TT])
        rtok = sb("rtok", [P, len(NORMS), TT])
        hid = sb("hid", [P, 4, 32])
        cmpk = sb("cmpk", [P, 32])
        cmpv = sb("cmpv", [32, P])
        bank = [ctx.enter_context(nc.psum_tensor(f"bank{i}", [P, SEQ], F32)) for i in range(8)]

        raw_in = [sem(f"raw_in{i}") for i in range(RING)]
        hi_made, lo_made, block_used = sem("hi_made"), sem("lo_made"), sem("block_used")
        acc_full, z_ready = sem("acc_full"), sem("z_ready")
        split_hi, split_lo = sem("split_hi"), sem("split_lo")
        sq_ready, sq_used = sem("sq_ready"), sem("sq_used")
        std_ready, rtok_ready, rms_full, rms_ready = sem("std_ready"), sem("rtok_ready"), sem("rms_full"), sem("rms_ready")
        x_in = [sem(f"x_in{m}") for m in range(KT)]
        par_in, con_in, rope_in, inv_in, p_in = (sem(s) for s in ("par_in", "con_in", "rope_in", "inv_in", "p_in"))
        rot_full, roped = sem("rot_full"), sem("roped")
        turned, v_tok = sem("turned"), sem("v_tok")
        s_full, masked, sink_put, exp_done = sem("s_full"), sem("masked"), sem("sink_put"), sem("exp_done")
        p_ready, pt_full, pt_ready, pv_done = sem("p_ready"), sem("pt_full"), sem("pt_ready"), sem("pv_done")
        o_out = sem("o_out")
        relu_made, mlp_hi, mlp_lo = sem("relu_made"), sem("mlp_hi"), sem("mlp_lo")
        src_ready = sem("src_ready")
        key_rope = sem("key_rope")
        gate_sig, decay_made, beta_sq, beta_made, gelu_made = (sem(s) for s in ("gate_sig", "decay_made", "beta_sq", "beta_made", "gelu_made"))
        lam_act, sp_made = sem("lam_act"), sem("sp_made")
        silu_made, hid_in, hid_sig, hid_made, cmp_full, cmp_ready = (sem(s) for s in ("silu_made", "hid_in", "hid_sig", "hid_made", "cmp_full", "cmp_ready"))
        gates_turned, gates_ready = sem("gates_turned"), sem("gates_ready")
        log_den, lse_ready, lse_full, lse_exp = sem("log_den"), sem("lse_ready"), sem("lse_full"), sem("lse_exp")
        ls_max, ple_sig = sem("ls_max"), sem("ple_sig")
        vstep, y_ready, stored = sem("vstep"), sem("y_ready"), sem("stored")

        def c(name, lo=0, hi=None):
            a, b = CCOL[name]
            return con[:, a + lo:(b if hi is None else a + hi)]

        def g(name, i=0, n=1):
            return par[:, PCOL[name][0] + i:PCOL[name][0] + i + n]

        ident = c("ident")

        def z(i, layer):
            return arena[:, i + 16 * (layer % 2), :]

        def Z(layer):
            return lambda i: z(i, layer)

        z0, z1, z2 = Z(0), Z(1), Z(2)
        splits = {}

        def place(name, op, first, n):
            for i in range(n):
                splits[name, i] = (op[:, 0, first + i, :], op[:, 1, first + i, :])

        for name, op, first, n in (
                ("even", opC, 0, 8), ("pool", opC, 0, 4), ("pooled", opC, 4, 4), ("eattn", opC, 0, 4),
                ("mlp0", opA, 0, 8), ("odd", opA, 0, 8), ("xc", opA, 0, 4), ("cq", opA, 4, 2), ("ckv", opA, 6, 1),
                ("lru", opA, 4, 4), ("mattn", opA, 0, 4), ("mlp1", opC, 0, 8), ("mix2", opC, 0, 8),
                ("conv2", opC, 0, 2), ("nsa", opC, 2, 3), ("dil", opC, 5, 3), ("ple", opA, 0, 8)):
            place(name, op, first, n)
        opE = nc.alloc_sbuf_tensor_at("opE", [P, 2, 4, SEQ], F32R, offset=base + 18 * SEQ * 4)
        place("cmp", opE, 0, 4)
        def dilate(ap, r):
            return ap.rearrange("p (a r) -> p r a", r=r)

        def residues(ap, r):
            return ap.rearrange("p (r a) -> p r a", r=r)

        def unit(u, family):
            if family == "even":
                lo, hi, b = u["lo"], u["hi"], slice(64 * u["g"], 64 * u["g"] + 64)
                off = P * (lo - u["qt"] + 1)
                return dict(q=z0(u["j"])[b, P * u["qt"]:P * (u["qt"] + 1)], k=z0(4)[b, P * lo:P * hi], n=P * (hi - lo),
                            mask=c("band", off, off + P * (hi - lo)), scale=HD ** -0.5, sink=4 * u["g"] + u["j"],
                            v=[z0(5)[:, P * t + 64 * u["g"]:P * t + 64 * u["g"] + 64] for t in range(lo, hi)],
                            out=(64 * u["g"], P * u["qt"]), gate=None)
            if family == "mla":
                h, qt = u["h"], u["qt"]
                at = 64 * (h % 2)
                return dict(q=z1(12 + h)[0:96, P * qt:P * (qt + 1)], k=z1(20 + h)[0:96, :], n=SEQ,
                            mask=c("causal", 0, SEQ), scale=(NOPE + ROPE) ** -0.5, sink=None,
                            v=[z1(28 + h // 2)[:, P * t + at:P * t + at + 64] for t in range(TT)],
                            out=(at, P * qt), gate=None)
            b = slice(64 * u["g"], 64 * u["g"] + 64)
            if "r" in u:
                qt, br = u["qt"], u["branch"]
                n = N_CMP if br == 0 else P * (qt + 1)
                col = 32 * qt + 9 * u["g"] + 3 * u["r"] + br
                return dict(q=z2(8 + u["r"])[b, P * qt:P * (qt + 1)], n=n,
                            k=cmpk[b, 0:N_CMP] if br == 0 else z2(11 + 2 * br)[b, 0:n],
                            mask=c("cmpmask", 32 * qt, 32 * qt + N_CMP) if br == 0 else c("causal", 640 - n, 640),
                            scale=HD ** -0.5, sink=None,
                            v=[cmpv[0:N_CMP, b]] if br == 0 else
                              [z2(12 + 2 * br)[:, P * t + b.start:P * t + b.stop] for t in range(qt + 1)],
                            out=(b.start, P * qt), gate=gates[:, col:col + 1], first=br == 0, last=br == 2)
            gi, t = u["gi"], u["tile"]
            lo = t - 1 if gi == 0 and t else t
            mask = [c("near", 0 if t else P, 2 * P), c("causal", 512, 640), c("blocks")][gi]
            return dict(q=z2(21 + gi)[b, P * t:P * (t + 1)], k=z2(24 + gi)[b, P * lo:P * (t + 1)], n=P * (t + 1 - lo),
                        mask=mask, scale=HD ** -0.5, sink=None,
                        v=[z2(27 + gi)[:, P * s + b.start:P * s + b.stop] for s in range(lo, t + 1)],
                        out=(b.start, P * t), gate=None)

        FAMILY = {"even": [unit(u, "even") | {"group": u["group"]} for u in EVEN],
                  "mla": [unit(u, "mla") | {"group": u["group"]} for u in MLA],
                  "last": [unit(u, "last") | {"group": u["group"]} for u in LAST]}
        GROUP0 = {"even": 0, "mla": 4, "last": 8}

        def last_of(family, group):
            return max(i for i, u in enumerate(FAMILY[family]) if u["group"] == group)

        NORM_LAG, TURN_LAG, VALUE_LAG = 2, 3, 4

        def probs(i, n):
            return more[:, i % 4 - 2, 0:n] if i % 4 >= 2 else tmp[:, 2 + i % 4, 0:n]

        def groups_after(family, step):
            n = max(u["group"] for u in FAMILY[family]) + 1
            return [k for k in range(n) if last_of(family, k) + VALUE_LAG + 1 == step]

        block = ctx.enter_context(nc.Block())

        @block.sync
        def _(sp):
            for n in range(RING):
                sp.dma_start(x[:, n, :], x_t[P * n:P * (n + 1), :]).then_inc(x_in[n], 16)
            for n in range(RING):
                sp.dma_start(raw[:, n, :], stream[n]).then_inc(raw_in[n], 16)
            with sp.Fori(1, NBLOCKS // RING) as i:
                for j in range(RING):
                    sp.wait_ge(lo_made, RING * i + (j + 1 - RING))
                    sp.dma_start(raw[:, j, :], stream[RING * i + j]).then_inc(raw_in[j], 16)
            for m in range(KT):
                sp.wait_ge(y_ready, m + 1)
                sp.dma_start(out_t[P * m:P * (m + 1), :], arena[:, m, :]).then_inc(stored, 16)
            sp.wait_ge(stored, 16 * KT)

        @block.gpsimd
        def _(pool):
            with pool.Fori(0, NBLOCKS // RING) as i:
                for j in range(RING):
                    pool.wait_ge(hi_made, RING * i + (j + 1))
                    pool.tensor_tensor(w_lo[:, j, :], raw[:, j, :], w_hi[:, j, :].bitcast(F32),
                                       ALU.subtract).then_inc(lo_made, 1)

        @block.tensor
        def _(pe):
            seen = {"split": 0}

            def need_split(name, i):
                n = SPLIT0[name] + i + 1
                if n > seen["split"]:
                    pe.wait_ge(split_lo, n)
                    seen["split"] = n

            def product(out, slot, k, hi, lo, first, last):
                wh, wl = w_hi[:, slot, P * k:P * (k + 1)], w_lo[:, slot, P * k:P * (k + 1)]
                pe.matmul(out, wh, hi, start=first, stop=False)
                pe.matmul(out, wh, lo, start=False, stop=False)
                return pe.matmul(out, wl, hi, start=False, stop=last)

            def head(stage, op, norm=None, summed=0):
                t0, b0 = TILE0[stage], SUB0[stage] // SUBS
                for k in range(KT):
                    if norm:
                        per = NORM_TILES[norm] // KT
                        norm_sums(norm, range(max(summed, per * k), per * (k + 1)))
                    need_split(op, k)
                    for i in range(HEAD):
                        if k == 0:
                            if t0 + i >= 4:
                                pe.wait_ge(z_ready, t0 + i - 3)
                            pe.wait_ge(lo_made, b0 + i + 1)
                        mm = product(bank[4 + (t0 + i) % 4][:, :], (b0 + i) % RING, k, *splits[op, k], k == 0, k == KT - 1)
                        if k == KT - 1:
                            mm.then_inc(acc_full, 1)

            def linear(name, operand, n=SEQ, subs=None, after=None, headed=0):
                t0, s, ntiles = TILE0[name], SUB0[name], NTILES[name]
                nsub = {a: k for a, _, k in STAGES}[name]
                count = subs or (lambda i: nsub)
                end = s + sum(count(i) for i in range(ntiles))
                s += SUBS * headed
                for i in range(headed, ntiles):
                    t = t0 + i
                    if t >= 4:
                        pe.wait_ge(z_ready, t - 3)
                    for k in range(count(i)):
                        if s % SUBS == 0:
                            pe.wait_ge(lo_made, s // SUBS + 1)
                        hi, lo = operand(i, k)
                        mm = product(bank[4 + t % 4][:, 0:n], s // SUBS % RING, s % SUBS, hi, lo, k == 0, k == count(i) - 1)
                        s += 1
                        if (s % SUBS == 0 or s == end) and k < count(i) - 1:
                            mm.then_inc(block_used, 1)
                    mm.then_inc(acc_full, 1)
                    if after:
                        after(i)

            def split_operand(name):
                def operand(i, k):
                    need_split(name, k)
                    return splits[name, k]
                return operand

            def norm_sums(name, tiles=None):
                for m in range(NORM_TILES[name]) if tiles is None else tiles:
                    pe.wait_ge(sq_ready, SQ0[name] + m + 1)
                    for t in range(TT):
                        col = t + (TT * (m % 2) if name == "final" else 0)
                        mm = pe.matmul(bank[0][:, col:col + 1], tmp[:, 4 + (SQ0[name] + m) % 2, P * t:P * (t + 1)], c("ones"),
                                       start=(m == 0 and t == 0), stop=(m == NORM_TILES[name] - 1), skip_group_check=True)
                    mm.then_inc(sq_used, 1)

            def norm_spread(name):
                pe.wait_ge(rtok_ready, NORM[name] + 1)
                if name == "mix2":
                    pe.wait_ge(rms_ready, NORM[name])
                for t in range(TT):
                    mm = pe.matmul(bank[1][:, P * t:P * (t + 1)], rtok[:, NORM[name], t:t + 1].broadcast_to([P, P]), ident,
                                   start=True, stop=True)
                mm.then_inc(rms_full, 1)

            def behind(name):
                return lambda i: norm_sums(name, [i - 2]) if i >= 2 else None

            turn_count = [0]

            def rotate(first, tiles, rot, m):
                for i, (tile, ready) in enumerate(tiles):
                    pe.wait_ge(z_ready, ready)
                    if i >= 2:
                        pe.wait_ge(roped, first + i - 1)
                    pe.matmul(bank[2 + i % 2][0:m, :], rot[0:m, 0:m], tile[0:m, :], start=True, stop=True).then_inc(rot_full, 1)

            def turn_values(tiles):
                for tile, ready in tiles:
                    pe.wait_ge(z_ready, ready)
                    if turn_count[0] >= 2:
                        pe.wait_ge(v_tok, turn_count[0] - 1)
                    for t in range(TT):
                        mm = pe.transpose(bank[turn_count[0] % 2][:, P * t:P * (t + 1)], tile[:, P * t:P * (t + 1)], ident)
                    mm.then_inc(turned, 1)
                    turn_count[0] += 1

            def attention(family):
                units, u0 = FAMILY[family], UNIT0[family]
                n = len(units)
                for step in range(n + VALUE_LAG):
                    if step < n:
                        u, gu = units[step], u0 + step
                        if step >= 2:
                            pe.wait_ge(masked, gu - 1)
                        pe.matmul(bank[2 + step % 2][:, 0:u["n"]], u["q"], u["k"], start=True, stop=True).then_inc(s_full, 1)
                    i = step - TURN_LAG
                    if 0 <= i < n:
                        u, gu = units[i], u0 + i
                        pe.wait_ge(p_ready, gu + 1)
                        if i >= 2:
                            pe.wait_ge(pt_ready, gu - 1)
                        for a in range(0, u["n"], P):
                            w = min(P, u["n"] - a)
                            mm = pe.transpose(bank[4 + i % 2][0:w, a:a + P], probs(i, SEQ)[:, a:a + w], ident)
                        mm.then_inc(pt_full, 1)
                    i = step - VALUE_LAG
                    if i >= 0:
                        u, gu = units[i], u0 + i
                        pe.wait_ge(pt_ready, gu + 1)
                        grp = GROUP0[family] + u["group"]
                        if u["group"] >= 2 and units[i - 1]["group"] != u["group"]:
                            if family == "last":
                                pe.wait_ge(o_out, u["group"] - 1)
                            else:
                                pe.wait_ge(split_lo, SPLIT0["eattn" if family == "even" else "mattn"] + u["group"] - 1)
                        at, col = u["out"]
                        for b, v in enumerate(u["v"]):
                            kw = v.shape[0]
                            mm = pe.matmul(bank[grp % 2][at:at + 64, col:col + P], v,
                                           tmp[0:kw, 4 + i % 2, P * b:P * (b + 1)],
                                           start=(b == 0 and u.get("first", True)),
                                           stop=(b == len(u["v"]) - 1 and u.get("last", True)))
                        mm.then_inc(pv_done, 1)

            def mlp(layer):
                op, arena0 = f"mlp{layer}", 16 * ((layer + 1) % 2)
                t0, b0 = TILE0[f"up{layer}"], SUB0[f"up{layer}"] // SUBS

                def up(i, j):
                    t = RING * i + (t0 + j)
                    pe.wait_ge(z_ready, t - 3)
                    pe.wait_ge(lo_made, RING * i + (b0 + j + 1))
                    for k in range(KT):
                        mm = product(bank[4 + (t0 + j) % 4][:, :], (b0 + j) % RING, k, *splits[op, k], k == 0, k == KT - 1)
                    mm.then_inc(acc_full, 1)

                head(f"up{layer}", op, op, KT - 2)
                norm_spread(op)
                for j in range(HEAD, RING):
                    up(0, j)
                with pe.Fori(1, FF // P // RING) as i:
                    for j in range(RING):
                        up(i, j)

                b1 = b0 + FF // P
                t1 = t0 + FF // P

                def down(i, j, first, last):
                    pe.wait_ge(lo_made, RING * i + (b1 + j + 1))
                    pe.wait_ge(mlp_lo, RING * i + (layer * FF // P + j + 1))
                    for m in range(KT):
                        if first and m == 4:
                            pe.wait_ge(z_ready, t1)
                        mm = product(bank[m][:, :], (b1 + j) % RING, m, mlp_op[:, 0, j % 2, :], mlp_op[:, 1, j % 2, :], first, last)
                        if last:
                            mm.then_inc(acc_full, 1)
                    if not last:
                        mm.then_inc(block_used, 1)

                for j in range(RING):
                    down(0, j, j == 0, False)
                with pe.Fori(1, FF // P // RING - 1) as i:
                    for j in range(RING):
                        down(i, j, False, False)
                for j in range(RING):
                    down(FF // P // RING - 1, j, False, j == RING - 1)

            pe.wait_ge(con_in, 16)
            head("ein", "even", "even")
            norm_spread("even")
            linear("ein", split_operand("even"), headed=HEAD)
            rotate(0, [(z0(i), TILE0["ein"] + i + 1) for i in range(5)], c("rot_even"), P)
            turn_values([(z0(5), TILE0["ein"] + 6)])
            linear("pool", lambda i, k: (need_split("pool", i), splits["pool", i])[1])
            pe.wait_ge(roped, 5)
            pe.wait_ge(v_tok, 1)
            pe.wait_ge(z_ready, TILE0["eout"])
            attention("even")
            linear("eout", lambda i, k: (need_split("pooled" if k >= 4 else "eattn", k % 4),
                                         splits["pooled" if k >= 4 else "eattn", k % 4])[1],
                   after=behind("mlp0"))
            mlp(0)

            pe.wait_ge(z_ready, TILE0["oin"])
            head("oin", "odd", "odd")
            norm_spread("odd")
            linear("oin", split_operand("odd"), headed=HEAD)
            linear("lru", lambda i, k: (need_split("xc", i % 4), splits["xc", i % 4])[1])
            norm_sums("cq")
            norm_spread("cq")
            norm_sums("ckv")
            norm_spread("ckv")
            linear("uq", split_operand("cq"))
            linear("ukn", split_operand("ckv"))
            linear("uv", split_operand("ckv"))
            rotate(5, [(z1(3), TILE0["oin"] + 4)] + [(z1(12 + h), TILE0["uq"] + h + 1) for h in range(MLA_HEADS)],
                   c("rot_mla"), 96)
            turn_values([(z1(28 + i), TILE0["uv"] + i + 1) for i in range(4)])
            pe.wait_ge(roped, 14)
            pe.wait_ge(key_rope, MLA_HEADS)
            pe.wait_ge(v_tok, 5)
            pe.wait_ge(z_ready, TILE0["oout"])
            attention("mla")
            linear("oout", lambda i, k: (need_split("lru" if k >= 4 else "mattn", k % 4),
                                         splits["lru" if k >= 4 else "mattn", k % 4])[1],
                   after=behind("mlp1"))
            mlp(1)

            pe.wait_ge(z_ready, TILE0["zin"])
            head("zin", "mix2", "final")
            norm_spread("final")
            norm_spread("mix2")
            def at_zin(n):
                if n == 8:
                    pe.wait_ge(silu_made, 1)
                    for t in range(TT):
                        mm = pe.transpose(bank[0][:, 32 * t:32 * (t + 1)], z2(17)[0:32, P * t:P * (t + 1)],
                                          ident[0:32, 0:32])
                    mm.then_inc(gates_turned, 1)
                if 11 <= n < 16:
                    pe.wait_ge(gates_ready, 1)
                    i = (14, 16, 27, 28, 29)[n - 11]
                    turn_values([(z2(i), TILE0["zin"] + ZIN.index(i) + 1)])
                if n == 20:
                    pe.wait_ge(hid_made, 1)
                    pe.matmul(bank[2][:, 0:32], g("w2k", 0, P), hid[:, 0, :], start=True, stop=True).then_inc(cmp_full, 1)
                    pe.wait_ge(hid_made, 2)
                    pe.matmul(bank[3][0:32, 0:P], hid[:, 1, :], g("w2v", 0, P), start=True, stop=True).then_inc(cmp_full, 1)

            def compress(i):
                b, kv = SUB0[f"cmp{i}"] // SUBS, i // 4
                pe.wait_ge(lo_made, b + 1)
                for k in range(SUBS):
                    pos = SUBS * (i % 4) + k
                    half, at = divmod(pos, CMP_STRIDE)
                    need_split("cmp", 2 * kv + half)
                    hi, lo = (ap[:, at:at + 31 * CMP_STRIDE + 1:CMP_STRIDE] for ap in splits["cmp", 2 * kv + half])
                    mm = product(bank[2 + kv][:, 0:32], b % RING, k, hi, lo, pos == 0, pos == CMP_BLOCK - 1)
                mm.then_inc(block_used, 1)

            linear("zin", split_operand("mix2"), headed=HEAD)
            for i in range(8):
                linear(f"zin_by{i}", split_operand("mix2"), after=lambda _, i=i: at_zin(6 + i))
                compress(i)
            linear("zin_rest", split_operand("mix2"), after=lambda i: at_zin(14 + i))
            pe.wait_ge(cmp_ready, 2)
            pe.wait_ge(v_tok, 10)
            pe.wait_ge(z_ready, TILE0["out2"])
            attention("last")
            pe.wait_ge(lse_ready, 1)
            for gi in range(3):
                for t in range(TT):
                    mm = pe.matmul(bank[2 + gi][:, P * t:P * (t + 1)],
                                   tmp[:, gi, P * t:P * (t + 1)], ident, start=True, stop=True)
                mm.then_inc(lse_full, 1)

            def out2_operand(i, k):
                name, j = ("conv2", k) if k < 2 else ("nsa", k - 2) if k < 5 else ("dil", k - 5)
                need_split(name, j)
                return splits[name, j]

            linear("out2", out2_operand)

            def ple_operand(i, k):
                if i % 2 == 0:
                    need_split("ple", k)
                    return splits["ple", k]
                pe.wait_ge(mlp_lo, 2 * FF // P + 2) if i == 1 and k == 0 else None
                return mlp_op[:, 0, k, :], mlp_op[:, 1, k, :]

            linear("ple", ple_operand, subs=lambda i: 2 if i % 2 else 8,
                   after=lambda i: norm_sums("out", [i // 2 - 1]) if i % 2 and i > 1 else None)
            norm_sums("out", [KT - 1])
            norm_spread("out")

        @block.scalar
        def _(act):
            prepared = [0]

            def prepare(n):
                while prepared[0] <= min(n, NBLOCKS - 1):
                    b = prepared[0]
                    act.wait_ge(raw_in[b % RING], 16 * (b // RING + 1))
                    if b >= RING:
                        what, count = BLOCK_END[b - RING]
                        act.wait_ge(acc_full if what == "tile" else block_used, count)
                    nc.scalar.activation(w_hi[:, b % RING, :], raw[:, b % RING, :], ACT.Copy).then_inc(hi_made, 1)
                    prepared[0] += 1

            def prepare_stage(name):
                i = [s[0] for s in STAGES].index(name)
                end = SUB0[STAGES[i + 1][0]] if i + 1 < len(STAGES) else NBLOCKS * SUBS
                prepare(end // SUBS - 1 + RING - 1)

            def hi_of(name, i, src, scale=1.0):
                nc.scalar.activation(splits[name, i][0], src, ACT.Copy, scale=scale).then_inc(split_hi, 1)

            def square(name, m, src, scale=1.0):
                q = SQ0[name] + m
                if q >= 2:
                    act.wait_ge(sq_used, q - 1)
                nc.scalar.activation(tmp[:, 4 + q % 2, :], src, ACT.Square, scale=scale).then_inc(sq_ready, 1)

            def root(name, n):
                act.wait_ge(sq_used, SQ0[name] + NORM_TILES[name])
                nc.scalar.activation(std[:, NORM[name], :], bank[0][:, 0:TT], ACT.Sqrt, bias=c("eps"),
                                     scale=1.0 / n).then_inc(std_ready, 1)

            def norm(name, gain, ready, stage=None):
                for m in range(KT):
                    if stage:
                        prepare(SUB0[stage] // SUBS + m + RING - 1)
                    ready(m)
                    square(name, m, x[:, m, :])
                    if gain:
                        hi_of(name, m, x[:, m, :], g(gain, m))
                root(name, D)

            def rows(stage):
                return lambda m: act.wait_ge(z_ready, TILE0[stage] + m + 1)

            def attention(family, evacuate):
                units, u0 = FAMILY[family], UNIT0[family]
                n = len(units)
                for step in range(n + VALUE_LAG + 1):
                    if step < n:
                        u, gu = units[step], u0 + step
                        act.wait_ge(masked, gu + 1)
                        if u["sink"] is not None:
                            act.wait_ge(sink_put, gu + 1)
                        if step >= 4:
                            act.wait_ge(pt_full, gu - 3)
                        w = u["n"] + (u["sink"] is not None)
                        nc.scalar.activation(probs(step, w), tmp[:, step % 2, 0:w], ACT.Exp,
                                             bias=negm[:, step:step + 1], scale=-1.0,
                                             accum_out=den[:, step:step + 1]).then_inc(exp_done, 1)
                    i = step - TURN_LAG
                    if 0 <= i < n:
                        u, gu = units[i], u0 + i
                        act.wait_ge(pt_full, gu + 1)
                        if i >= 2:
                            act.wait_ge(pv_done, gu - 1)
                        w, m = (u["n"] + P - 1) // P * P, min(P, u["n"])
                        nc.scalar.activation(tmp[0:m, 4 + i % 2, 0:w], bank[4 + i % 2][0:m, 0:w],
                                             ACT.Copy).then_inc(pt_ready, 1)
                    for k in groups_after(family, step):
                        evacuate(k)

            def group_done(family, k):
                act.wait_ge(pv_done, UNIT0[family] + last_of(family, k) + 1)

            def mlp(layer):
                t0, b0 = TILE0[f"up{layer}"], SUB0[f"up{layer}"] // SUBS
                arena0 = 16 * ((layer + 1) % 2)
                used0 = BLOCK_END[b0 + FF // P][1] - 1
                prepare(b0 + RING - 2)

                def ahead(i, j, base, first=False):
                    b = base + j + RING - 1
                    act.wait_ge(raw_in[b % RING], 16 * i + 16 * (b // RING + 1))
                    if base == b0 or first:
                        act.wait_ge(acc_full, RING * i + (TILE0[f"up{layer}"] + base - b0 + j))
                    else:
                        act.wait_ge(block_used, RING * i + (used0 + j))
                    nc.scalar.activation(w_hi[:, b % RING, :], raw[:, b % RING, :], ACT.Copy).then_inc(hi_made, 1)

                with act.Fori(0, FF // P // RING) as i:
                    for j in range(RING):
                        ahead(i, j, b0)
                        t = RING * i + (t0 + j)
                        act.wait_ge(acc_full, t + 1)
                        act.wait_ge(z_ready, t - 1)
                        nc.scalar.activation(tmp[:, j % 2, :], bank[4 + (t0 + j) % 4][:, :], ACT.Relu).then_inc(relu_made, 1)

                b1, t1, k0 = b0 + FF // P, t0 + FF // P, layer * FF // P
                src = arena[:, arena0:arena0 + FF // P, :].rearrange("p a b -> p (a b)")
                for k in range(2):
                    act.wait_ge(z_ready, t0 + k + 1)
                    nc.scalar.activation(mlp_op[:, 0, k, :], src[:, SEQ * k:SEQ * (k + 1)], ACT.Copy).then_inc(mlp_hi, 1)

                def down(i, j):
                    ahead(i, j, b1)
                    act.wait_ge(z_ready, t1)
                    nc.scalar.activation(mlp_op[:, 0, (j + 1) % 2, :], src[:, bass.ds(SEQ * RING * i + SEQ * (j + 1), SEQ)],
                                         ACT.Copy).then_inc(mlp_hi, 1)

                for j in range(RING):
                    if j == 0:
                        ahead(0, 0, b1, True)
                    else:
                        down(0, j)
                with act.Fori(1, FF // P // RING - 1) as i:
                    for j in range(RING):
                        down(i, j)
                for j in range(RING):
                    if j < RING - 1:
                        down(FF // P // RING - 1, j)
                    else:
                        ahead(FF // P // RING - 1, j, b1)
                prepared[0] = b1 + FF // P + RING - 1

            act.dma_start(par[:, :], params).then_inc(par_in, 16)
            for m in range(RING, KT):
                act.dma_start(x[:, m, :], x_t[P * m:P * (m + 1), :]).then_inc(x_in[m], 16)
            act.dma_start(con[:, :], consts).then_inc(con_in, 16)
            act.dma_start(rope[:, :, :], ropes[0]).then_inc(rope_in, 16)
            act.dma_start(arena[:, 29:33, :], invcnt).then_inc(inv_in, 16)
            act.wait_ge(par_in, 16)

            def arrived(m):
                act.wait_ge(x_in[m], 16)
                if m < RING - 1:
                    prepare(m)
                if m == KT - 1:
                    act.wait_ge(con_in, 16)

            norm("even", "g_even", arrived)
            nc.scalar.activation(small[:, 0, :], g("lam", 0, 8), ACT.Abs).then_inc(lam_act, 1)
            act.wait_ge(lam_act, 1)
            nc.scalar.activation(small[:, 1, :], small[:, 0, :], ACT.Exp, scale=-1.0).then_inc(lam_act, 1)
            prepare_stage("ein")
            for i in range(4):
                act.wait_ge(src_ready, i + 1)
                act.wait_ge(acc_full, TILE0["ein"] + 10)
                hi_of("pool", i, z0(14 + i))
            prepare_stage("pool")
            for i in range(4):
                act.wait_ge(z_ready, TILE0["pool"] + i + 1)
                hi_of("pooled", i, z0(10 + i))

            def even_out(k):
                if k == 0:
                    act.wait_ge(acc_full, TILE0["pool"] + 4)
                group_done("even", k)
                hi_of("eattn", k, bank[(GROUP0["even"] + k) % 2][:, :])

            attention("even", even_out)
            act.dma_start(rope[:, :, :], ropes[1]).then_inc(rope_in, 16)
            norm("mlp0", "g_mlp0", rows("eout"), "eout")
            mlp(0)

            norm("odd", "g_odd", rows("down0"))
            prepare_stage("oin")
            for i in range(4):
                act.wait_ge(src_ready, 4 + i + 1)
                act.wait_ge(acc_full, TILE0["oin"] + 12)
                hi_of("xc", i, z1(28 + i))
            prepare_stage("lru")
            for i in range(16):
                act.wait_ge(z_ready, TILE0["lru"] + i + 1)
                nc.scalar.activation(z1(12 + i), z1(12 + i), ACT.Sigmoid).then_inc(gate_sig, 1)
            act.wait_ge(sp_made, 2)

            def decay_tmp(u):
                return z1(4 + u) if u < 4 else tmp[:, u - 4, :]

            def gate_tile(kind, u):
                return z1(12 + 8 * (u // 4) + 4 * kind + u % 4)

            for u in range(8):
                act.wait_ge(gate_sig, 8 * (u // 4) + u % 4 + 1)
                nc.scalar.activation(decay_tmp(u), gate_tile(0, u), ACT.Exp, scale=small[:, 14, u:u + 1]).then_inc(decay_made, 1)
                nc.scalar.activation(gate_tile(0, u), gate_tile(0, u), ACT.Tanh, scale=small[:, 15, u:u + 1]).then_inc(decay_made, 1)
            for u in range(8):
                act.wait_ge(beta_sq, u + 1)
                nc.scalar.activation(decay_tmp(u), decay_tmp(u), ACT.Sqrt, scale=-1.0).then_inc(beta_made, 1)
            for j in range(4):
                nc.scalar.activation(z1(8 + j), z1(8 + j), ACT.Gelu_apprx_tanh).then_inc(gelu_made, 1)
            act.wait_ge(src_ready, 12)
            for m in range(2):
                square("cq", m, z1(m))
                hi_of("cq", m, z1(m), g("g_cq", m))
            root("cq", 2 * P)
            square("ckv", 0, z1(2))
            hi_of("ckv", 0, z1(2), g("g_ckv"))
            root("ckv", P)
            prepare_stage("uq")
            prepare_stage("ukn")
            prepare_stage("uv")
            act.wait_ge(roped, 6)
            for h in range(MLA_HEADS):
                act.wait_ge(z_ready, TILE0["ukn"] + h + 1)
                nc.scalar.activation(z1(20 + h)[64:96, :], z1(3)[64:96, :], ACT.Copy).then_inc(key_rope, 1)
            for i in range(4):
                act.wait_ge(acc_full, TILE0["uv"] + 4)
                hi_of("lru", i, z1(8 + i))

            def mla_out(k):
                group_done("mla", k)
                hi_of("mattn", k, bank[(GROUP0["mla"] + k) % 2][:, :])

            attention("mla", mla_out)
            norm("mlp1", "g_mlp1", rows("oout"), "oout")
            mlp(1)

            act.wait_ge(src_ready, 13)
            for m in range(KT):
                act.wait_ge(z_ready, TILE0["down1"] + m + 1)
                square("final", 2 * m, x[:, m, :])
                square("final", 2 * m + 1, x[:, m, :], g("g_final", m))
                hi_of("mix2", m, x[:, m, :], small[:, 12, m:m + 1])
            root("final", D)
            act.wait_ge(src_ready, 14)
            nc.scalar.activation(std[:, NORM["mix2"], :], small[:, 11, 0:TT], ACT.Sqrt, bias=c("eps"),
                                 scale=1.0 / D).then_inc(std_ready, 1)
            block0 = SUB0["zin"] // SUBS
            for n in range(33):
                prepare(block0 + n + min(max(n - 6, 0), 8) + RING - 1)
                if n == 3:
                    for i in range(4):
                        act.wait_ge(src_ready, 14 + i + 1)
                        hi_of("cmp", i, tmp[:, i, :])
                if n == 7:
                    act.wait_ge(z_ready, TILE0["zin"] + ZIN.index(17) + 1)
                    nc.scalar.activation(z2(17)[0:32, :], z2(17)[0:32, :], ACT.Sigmoid).then_inc(silu_made, 1)
                if n == 17:
                    for i in range(2):
                        act.wait_ge(hid_in, i + 1)
                        nc.scalar.activation(hid[:, 2 + i, :], hid[:, i, :], ACT.Sigmoid).then_inc(hid_sig, 1)
                for i in {20: (6, 7), 26: (18, 19, 20, 30, 31, 32)}.get(n, ()):
                    act.wait_ge(z_ready, TILE0["zin"] + ZIN.index(i) + 1)
                    nc.scalar.activation(z2(i), z2(i), ACT.Silu).then_inc(silu_made, 1)
            for i in range(2):
                act.wait_ge(src_ready, 18 + i + 1)
                act.wait_ge(acc_full, TILE0["zin"] + 33)
                hi_of("conv2", i, z2(4 + i))

            def last_out(k):
                if k < NSA_R:
                    act.wait_ge(o_out, k + 1)
                    hi_of("nsa", k, z2(18 + k))

            attention("last", last_out)
            first = 3 * TT * 2 * NSA_R
            nc.scalar.activation(rden[:, 0:24], den[:, first:first + 24], ACT.Ln).then_inc(log_den, 1)
            for gi in range(3):
                act.wait_ge(ls_max, gi + 1)
                nc.scalar.activation(z2(24 + gi), z2(24 + gi), ACT.Exp).then_inc(lse_exp, 1)
            for gi in range(3):
                act.wait_ge(src_ready, 20 + gi + 1)
                hi_of("dil", gi, z2(30 + gi))
            act.dma_start(arena[:, 24:26, :], p_t.rearrange("(m p) n -> p m n", p=P)).then_inc(p_in, 16)
            act.wait_ge(p_in, 16)
            for k in range(2):
                nc.scalar.activation(mlp_op[:, 0, k, :], arena[:, 24 + k, :], ACT.Copy).then_inc(mlp_hi, 1)
            for m in range(KT):
                prepare(SUB0["out2"] // SUBS + m + RING - 1)
                act.wait_ge(z_ready, TILE0["out2"] + m + 1)
                hi_of("ple", m, x[:, m, :])
            for m in range(KT):
                prepare((SUB0["ple"] + 10 * m + 9) // SUBS + RING - 1)
                act.wait_ge(z_ready, TILE0["ple"] + 2 * m + 1)
                nc.scalar.activation(tmp[:, m % 2, :], tmp[:, m % 2, :], ACT.Sigmoid).then_inc(ple_sig, 1)
                act.wait_ge(z_ready, TILE0["ple"] + 2 * m + 2)
                square("out", m, x[:, m, :])
            root("out", D)

        @block.vector
        def _(dve):
            steps = [0]

            def mark(ins):
                ins.then_inc(vstep, 1)
                steps[0] += 1
                return steps[0]

            def step(ins):
                dve.wait_ge(vstep, mark(ins))

            TTn, TS, STT = nc.vector.tensor_tensor, nc.vector.tensor_scalar, nc.vector.scalar_tensor_tensor

            def lo_of(name, i, src, scale=None):
                e = SPLIT0[name] + i
                dve.wait_ge(split_hi, e + 1)
                hi, lo = splits[name, i]
                if scale is None:
                    return TTn(lo, src, hi.bitcast(F32), ALU.subtract).then_inc(split_lo, 1)
                return STT(lo, src, scale, hi.bitcast(F32), ALU.mult, ALU.subtract).then_inc(split_lo, 1)

            def spread(name, slot=0, then=None, gain=None):
                k = NORM[name]
                dve.wait_ge(std_ready, k + 1)
                if gain is None:
                    nc.vector.reciprocal(rtok[:, k, :], std[:, k, :]).then_inc(rtok_ready, 1)
                else:
                    step(nc.vector.reciprocal(small[:, 9, 0:TT], std[:, k, :]))
                    TTn(rtok[:, k, :], small[:, 9, 0:TT], gain, ALU.mult).then_inc(rtok_ready, 1)
                if then:
                    dve.wait_ge(rtok_ready, k + 1)
                    then()
                dve.wait_ge(rms_full, k + 1)
                nc.vector.tensor_copy(rms[:, slot, :], bank[1][:, :]).then_inc(rms_ready, 1)
                dve.wait_ge(rms_ready, k + 1)

            def norm(name, gain, ready=None):
                for m in range(KT):
                    if ready:
                        ready(m)
                    lo_of(name, m, x[:, m, :], g(gain, m))
                spread(name)

            def taken(name, i):
                t = TILE0[name] + i
                dve.wait_ge(acc_full, t + 1)
                return bank[4 + t % 4]

            def scaled(name, i, out, slot=0, m=P):
                src = taken(name, i)
                TTn(out[0:m, :], src[0:m, :], rms[0:m, slot, :], ALU.mult).then_inc(z_ready, 1)

            def residual(name):
                for m in range(KT):
                    src = taken(name, m)
                    TTn(x[:, m, :], src[:, :], x[:, m, :], ALU.add).then_inc(z_ready, 1)

            def rotate(first, tiles, m):
                for i, tile in enumerate(tiles):
                    dve.wait_ge(rot_full, first + i + 1)
                    if i >= 2:
                        dve.wait_ge(roped, first + i - 1)
                    a, b = tmp[0:m, 2 * (i % 2), :], tmp[0:m, 2 * (i % 2) + 1, :]
                    mark(TTn(a, tile[0:m, :], rope[0:m, 0, :], ALU.mult))
                    step(TTn(b, bank[2 + i % 2][0:m, :], rope[0:m, 1, :], ALU.mult))
                    TTn(tile[0:m, :], a, b, ALU.add).then_inc(roped, 1)

            values = [0]

            def turn_values(tiles):
                for tile in tiles:
                    values[0] += 1
                    dve.wait_ge(turned, values[0])
                    nc.vector.tensor_copy(tile, bank[(values[0] - 1) % 2][:, :]).then_inc(v_tok, 1)

            def attention(family, evacuate):
                units, u0 = FAMILY[family], UNIT0[family]
                n = len(units)
                for s in range(n + VALUE_LAG + 1):
                    i = s - NORM_LAG
                    if 0 <= i < n:
                        dve.wait_ge(exp_done, u0 + i + 1)
                        inverted = mark(nc.vector.reciprocal(rden[:, i:i + 1], den[:, i:i + 1]))
                    if s < n:
                        u, gu = units[s], u0 + s
                        if s >= 2:
                            dve.wait_ge(exp_done, gu - 1)
                        if u["sink"] is not None:
                            col = small[:, 13, u["sink"]:u["sink"] + 1]
                            nc.vector.tensor_copy(tmp[:, s % 2, u["n"]:u["n"] + 1], col).then_inc(sink_put, 1)
                        dve.wait_ge(s_full, gu + 1)
                        nc.vector.tensor_tensor_reduce(
                            tmp[:, s % 2, 0:u["n"]], bank[2 + s % 2][:, 0:u["n"]], u["mask"], -u["scale"],
                            3e38 if u["sink"] is None else col, ALU.add, ALU.min, negm[:, s:s + 1]).then_inc(masked, 1)
                    if 0 <= i < n:
                        u = units[i]
                        dve.wait_ge(vstep, inverted)
                        pr = probs(i, u["n"])
                        if u["gate"] is None:
                            TS(pr, pr, rden[:, i:i + 1], None, ALU.mult).then_inc(p_ready, 1)
                        else:
                            TS(pr, pr, rden[:, i:i + 1], u["gate"], ALU.mult, ALU.mult).then_inc(p_ready, 1)
                    for k in groups_after(family, s):
                        evacuate(k)

            def group_bank(family, k):
                dve.wait_ge(pv_done, UNIT0[family] + last_of(family, k) + 1)
                return bank[(GROUP0[family] + k) % 2]

            def mlp(layer):
                t0 = TILE0[f"up{layer}"]
                arena0 = 16 * ((layer + 1) % 2)
                u = arena[:, arena0:arena0 + FF // P, :].rearrange("p a b -> p (a b)")
                step(TTn(rms[:, 1, :], rms[:, 0, :], rms[:, 0, :], ALU.mult))
                v0 = steps[0]
                with dve.Fori(0, FF // P // RING) as i:
                    for j in range(RING):
                        t = RING * i + (t0 + j)
                        dve.wait_ge(relu_made, RING * i + (layer * FF // P + j + 1))
                        TTn(tmp[:, j % 2, :], tmp[:, j % 2, :], rms[:, 1, :], ALU.mult).then_inc(vstep, 1)
                        dve.wait_ge(vstep, RING * i + (v0 + j + 1))
                        TTn(u[:, bass.ds(SEQ * RING * i + SEQ * j, SEQ)], bank[4 + (t0 + j) % 4][:, :], tmp[:, j % 2, :],
                            ALU.mult).then_inc(z_ready, 1)
                steps[0] += FF // P
                with dve.Fori(0, FF // P // RING) as i:
                    for j in range(RING):
                        dve.wait_ge(mlp_hi, RING * i + (layer * FF // P + j + 1))
                        TTn(mlp_op[:, 1, j % 2, :], u[:, bass.ds(SEQ * RING * i + SEQ * j, SEQ)],
                            mlp_op[:, 0, j % 2, :].bitcast(F32), ALU.subtract).then_inc(mlp_lo, 1)
                for m in range(KT):
                    dve.wait_ge(acc_full, TILE0[f"down{layer}"] + m + 1)
                    TTn(x[:, m, :], bank[m][:, :], x[:, m, :], ALU.add).then_inc(z_ready, 1)

            def cut_conv(out, src, taps, w, bias, done=None):
                at = [i for i, s in enumerate(taps) if s == 0][0]
                step(TS(out, src, w(at), bias, ALU.mult, ALU.add))
                others = [i for i, s in enumerate(taps) if s]
                for i in others:
                    a, b = max(0, -taps[i]), SEQ - max(0, taps[i])
                    ins = STT(out[:, a:b], src[:, a + taps[i]:b + taps[i]], w(i), out[:, a:b], ALU.mult, ALU.add)
                    if done is not None and i == others[-1]:
                        ins.then_inc(done, 1)
                    else:
                        step(ins)

            def log_decay():
                dve.wait_ge(lam_act, 2)
                step(TS(small[:, 2, :], small[:, 1, :], 2.0, None, ALU.add))
                step(nc.vector.reciprocal(small[:, 3, :], small[:, 2, :]))
                step(TTn(small[:, 4, :], small[:, 3, :], small[:, 1, :], ALU.mult))
                step(TTn(small[:, 5, :], small[:, 4, :], small[:, 4, :], ALU.mult))
                terms = 10
                step(TS(small[:, 6, :], small[:, 5, :], 1.0 / (2 * terms + 1), 1.0 / (2 * terms - 1), ALU.mult, ALU.add))
                for k in range(terms - 2, -1, -1):
                    step(TTn(small[:, 6, :], small[:, 6, :], small[:, 5, :], ALU.mult))
                    step(TS(small[:, 6, :], small[:, 6, :], 1.0 / (2 * k + 1), None, ALU.add))
                step(TTn(small[:, 7, :], small[:, 6, :], small[:, 4, :], ALU.mult))
                step(TS(small[:, 8, :], g("lam", 0, 8), -1.0, 0.0, ALU.mult, ALU.max))
                step(STT(small[:, 9, :], small[:, 7, :], 2.0, small[:, 8, :], ALU.mult, ALU.add))
                TS(small[:, 14, :], small[:, 9, :], -LRU_C, None, ALU.mult).then_inc(sp_made, 1)
                TS(small[:, 15, :], small[:, 9, :], -LRU_C / 2, None, ALU.mult).then_inc(sp_made, 1)

            dve.wait_ge(par_in, 16)
            TS(small[:, 13, :], g("sink", 0, 8), -1.0, None, ALU.mult)

            norm("even", "g_even", lambda m: dve.wait_ge(x_in[m], 16))
            log_decay()
            for i in range(10):
                scaled("ein", i, z0(i))
            dve.wait_ge(rope_in, 16)
            rotate(0, [z0(i) for i in range(5)], P)
            turn_values([z0(5)])
            dve.wait_ge(inv_in, 16)
            wide = [tmp[:, 2 * i:2 * i + 2, :].rearrange("p a b -> p (a b)") for i in range(2)]
            for grp in range(4):
                u = z0(6 + grp)
                dve.wait_ge(z_ready, TILE0["ein"] + 6 + grp + 1)
                if grp:
                    dve.wait_ge(src_ready, grp)
                else:
                    dve.wait_ge(roped, 5)
                step(nc.vector.memset(wide[0][:, 0:8], 0.0))
                step(nc.vector.memset(wide[0][:, SEQ + 8:SEQ + 16], 0.0))
                step(nc.vector.tensor_copy(wide[0][:, 8:SEQ + 8], u))
                step(TTn(wide[1][:, 1:SEQ + 16], wide[0][:, 0:SEQ + 15], wide[0][:, 1:SEQ + 16], ALU.add))
                a, lo, hi = 1, 1, SEQ + 16
                for k in range(grp):
                    h = 1 << k
                    lo, hi = lo + h, hi - h
                    step(TTn(wide[1 - a][:, lo:hi], wide[a][:, lo - h:hi - h], wide[a][:, lo + h:hi + h], ALU.add))
                    a = 1 - a
                total = wide[a][:, 8:SEQ + 8]
                step(TTn(total, total, arena[:, 29 + grp, :], ALU.mult))
                TTn(z0(14 + grp), total, u, ALU.subtract).then_inc(src_ready, 1)
            for i in range(4):
                lo_of("pool", i, z0(14 + i))
            for i in range(4):
                src = taken("pool", i)
                TS(z0(10 + i), src[:, :], g("pool_scale", i), None, ALU.mult).then_inc(z_ready, 1)
            for i in range(4):
                lo_of("pooled", i, z0(10 + i))

            def even_out(k):
                src = group_bank("even", k)
                lo_of("eattn", k, src[:, :])

            dve.wait_ge(src_ready, 4)
            attention("even", even_out)
            residual("eout")
            norm("mlp0", "g_mlp0")
            mlp(0)

            norm("odd", "g_odd")
            for i in range(12):
                scaled("oin", i, z1(i))
            for j in range(4):
                dve.wait_ge(z_ready, TILE0["oin"] + 4 + j + 1)
                cut_conv(z1(28 + j), z1(4 + j), (-2, -1, 0, 1), lambda i, j=j: g("conv_w", 4 * i + j), g("conv_b", j),
                         src_ready)
            for j in range(4):
                lo_of("xc", j, z1(28 + j))
            for i in range(16):
                src = taken("lru", i)
                TS(z1(12 + i), src[:, :], g("gate_b", i), None, ALU.add).then_inc(z_ready, 1)

            def decay_tmp(u):
                return z1(4 + u) if u < 4 else tmp[:, u - 4, :]

            def gate_tile(kind, u):
                return z1(12 + 8 * (u // 4) + 4 * kind + u % 4)

            for u in range(8):
                dve.wait_ge(decay_made, 2 * u + 2)
                e, r = decay_tmp(u), gate_tile(0, u)
                step(STT(e, e, 1.0, r, ALU.add, ALU.mult))
                step(TS(r, e, 1.0, None, ALU.add))
                STT(e, r, 1.0, e, ALU.add, ALU.mult).then_inc(beta_sq, 1)
            for u in range(8):
                dve.wait_ge(gate_sig, 8 * (u // 4) + 4 + u % 4 + 1)
                ig = gate_tile(1, u)
                step(TTn(ig, ig, z1(28 + u % 4), ALU.mult))
                dve.wait_ge(beta_made, u + 1)
                step(TTn(ig, ig, decay_tmp(u), ALU.mult))
                back = slice(None, None, -1) if u >= 4 else slice(None)
                ins = nc.vector.tensor_tensor_scan(decay_tmp(u)[:, back], gate_tile(0, u)[:, back], ig[:, back], 0.0,
                                                   ALU.mult, ALU.add)
                step(ins)
                if u >= 4:
                    j = u - 4
                    step(TTn(decay_tmp(j), decay_tmp(j), decay_tmp(u), ALU.add))
                    dve.wait_ge(gelu_made, j + 1)
                    TTn(z1(8 + j), z1(8 + j), decay_tmp(j), ALU.mult).then_inc(src_ready, 1)
            for m in range(2):
                lo_of("cq", m, z1(m), g("g_cq", m))
            spread("cq", 1)
            lo_of("ckv", 0, z1(2), g("g_ckv"))
            spread("ckv", 2)
            for h in range(MLA_HEADS):
                scaled("uq", h, z1(12 + h), 1, 96)
            for h in range(MLA_HEADS):
                scaled("ukn", h, z1(20 + h), 2, 64)
            for i in range(4):
                scaled("uv", i, z1(28 + i), 2)
            dve.wait_ge(rope_in, 32)
            rotate(5, [z1(3)] + [z1(12 + h) for h in range(MLA_HEADS)], 96)
            turn_values([z1(28 + i) for i in range(4)])
            for i in range(4):
                lo_of("lru", i, z1(8 + i))

            def mla_out(k):
                src = group_bank("mla", k)
                lo_of("mattn", k, src[:, :])

            attention("mla", mla_out)
            residual("oout")
            TTn(small[:, 12, :], g("g_final", 0, 8), g("g_mix2", 0, 8), ALU.mult).then_inc(src_ready, 1)
            norm("mlp1", "g_mlp1")
            mlp(1)

            def second_norm():
                first = rtok[:, NORM["final"], :]
                step(TTn(small[:, 11, 4:8], first, first, ALU.mult))
                TTn(small[:, 11, 0:TT], small[:, 11, 4:8], bank[0][:, TT:2 * TT], ALU.mult).then_inc(src_ready, 1)

            for m in range(KT):
                lo_of("mix2", m, x[:, m, :], small[:, 12, m:m + 1])
            spread("final", 1, then=second_norm)
            spread("mix2", gain=rtok[:, NORM["final"], :])
            def code_positions():
                for i in range(4):
                    kv, half = i // 2, i % 2
                    code = g("pe", CMP_BLOCK * kv + CMP_STRIDE * half, CMP_STRIDE).rearrange("p (o i) -> p o i", o=1)
                    n = SEQ // CMP_STRIDE - half
                    if half:
                        step(nc.vector.memset(tmp[:, i, CMP_STRIDE * n:], 0.0))
                    TTn(tmp[:, i, 0:CMP_STRIDE * n].rearrange("p (n i) -> p n i", i=CMP_STRIDE),
                        z2(11 + kv)[:, CMP_STRIDE * half:].rearrange("p (n i) -> p n i", i=CMP_STRIDE),
                        code.broadcast_to([P, n, CMP_STRIDE]), ALU.add).then_inc(src_ready, 1)
                for i in range(4):
                    lo_of("cmp", i, tmp[:, i, :])

            def gated_conv(j):
                step(TTn(z2(2 + j), z2(2 + j), z2(4 + j), ALU.mult))
                cut_conv(z2(4 + j), z2(2 + j), (-2, -1, 0), lambda i: g("conv2_w", 2 * i + j), g("conv2_b", j))
                step(TTn(z2(4 + j), z2(4 + j), z2(j), ALU.mult))

            for n, i in enumerate(ZIN):
                if i == 18:
                    dve.wait_ge(block_used, BLOCK_END[SUB0["cmp7"] // SUBS][1])
                gi = (i - 21) % 3
                if 21 <= i < 30 and gi:
                    src = taken("zin", n)
                    r = DILATIONS[gi]
                    TTn(residues(z2(i), r), dilate(src[:, :], r), dilate(rms[:, 0, :], r), ALU.mult).then_inc(z_ready, 1)
                else:
                    scaled("zin", n, z2(i))
                if n == 2:
                    dve.wait_ge(z_ready, TILE0["zin"] + 2)
                    code_positions()
                if HEAD < n <= HEAD + KT:
                    m = n - HEAD - 1
                    STT(x[:, m, :], x[:, m, :], g("g_final", m), rms[:, 1, :], ALU.mult, ALU.mult)
                if n == 9:
                    dve.wait_ge(gates_turned, 1)
                    step(nc.vector.tensor_copy(gates[:, :], bank[0][:, 0:TT * 32]))
                    TS(gates[:, 0:18:3], gates[:, 0:18:3], c("late"), None, ALU.mult).then_inc(gates_ready, 1)
                if 12 <= n < 17:
                    turn_values([z2((14, 16, 27, 28, 29)[n - 12])])
                if n == 15:
                    for kv in range(2):
                        dve.wait_ge(block_used, BLOCK_END[SUB0[f"cmp{4 * kv + 3}"] // SUBS][1])
                        nc.vector.tensor_copy(hid[:, kv, :], bank[2 + kv][:, 0:32]).then_inc(hid_in, 1)
                if n in (17, 18):
                    dve.wait_ge(z_ready, TILE0["zin"] + 16)
                    gated_conv(n - 17)
                if n == 19:
                    for kv in range(2):
                        dve.wait_ge(hid_sig, kv + 1)
                        TTn(hid[:, kv, :], hid[:, kv, :], hid[:, 2 + kv, :], ALU.mult).then_inc(hid_made, 1)
                if n == 21:
                    dve.wait_ge(cmp_full, 1)
                    nc.vector.tensor_copy(cmpk[:, :], bank[2][:, 0:32]).then_inc(cmp_ready, 1)
                    dve.wait_ge(cmp_full, 2)
                    nc.vector.tensor_copy(cmpv[:, :], bank[3][0:32, 0:P]).then_inc(cmp_ready, 1)
                if n == 22:
                    for j in range(2):
                        dve.wait_ge(silu_made, 2 + j)
                        TTn(z2(4 + j), z2(4 + j), z2(6 + j), ALU.mult).then_inc(src_ready, 1)
            for j in range(2):
                lo_of("conv2", j, z2(4 + j))
            dve.wait_ge(silu_made, 9)

            def last_out(k):
                src = group_bank("last", k)
                if k < NSA_R:
                    TTn(z2(18 + k), src[:, :], z2(18 + k), ALU.mult).then_inc(o_out, 1)
                    lo_of("nsa", k, z2(18 + k))
                else:
                    r = DILATIONS[k - NSA_R]
                    nc.vector.tensor_copy(dilate(z2(21 + k - NSA_R), r), residues(src[:, :], r)).then_inc(o_out, 1)

            attention("last", last_out)
            dve.wait_ge(log_den, 1)
            first = 3 * TT * 2 * NSA_R
            step(TTn(rden[:, 24:48], rden[:, 0:24], negm[:, first:first + 24], ALU.subtract))
            nc.vector.tensor_copy(tmp[:, 0:3, :].rearrange("p a (b e) -> p (a b) e", e=64),
                                  rden[:, 24:48].rearrange("p (n o) -> p n o", o=1).broadcast_to([P, 24, 64])).then_inc(lse_ready, 1)
            for gi in range(3):
                r = DILATIONS[gi]
                dve.wait_ge(lse_full, gi + 1)
                step(nc.vector.tensor_copy(dilate(z2(24 + gi), r), residues(bank[2 + gi][:, :], r)))
            step(TTn(tmp[:, 3, :], z2(24), z2(25), ALU.max))
            step(TTn(tmp[:, 3, :], tmp[:, 3, :], z2(26), ALU.max))
            for gi in range(3):
                TTn(z2(24 + gi), z2(24 + gi), tmp[:, 3, :], ALU.subtract).then_inc(ls_max, 1)
            dve.wait_ge(lse_exp, 3)
            step(TTn(tmp[:, 4, :], z2(24), z2(25), ALU.add))
            step(TTn(tmp[:, 4, :], tmp[:, 4, :], z2(26), ALU.add))
            step(nc.vector.reciprocal(tmp[:, 5, :], tmp[:, 4, :]))
            for gi in range(3):
                step(TTn(z2(24 + gi), z2(24 + gi), tmp[:, 5, :], ALU.mult))
                step(TTn(z2(24 + gi), z2(24 + gi), z2(21 + gi), ALU.mult))
                TTn(z2(30 + gi), z2(30 + gi), z2(24 + gi), ALU.mult).then_inc(src_ready, 1)
            for gi in range(3):
                lo_of("dil", gi, z2(30 + gi))
            for k in range(2):
                dve.wait_ge(mlp_hi, 2 * FF // P + k + 1)
                TTn(mlp_op[:, 1, k, :], arena[:, 24 + k, :], mlp_op[:, 0, k, :].bitcast(F32), ALU.subtract).then_inc(mlp_lo, 1)
            residual("out2")
            for m in range(KT):
                lo_of("ple", m, x[:, m, :])
            for m in range(KT):
                src = taken("ple", 2 * m)
                nc.vector.tensor_copy(tmp[:, m % 2, :], src[:, :]).then_inc(z_ready, 1)
                src = taken("ple", 2 * m + 1)
                dve.wait_ge(ple_sig, m + 1)
                step(TTn(tmp[:, 2, :], src[:, :], tmp[:, m % 2, :], ALU.mult))
                TTn(x[:, m, :], x[:, m, :], tmp[:, 2, :], ALU.add).then_inc(z_ready, 1)
            spread("out")
            for m in range(KT):
                STT(arena[:, m, :], x[:, m, :], g("g_out", m), rms[:, 0, :], ALU.mult, ALU.mult).then_inc(y_ready, 1)


def sub_blocks(w, cols=None):
    k, _ = w.shape
    if cols is not None:
        wide = np.zeros((k, len(cols)), w.dtype)
        there = np.asarray(cols) >= 0
        wide[:, there] = w[:, np.asarray(cols)[there]]
        w = wide
    m = w.shape[1]
    if m % P:
        w = np.concatenate([w, np.zeros((k, P - m % P), w.dtype)], axis=1)
    return w.reshape(k // P, P, -1, P).transpose(2, 0, 1, 3)


def pair_diagonal(w):
    n, a, b = w.shape
    out = np.zeros((n, 2 * a, 2 * b), w.dtype)
    out[:, :a, :b] = w
    out[:, a:, b:] = w
    return out


def padded(blocks):
    blocks = blocks.reshape(-1, P, P)
    short = -len(blocks) % SUBS
    return np.concatenate([blocks, np.zeros((short, P, P), blocks.dtype)]) if short else blocks


def heads(n_pairs, stride, offset=0, dh=64):
    return [offset + dh * (j + stride * s) + i for j in range(n_pairs) for s in range(2) for i in range(dh)]


def weight_stream(a):
    span = lambda lo, n: list(range(lo, lo + n))
    out = []
    ein = heads(4, 4) + span(512, 768)
    out.append(padded(sub_blocks(a["e_w_in"][0], ein)))
    out.append(padded(a["e_w_pool"][0]))
    rows = heads(4, 4) + span(512, 512)
    out.append(padded(sub_blocks(a["e_w_out"][0][rows])))

    def mlp(layer):
        out.append(padded(sub_blocks(a["w_mlp1"][layer])))
        out.append(padded(sub_blocks(a["w_mlp2"][layer]).transpose(1, 0, 2, 3)))

    mlp(0)
    oin = span(0, 384) + [-1] * 64 + span(384, 32) + [-1] * 32 + span(416, 1024)
    out.append(padded(sub_blocks(a["o_w_in"][0], oin)))
    gates = np.stack([a["o_lru_wa"][0], a["o_lru_wx"][0]], axis=1)
    lru = np.zeros((2, 2, 4, P, P), gates.dtype)
    lru[:, :, :, :64, :64] = gates[:, :, 0::2]
    lru[:, :, :, 64:, 64:] = gates[:, :, 1::2]
    out.append(padded(lru))
    uq = [96 * h + i if i < 96 else -1 for h in range(MLA_HEADS) for i in range(P)]
    out.append(padded(sub_blocks(a["o_w_uq"][0], uq)))
    ukn = [P * h + i if i < 64 else -1 for h in range(MLA_HEADS) for i in range(P)]
    out.append(padded(sub_blocks(a["o_w_ukv"][0], ukn)))
    uv = [P * h + 64 + i for h in range(MLA_HEADS) for i in range(64)]
    out.append(padded(sub_blocks(a["o_w_ukv"][0], uv)))
    out.append(padded(sub_blocks(a["o_w_out"][0])))
    mlp(1)
    q0 = 1024
    g0 = q0 + 384 + 6 * 128
    zin = (span(0, 1024) + heads(3, 3, q0) + span(q0 + 384, 768) + span(g0, 18) + [-1] * 110
           + heads(3, 3, g0 + 18) + span(g0 + 18 + 384, 4 * 384))
    tiles = sub_blocks(a["w_in_2"][0], zin)[ZIN]
    out.append(padded(tiles[:6]))
    compression = np.concatenate([pair_diagonal(a["cmp_w1_2"][0, kv].reshape(CMP_BLOCK, HD, HD)) for kv in range(2)])
    for i in range(8):
        out += [padded(tiles[6 + i]), padded(compression[SUBS * i:SUBS * (i + 1)])]
    out.append(padded(tiles[14:]))
    rows = span(0, 256) + heads(3, 3, 256) + span(640, 384)
    out.append(padded(sub_blocks(a["w_out_2"][0][rows])))
    gate, proj = sub_blocks(a["w_ple_gate_2"][0]), sub_blocks(a["w_ple_proj_2"][0])
    out.append(padded(np.concatenate([gate, proj], axis=1)))
    stream = np.concatenate(out)
    assert len(stream) == NBLOCKS * SUBS
    return np.ascontiguousarray(stream.reshape(NBLOCKS, SUBS, P, P).transpose(0, 2, 1, 3)).reshape(NBLOCKS, P, D)


def small_params(a):
    tiles = lambda v: v.reshape(-1, P).T
    pe = a["cmp_pe_2"][0].transpose(2, 0, 1).reshape(HD, 2 * CMP_BLOCK)
    w2 = pair_diagonal(a["cmp_w2_2"][0])
    bias = np.stack([a["o_lru_ba"][0], a["o_lru_bx"][0]], axis=1)
    parts = dict(g_even=tiles(a["e_norm_mix"][0]), g_mlp0=tiles(a["norm_mlp"][0]), g_odd=tiles(a["o_norm_mix"][0]),
                 g_mlp1=tiles(a["norm_mlp"][1]), g_final=tiles(a["final_norm"]), g_mix2=tiles(a["norm_mix_2"][0]),
                 g_out=tiles(a["norm_final_2"]), g_cq=tiles(a["o_g_cq"][0]), g_ckv=tiles(a["o_g_ckv"][0]),
                 pool_scale=tiles(a["e_pool_scale"][0]), conv_w=tiles(a["o_conv_w"][0]), conv_b=tiles(a["o_conv_b"][0]),
                 gate_b=tiles(bias), lam=tiles(a["o_lru_lambda"][0]), conv2_w=tiles(a["conv_w_2"][0]),
                 conv2_b=tiles(a["conv_b_2"][0]), pe=np.concatenate([pe, pe]),
                 sink=np.broadcast_to(a["e_sink"][0], (P, 8)), w2k=w2[0], w2v=w2[1])
    return np.ascontiguousarray(np.concatenate([parts[n].reshape(P, w) for n, w in PARAM_COLS], axis=1))


def small_consts():
    p = np.arange(P)[:, None]
    mask = lambda ok: np.where(ok, 0.0, NEG)
    c = np.arange(640)[None]
    band = np.arange(384)[None]
    near = np.arange(256)[None]
    b = np.arange(P)[None]
    tok = (np.arange(TT) * P)[None, :, None] + p[:, :, None]
    n = np.arange(32)[None, None, :]
    rot = np.zeros((2, P, P))
    for first, half, which in ((0, 32, 0), (64, 32, 0), (64, 16, 1)):
        for i in range(half):
            rot[which, first + half + i, first + i] = -1.0
            rot[which, first + i, first + half + i] = 1.0
    parts = dict(causal=mask(c - 512 <= p), band=mask(np.abs(band - P - p) <= 128),
                 near=mask((p + P - near >= 0) & (p + P - near <= 128)),
                 blocks=mask((p // 32 == b // 32) & (b <= p)),
                 cmpmask=mask(CMP_STRIDE * n + CMP_BLOCK - 1 <= tok).reshape(P, TT * 32),
                 ident=np.eye(P), rot_even=rot[0], rot_mla=rot[1], late=(p >= CMP_BLOCK - 1) * 1.0,
                 ones=np.ones((P, 1)), eps=np.full((P, 1), EPS))
    return np.concatenate([parts[k].reshape(P, w) for k, w in CONST_COLS], axis=1).astype(np.float32)


def rope_tables():
    out = np.zeros((2, P, 2, SEQ), np.float32)
    out[1, :64, 0] = 1.0
    for layer, first, half, n in ((0, 0, 32, 4), (1, 64, 16, 2)):
        inv = np.float32(10000.0) ** (-np.arange(half, dtype=np.float32) / np.float32(half))
        ang = np.arange(SEQ, dtype=np.float32)[None] * inv[:, None]
        for j in range(n):
            out[layer, first + half * j:first + half * (j + 1), 0] = np.cos(ang)
            out[layer, first + half * j:first + half * (j + 1), 1] = np.sin(ang)
    return out


def window_counts():
    t = np.arange(SEQ)
    rows = [1.0 / (np.clip(t + w // 2, 0, SEQ) - np.clip(t - w // 2, 0, SEQ)) for w in (2, 4, 8, 16)]
    return np.ascontiguousarray(np.broadcast_to(np.stack(rows)[None], (P, 4, SEQ))).astype(np.float32)


def kernel(**inputs):
    import concourse.bacc as bacc
    from concourse.bass_utils import run_bass_kernel_spmd

    a = {k: np.asarray(v) for k, v in inputs.items()}
    arrays = dict(x_t=np.ascontiguousarray(a["x"][0].T), stream=weight_stream(a), params=small_params(a),
                  consts=small_consts(), ropes=rope_tables(), invcnt=window_counts(),
                  p_t=np.ascontiguousarray(a["p_2"][0, 0].T))
    nc = bacc.Bacc("TRN2", target_bir_lowering=False, num_devices=1)
    args = {n: nc.dram_tensor(n + "_dram", v.shape, mybir.dt.from_np(v.dtype), kind="ExternalInput").ap()
            for n, v in arrays.items()}
    out = nc.dram_tensor("out_t_dram", (D, SEQ), F32, kind="ExternalOutput").ap()
    program(nc, out_t=out, **args)
    r = run_bass_kernel_spmd(nc, [{n + "_dram": v for n, v in arrays.items()}], core_ids=[0])
    return np.ascontiguousarray(r.results[0]["out_t_dram"].T)[None]
```

```python
from contextlib import ExitStack

import concourse.bass as bass
import numpy as np
from concourse import mybir

F32 = mybir.dt.float32
F32R = mybir.dt.float32r
ALU = mybir.AluOpType
ACT = mybir.ActivationFunctionType
AX = mybir.AxisListType.X

P = 128
SEQ = 512
D = 1024
KT = D // P
TT = SEQ // P
FF = 4 * D
SUBS = 8
RING = 4
EPS = 1e-6
NEG = -1e30
EVEN_HEADS, EVEN_GROUP = 8, 4
LRU_C = 8.0
MLA_HEADS, NOPE, ROPE = 8, 64, 32
NSA_R, HD = 3, 64
CMP_BLOCK, CMP_STRIDE = 32, 16
N_CMP = (SEQ - CMP_BLOCK) // CMP_STRIDE + 1
DILATIONS = (1, 4, 16)

STAGES = [("ein", 10, 8), ("pool", 4, 1), ("eout", 8, 8), ("up0", 32, 8), ("down0", 8, 32),
          ("oin", 6, 8), ("lru_a", 8, 1), ("oin_b", 2, 8), ("lru_b", 8, 1), ("oin_c", 4, 8), ("uq", 8, 2), ("ukn", 8, 1), ("uv", 4, 1), ("oout", 8, 8),
          ("up1", 32, 8), ("down1", 8, 32), ("zin", 6, 8),
          *((f"{kind}{i}", n, 8) for i in range(8) for kind, n in (("zin_by", 1), ("cmp", 0))),
          ("zin_rest", 19, 8), ("out2", 8, 8), ("ple", 16, 5)]
EIN = [6, 7, 8, 9, 4, 5, 0, 1, 2, 3]
EVEN_ROTATED = [4, 0, 1, 2, 3]
OIN = [4, 5, 6, 7, 8, 9, 10, 11, 0, 1, 2, 3]
LRU_UNITS = [0, 4, 1, 5, 2, 6, 3, 7]
ZIN = [11, 12, 13, 14, 16, 17, 27, 28, 29, 15, 2, 4, 3, 5, 0, 1, 6, 7, 18, 19, 20, 30, 31, 32, 8, 9, 10,
       21, 22, 23, 24, 25, 26]
assert sorted(ZIN) == list(range(33))
TILE0, SUB0, NTILES = {}, {}, {}
_t = _s = 0
for _name, _n, _k in STAGES:
    TILE0[_name], SUB0[_name], NTILES[_name] = _t, _s, _n
    _t += _n
    _s += -(-max(_n, 1) * _k // SUBS) * SUBS
NBLOCKS = _s // SUBS
assert NBLOCKS % RING == 0



def block_ends():
    out, used = [], 0
    for name, tiles, k in STAGES:
        ends, s, t = {}, SUB0[name], TILE0[name]
        if name.startswith("down"):
            ends = {s + tiles * k - tiles + i: t + i + 1 for i in range(tiles)}
        else:
            for i in range(tiles):
                s += k if name != "ple" else (8, 2)[i % 2]
                ends[s - 1] = t + i + 1
        end = SUB0[name] + max(tiles, 1) * k
        for b in range(SUB0[name] // SUBS, -(-end // SUBS)):
            last = min(SUBS * (b + 1), end) - 1
            if last in ends:
                out.append(("tile", ends[last]))
            else:
                used += 1
                out.append(("block", used))
    return out


BLOCK_END = block_ends()
assert len(BLOCK_END) == NBLOCKS

SPLITS = [("even", 8), ("pool", 4), ("pooled", 4), ("eattn", 4), ("mlp0", 8), ("odd", 8), ("xc", 4),
          ("cq", 2), ("ckv", 1), ("lru", 4), ("mattn", 4), ("mlp1", 8), ("mix2", 8), ("cmp", 4),
          ("conv2", 2), ("nsa", 3), ("dil", 3), ("ple", 8)]
HEAD = 3
SPLIT0 = {}
_t = 0
for _name, _n in SPLITS:
    SPLIT0[_name] = _t
    _t += _n

NORMS = [("even", 8), ("mlp0", 8), ("odd", 8), ("cq", 2), ("ckv", 1), ("mlp1", 8), ("final", 16),
         ("mix2", 0), ("out", 8)]
NORM, SQ0, NORM_TILES = {}, {}, dict(NORMS)
_t = 0
for _i, (_name, _n) in enumerate(NORMS):
    NORM[_name], SQ0[_name] = _i, _t
    _t += _n

PARAM_COLS = [("g_even", 8), ("g_mlp0", 8), ("g_odd", 8), ("g_mlp1", 8), ("g_final", 8), ("g_mix2", 8),
              ("g_out", 8), ("g_cq", 2), ("g_ckv", 1), ("pool_scale", 4), ("conv_w", 16), ("conv_b", 4),
              ("gate_b", 16), ("lam", 8), ("conv2_w", 6), ("conv2_b", 2), ("pe", 64), ("sink", 8),
              ("w2k", 128), ("w2v", 128)]
CONST_COLS = [("causal", 640), ("band", 384), ("near", 256), ("blocks", 128), ("cmpmask", TT * 32),
              ("ident", 128), ("rot_even", 128), ("rot_mla", 128), ("late", 1), ("ones", 1), ("eps", 1)]


def columns(cols):
    at, out = 0, {}
    for name, n in cols:
        out[name] = (at, at + n)
        at += n
    return out, at


PCOL, NPARAM = columns(PARAM_COLS)
CCOL, NCONST = columns(CONST_COLS)


def even_units():
    return [dict(j=j, g=g, qt=qt, lo=max(0, qt - 1), hi=min(TT, qt + 2), group=j)
            for j in range(EVEN_GROUP) for g in range(2) for qt in range(TT)]


def mla_units():
    return [dict(h=h, qt=qt, group=h // 2) for h in range(MLA_HEADS) for qt in range(TT)]


def nsa_units():
    return [dict(r=r, g=g, qt=qt, branch=b, group=r)
            for r in range(NSA_R) for qt in range(TT) for g in range(2) for b in range(3)]


def dilated_units():
    return [dict(gi=gi, tile=t, g=g, group=NSA_R + gi) for gi in range(3) for t in range(TT) for g in range(2)]


EVEN, MLA, LAST = even_units(), mla_units(), nsa_units() + dilated_units()
UNIT0 = {"even": 0, "mla": len(EVEN), "last": len(EVEN) + len(MLA)}


def program(nc, x_t, stream, params, consts, ropes, invcnt, p_t, out_t):
    with ExitStack() as ctx:
        def sb(name, shape, dt=F32):
            return ctx.enter_context(nc.sbuf_tensor(name, shape, dt))

        def sem(name):
            return ctx.enter_context(nc.semaphore(name))

        arena = sb("arena", [P, 49, SEQ])
        base = nc.sbuf_base - 49 * SEQ * 4
        opA = nc.alloc_sbuf_tensor_at("opA", [P, 2, KT, SEQ], F32R, offset=base)
        op_any = nc.alloc_sbuf_tensor_at("op_any", [P, 49, SEQ], F32R, offset=base)
        opC = nc.alloc_sbuf_tensor_at("opC", [P, 2, KT, SEQ], F32R, offset=base + 33 * SEQ * 4)
        x = sb("x", [P, KT, SEQ])
        raw = sb("raw", [P, RING, D])
        w_hi = sb("w_hi", [P, RING, D], F32R)
        w_lo = sb("w_lo", [P, RING, D], F32R)
        mlp_op = sb("mlp_op", [P, 2, 2, SEQ], F32R)
        more = nc.alloc_sbuf_tensor_at("more", [P, 4, SEQ], F32, offset=nc.sbuf_base - 4 * SEQ * 4)
        tmp = sb("tmp", [P, 6, SEQ])
        rms = sb("rms", [P, 3, SEQ])
        rope = sb("rope", [P, 2, SEQ])
        con = sb("con", [P, NCONST])
        par = sb("par", [P, NPARAM])
        negm = sb("negm", [P, 96])
        den = sb("den", [P, 96])
        rden = sb("rden", [P, 96])
        gates = sb("gates", [P, TT * 32])
        small = sb("small", [P, 16, 8])
        std = sb("std", [P, len(NORMS), TT])
        rtok = sb("rtok", [P, len(NORMS), TT])
        unread = sb("unread", [P, len(NORMS)])
        hid = sb("hid", [P, 4, 32])
        cmpk = sb("cmpk", [P, 32])
        cmpv = sb("cmpv", [32, P])
        bank = [ctx.enter_context(nc.psum_tensor(f"bank{i}", [P, SEQ], F32)) for i in range(8)]

        raw_in = [sem(f"raw_in{i}") for i in range(RING)]
        hi_made, lo_made, block_used = sem("hi_made"), sem("lo_made"), sem("block_used")
        acc_full, z_ready = sem("acc_full"), sem("z_ready")
        split_hi, split_lo = sem("split_hi"), sem("split_lo")
        sq_ready, sq_used, sums_full = sem("sq_ready"), sem("sq_used"), sem("sums_full")
        std_ready, rtok_ready, rms_full, rms_ready = sem("std_ready"), sem("rtok_ready"), sem("rms_full"), sem("rms_ready")
        x_in = [sem(f"x_in{m}") for m in range(KT)]
        par_in, con_in, rope_in, inv_in, p_in = (sem(s) for s in ("par_in", "con_in", "rope_in", "inv_in", "p_in"))
        rot_full, roped = sem("rot_full"), sem("roped")
        ckv_scaled = sem("ckv_scaled")
        turned, v_tok = sem("turned"), sem("v_tok")
        s_full, masked, sink_put, exp_done = sem("s_full"), sem("masked"), sem("sink_put"), sem("exp_done")
        p_ready, pt_full, pt_ready, pv_done = sem("p_ready"), sem("pt_full"), sem("pt_ready"), sem("pv_done")
        o_out = sem("o_out")
        relu_made, mlp_hi, mlp_lo = sem("relu_made"), sem("mlp_hi"), sem("mlp_lo")
        src_ready = sem("src_ready")
        key_rope = sem("key_rope")
        decay_made, beta_sq, beta_made, gelu_made = (sem(s) for s in ("decay_made", "beta_sq", "beta_made", "gelu_made"))
        lam_act, sp_made = sem("lam_act"), sem("sp_made")
        silu_made, hid_in, hid_sig, hid_made, cmp_full, cmp_ready = (sem(s) for s in ("silu_made", "hid_in", "hid_sig", "hid_made", "cmp_full", "cmp_ready"))
        gates_turned, gates_ready = sem("gates_turned"), sem("gates_ready")
        log_den, lse_ready, lse_full, lse_exp = sem("log_den"), sem("lse_ready"), sem("lse_full"), sem("lse_exp")
        ls_max, ple_sig = sem("ls_max"), sem("ple_sig")
        vstep, y_ready, stored = sem("vstep"), sem("y_ready"), sem("stored")

        def c(name, lo=0, hi=None):
            a, b = CCOL[name]
            return con[:, a + lo:(b if hi is None else a + hi)]

        def g(name, i=0, n=1):
            return par[:, PCOL[name][0] + i:PCOL[name][0] + i + n]

        ident = c("ident")

        def square_sum(name, m=0):
            return rms[:, 1 if name == "cq" or name == "final" and m % 2 == 0 else 2, :]

        def z(i, layer):
            return arena[:, i + 16 * (layer % 2), :]

        def Z(layer):
            return lambda i: z(i, layer)

        z0, z1, z2 = Z(0), Z(1), Z(2)
        splits = {}

        def place(name, op, first, n):
            for i in range(n):
                splits[name, i] = (op[:, 0, first + i, :], op[:, 1, first + i, :])

        for name, op, first, n in (
                ("even", opC, 0, 8), ("pooled", opC, 4, 4), ("eattn", opC, 0, 4),
                ("mlp0", opA, 0, 8), ("odd", opA, 0, 8), ("ckv", opA, 6, 1), ("mlp1", opC, 0, 8), ("mix2", opC, 0, 8),
                ("conv2", opC, 0, 2), ("nsa", opC, 2, 3), ("dil", opC, 5, 3), ("ple", opA, 0, 8)):
            place(name, op, first, n)
        for i in range(4):
            splits["pool", i] = (op_any[:, 18 + i, :], op_any[:, 22 + i, :])
        for i in range(4):
            splits["xc", i] = splits["cq", i % 2] = (mlp_op[:, 0, i % 2, :], mlp_op[:, 1, i % 2, :])
            splits["lru", i] = (op_any[:, 16 + 4 + i, :], op_any[:, 16 + 8 + i, :])
            splits["mattn", i] = (op_any[:, (4, 5, 12, 13)[i], :], op_any[:, 16 + (0, 1, 14, 15)[i], :])
        mla_q = [arena[:, i, :] for i in (0, 1, 2, 3, 8, 9, 10, 11)]
        mla_k = [z1(i) for i in (12, 13, 16, 17, 20, 21, 24, 25)]
        mla_v = [z1(28), z1(29), arena[:, 7, :], arena[:, 15, :]]

        def decay_tmp(u):
            return z1(4 + u) if u < 4 else tmp[:, u - 4, :]

        def gate(kind, u):
            return 8 * (u // 4) + 4 * kind + u % 4

        def gate_tile(kind, u):
            return z1(12 + gate(kind, u))

        opE = nc.alloc_sbuf_tensor_at("opE", [P, 2, 4, SEQ], F32R, offset=base + 18 * SEQ * 4)
        place("cmp", opE, 0, 4)
        def down_bank(layer, m):
            return bank[4 + (TILE0[f"down{layer}"] + m) % 4 if m < 4 else m - 4]

        def dilate(ap, r):
            return ap.rearrange("p (a r) -> p r a", r=r)

        def residues(ap, r):
            return ap.rearrange("p (r a) -> p r a", r=r)

        def unit(u, family):
            if family == "even":
                lo, hi, b = u["lo"], u["hi"], slice(64 * u["g"], 64 * u["g"] + 64)
                off = P * (lo - u["qt"] + 1)
                return dict(q=z0(u["j"])[b, P * u["qt"]:P * (u["qt"] + 1)], k=z0(4)[b, P * lo:P * hi], n=P * (hi - lo),
                            mask=c("band", off, off + P * (hi - lo)), scale=HD ** -0.5, sink=4 * u["g"] + u["j"],
                            v=[z0(5)[:, P * t + 64 * u["g"]:P * t + 64 * u["g"] + 64] for t in range(lo, hi)],
                            out=(64 * u["g"], P * u["qt"]), gate=None)
            if family == "mla":
                h, qt = u["h"], u["qt"]
                at = 64 * (h % 2)
                return dict(q=mla_q[h][0:96, P * qt:P * (qt + 1)], k=mla_k[h][0:96, :], n=SEQ,
                            mask=c("causal", 0, SEQ), scale=(NOPE + ROPE) ** -0.5, sink=None,
                            v=[mla_v[h // 2][:, P * t + at:P * t + at + 64] for t in range(TT)],
                            out=(at, P * qt), gate=None)
            b = slice(64 * u["g"], 64 * u["g"] + 64)
            if "r" in u:
                qt, br = u["qt"], u["branch"]
                n = N_CMP if br == 0 else P * (qt + 1)
                col = 32 * qt + 9 * u["g"] + 3 * u["r"] + br
                return dict(q=z2(8 + u["r"])[b, P * qt:P * (qt + 1)], n=n,
                            k=cmpk[b, 0:N_CMP] if br == 0 else z2(11 + 2 * br)[b, 0:n],
                            mask=c("cmpmask", 32 * qt, 32 * qt + N_CMP) if br == 0 else c("causal", 640 - n, 640),
                            scale=HD ** -0.5, sink=None,
                            v=[cmpv[0:N_CMP, b]] if br == 0 else
                              [z2(12 + 2 * br)[:, P * t + b.start:P * t + b.stop] for t in range(qt + 1)],
                            out=(b.start, P * qt), gate=gates[:, col:col + 1], first=br == 0, last=br == 2)
            gi, t = u["gi"], u["tile"]
            lo = t - 1 if gi == 0 and t else t
            mask = [c("near", 0 if t else P, 2 * P), c("causal", 512, 640), c("blocks")][gi]
            return dict(q=z2(21 + gi)[b, P * t:P * (t + 1)], k=z2(24 + gi)[b, P * lo:P * (t + 1)], n=P * (t + 1 - lo),
                        mask=mask, scale=HD ** -0.5, sink=None,
                        v=[z2(27 + gi)[:, P * s + b.start:P * s + b.stop] for s in range(lo, t + 1)],
                        out=(b.start, P * t), gate=None)

        FAMILY = {"even": [unit(u, "even") | {"group": u["group"]} for u in EVEN],
                  "mla": [unit(u, "mla") | {"group": u["group"]} for u in MLA],
                  "last": [unit(u, "last") | {"group": u["group"]} for u in LAST]}
        GROUP0 = {"even": 0, "mla": 4, "last": 8}

        def last_of(family, group):
            return max(i for i, u in enumerate(FAMILY[family]) if u["group"] == group)

        NORM_LAG, TURN_LAG, VALUE_LAG = 2, 3, 4
        SCORE_BANKS = {"even": (2, 3, 6), "mla": (2, 3, 6), "last": (2, 3, 6, 7)}

        def probs(i, n):
            return more[:, i % 4 - 2, 0:n] if i % 4 >= 2 else tmp[:, 2 + i % 4, 0:n]

        def groups_after(family, step):
            n = max(u["group"] for u in FAMILY[family]) + 1
            return [k for k in range(n) if last_of(family, k) + VALUE_LAG + 1 == step]

        block = ctx.enter_context(nc.Block())

        @block.sync
        def _(sp):
            for what, n in (("x", 0), ("w", 0), ("x", 1), ("w", 1), ("w", 2), ("x", 2), ("x", 3), ("w", 3)):
                if what == "x":
                    sp.dma_start(x[:, n, :], x_t[P * n:P * (n + 1), :]).then_inc(x_in[n], 16)
                else:
                    sp.dma_start(raw[:, n, :], stream[n]).then_inc(raw_in[n], 16)
            with sp.Fori(1, NBLOCKS // RING) as i:
                for j in range(RING):
                    sp.wait_ge(lo_made, RING * i + (j + 1 - RING))
                    sp.dma_start(raw[:, j, :], stream[RING * i + j]).then_inc(raw_in[j], 16)
            for m in range(KT):
                sp.wait_ge(y_ready, m + 1)
                sp.dma_start(out_t[P * m:P * (m + 1), :], arena[:, m, :]).then_inc(stored, 16)
            sp.wait_ge(stored, 16 * KT)

        @block.gpsimd
        def _(pool):
            with pool.Fori(0, NBLOCKS // RING) as i:
                for j in range(RING):
                    pool.wait_ge(hi_made, RING * i + (j + 1))
                    pool.tensor_tensor(w_lo[:, j, :], raw[:, j, :], w_hi[:, j, :].bitcast(F32),
                                       ALU.subtract).then_inc(lo_made, 1)

        @block.tensor
        def _(pe):
            seen = {"split": 0}

            def need_split(name, i):
                n = SPLIT0[name] + i + 1
                if n > seen["split"]:
                    pe.wait_ge(split_lo, n)
                    seen["split"] = n

            def product(out, slot, k, hi, lo, first, last):
                wh, wl = w_hi[:, slot, P * k:P * (k + 1)], w_lo[:, slot, P * k:P * (k + 1)]
                pe.matmul(out, wh, hi, start=first, stop=False)
                pe.matmul(out, wh, lo, start=False, stop=False)
                return pe.matmul(out, wl, hi, start=False, stop=last)

            def head(stage, op, norm, after_down=False):
                t0, b0 = TILE0[stage], SUB0[stage] // SUBS
                for k in range(KT):
                    need_split(op, k)
                    for i in range(HEAD):
                        if k == 0:
                            if t0 + i >= 4:
                                pe.wait_ge(z_ready, t0 + i - (7 if after_down else 3))
                            pe.wait_ge(lo_made, b0 + i + 1)
                        mm = product(bank[4 + (t0 + i) % 4][:, :], (b0 + i) % RING, k, *splits[op, k], k == 0, k == KT - 1)
                        if k == KT - 1:
                            mm.then_inc(acc_full, 1)
                if after_down:
                    pe.wait_ge(z_ready, t0)
                if stage == "ein":
                    pe.wait_ge(con_in, 16)
                norm_sums(norm)

            def linear(name, operand, n=SEQ, subs=None, after=None, headed=0):
                t0, s, ntiles = TILE0[name], SUB0[name], NTILES[name]
                nsub = {a: k for a, _, k in STAGES}[name]
                count = subs or (lambda i: nsub)
                end = s + sum(count(i) for i in range(ntiles))
                s += SUBS * headed
                for i in range(headed, ntiles):
                    t = t0 + i
                    if t >= 4:
                        pe.wait_ge(z_ready, t - 3)
                    for k in range(count(i)):
                        if s % SUBS == 0:
                            pe.wait_ge(lo_made, s // SUBS + 1)
                        hi, lo = operand(i, k)
                        mm = product(bank[4 + t % 4][:, 0:n], s // SUBS % RING, s % SUBS, hi, lo, k == 0, k == count(i) - 1)
                        s += 1
                        if (s % SUBS == 0 or s == end) and k < count(i) - 1:
                            mm.then_inc(block_used, 1)
                    mm.then_inc(acc_full, 1)
                    if after:
                        after(i)

            def split_operand(name):
                def operand(i, k):
                    need_split(name, k)
                    return splits[name, k]
                return operand

            def norm_sums(name):
                pe.wait_ge(sq_used, SQ0[name] + NORM_TILES[name])
                kinds = 2 if name == "final" else 1
                for col in range(TT * kinds):
                    t = col % TT
                    mm = pe.matmul(bank[2 if name == "ckv" else 0][:, col:col + 1],
                                   square_sum(name, col // TT)[:, P * t:P * (t + 1)], c("ones"),
                                   start=col == 0, stop=col == TT * kinds - 1, skip_group_check=True)
                mm.then_inc(sums_full, 1)

            def norm_spread(name):
                pe.wait_ge(rtok_ready, NORM[name] + 1)
                if name == "mix2":
                    pe.wait_ge(rms_ready, NORM[name])
                for t in range(TT):
                    mm = pe.matmul(bank[3 if name == "ckv" else 1][:, P * t:P * (t + 1)], rtok[:, NORM[name], t:t + 1].broadcast_to([P, P]), ident,
                                   start=True, stop=True)
                mm.then_inc(rms_full, 1)

            turn_count = [0]

            def rotate(n, tile, ready, rot, m, b):
                pe.wait_ge(z_ready, ready)
                if b == 7:
                    pe.wait_ge(roped, n)
                elif n >= 2:
                    pe.wait_ge(roped, n - 1)
                pe.matmul(bank[b][0:m, :], rot[0:m, 0:m], tile[0:m, :], start=True, stop=True).then_inc(rot_full, 1)

            def turn_values(tiles):
                for tile, ready in tiles:
                    pe.wait_ge(z_ready, ready)
                    if turn_count[0] >= 2:
                        pe.wait_ge(v_tok, turn_count[0] - 1)
                    for t in range(TT):
                        mm = pe.transpose(bank[turn_count[0] % 2][:, P * t:P * (t + 1)], tile[:, P * t:P * (t + 1)], ident)
                    mm.then_inc(turned, 1)
                    turn_count[0] += 1

            def attention(family, beside=lambda step: None):
                units, u0 = FAMILY[family], UNIT0[family]
                n = len(units)
                score_banks = SCORE_BANKS[family]
                more_ahead = len(score_banks) - 1
                for step in range(n + VALUE_LAG + more_ahead):
                    beside(step)
                    if step < n:
                        u, gu = units[step], u0 + step
                        if step >= len(score_banks):
                            pe.wait_ge(masked, gu + 1 - len(score_banks))
                        pe.matmul(bank[score_banks[step % len(score_banks)]][:, 0:u["n"]], u["q"], u["k"], start=True, stop=True).then_inc(s_full, 1)
                    i = step - TURN_LAG - more_ahead
                    if 0 <= i < n:
                        u, gu = units[i], u0 + i
                        pe.wait_ge(p_ready, gu + 1)
                        if i >= 2:
                            pe.wait_ge(pt_ready, gu - 1)
                        for a in range(0, u["n"], P):
                            w = min(P, u["n"] - a)
                            mm = pe.transpose(bank[4 + i % 2][0:w, a:a + P], probs(i, SEQ)[:, a:a + w], ident)
                        mm.then_inc(pt_full, 1)
                    i = step - VALUE_LAG - more_ahead
                    if i >= 0:
                        u, gu = units[i], u0 + i
                        pe.wait_ge(pt_ready, gu + 1)
                        grp = GROUP0[family] + u["group"]
                        if u["group"] >= 2 and units[i - 1]["group"] != u["group"]:
                            if family == "last":
                                pe.wait_ge(o_out, u["group"] - 1)
                            else:
                                pe.wait_ge(split_lo, SPLIT0["eattn" if family == "even" else "mattn"] + u["group"] - 1)
                        at, col = u["out"]
                        for b, v in enumerate(u["v"]):
                            kw = v.shape[0]
                            mm = pe.matmul(bank[grp % 2][at:at + 64, col:col + P], v,
                                           tmp[0:kw, 4 + i % 2, P * b:P * (b + 1)],
                                           start=(b == 0 and u.get("first", True)),
                                           stop=(b == len(u["v"]) - 1 and u.get("last", True)))
                        mm.then_inc(pv_done, 1)

            def mlp(layer):
                op, arena0 = f"mlp{layer}", 16 * ((layer + 1) % 2)
                t0, b0 = TILE0[f"up{layer}"], SUB0[f"up{layer}"] // SUBS

                def up(i, j):
                    t = RING * i + (t0 + j)
                    pe.wait_ge(z_ready, t - 3)
                    pe.wait_ge(lo_made, RING * i + (b0 + j + 1))
                    for k in range(KT):
                        mm = product(bank[4 + (t0 + j) % 4][:, :], (b0 + j) % RING, k, *splits[op, k], k == 0, k == KT - 1)
                    mm.then_inc(acc_full, 1)

                head(f"up{layer}", op, op)
                norm_spread(op)
                for j in range(HEAD, RING):
                    up(0, j)
                with pe.Fori(1, FF // P // RING) as i:
                    for j in range(RING):
                        up(i, j)

                b1 = b0 + FF // P
                t1 = t0 + FF // P

                def down(i, j, first, last):
                    pe.wait_ge(lo_made, RING * i + (b1 + j + 1))
                    pe.wait_ge(mlp_lo, RING * i + (layer * FF // P + j + 1))
                    for m in (4, 5, 6, 7, 0, 1, 2, 3) if first else range(KT):
                        if first and m == 0:
                            pe.wait_ge(z_ready, t1)
                        mm = product(down_bank(layer, m)[:, :], (b1 + j) % RING, m, mlp_op[:, 0, j % 2, :], mlp_op[:, 1, j % 2, :], first, last)
                        if last:
                            mm.then_inc(acc_full, 1)
                    if not last:
                        mm.then_inc(block_used, 1)

                for j in range(RING):
                    down(0, j, j == 0, False)
                with pe.Fori(1, FF // P // RING - 1) as i:
                    for j in range(RING):
                        down(i, j, False, False)
                for j in range(RING):
                    down(FF // P // RING - 1, j, False, j == RING - 1)

            head("ein", "even", "even")
            norm_spread("even")
            def rotate_even(n):
                i = EVEN_ROTATED[n]
                rotate(n, z0(i), TILE0["ein"] + EIN.index(i) + 1, c("rot_even"), P, 2 + n % 2 if n < 3 else 7)

            def after_ein(n):
                if n == 5:
                    rotate_even(0)
                if n == 6:
                    turn_values([(z0(5), TILE0["ein"] + EIN.index(5) + 1)])
                if n in (7, 8):
                    rotate_even(n - 6)

            linear("ein", split_operand("even"), headed=HEAD, after=after_ein)
            linear("pool", lambda i, k: (need_split("pool", i), splits["pool", i])[1])

            def beside_even(step):
                if step in (1, 9):
                    rotate_even(3 + step // 8)
                if step % 8 == 0 and step < len(EVEN):
                    pe.wait_ge(roped, 2 + step // 8)

            pe.wait_ge(v_tok, 1)
            pe.wait_ge(z_ready, TILE0["eout"])
            attention("even", beside_even)
            linear("eout", lambda i, k: (need_split("pooled" if k >= 4 else "eattn", k % 4),
                                         splits["pooled" if k >= 4 else "eattn", k % 4])[1])
            mlp(0)

            head("oin", "odd", "odd", after_down=True)
            norm_spread("odd")
            linear("oin", split_operand("odd"), headed=HEAD)
            for part, at in (("a", 0), ("b", 2)):
                linear(f"lru_{part}", lambda i, k: (need_split("xc", at + i // 4), splits["xc", at + i // 4])[1])
                if part == "a":
                    linear("oin_b", split_operand("odd"))
            linear("oin_c", split_operand("odd"))
            norm_sums("cq")
            norm_sums("ckv")

            def spread_ranks(i):
                if i == 2:
                    norm_spread("cq")
                    norm_spread("ckv")
                    rotate(5, z1(3), TILE0["oin_c"] + 4, c("rot_mla"), 96, 2)

            linear("uq", split_operand("cq"), after=spread_ranks)
            for h in range(2):
                rotate(6 + h, mla_q[h], TILE0["uq"] + h + 1, c("rot_mla"), 96, 3 - h)
            linear("ukn", split_operand("ckv"))
            linear("uv", split_operand("ckv"))
            turn_values([(mla_v[i], TILE0["uv"] + i + 1) for i in range(4)])
            pe.wait_ge(v_tok, 5)
            pe.wait_ge(roped, 8)
            pe.wait_ge(z_ready, TILE0["oout"])

            def beside_mla(step):
                h = step // 4 + 2
                if step % 4 == 1 and h < MLA_HEADS:
                    rotate(6 + h, mla_q[h], TILE0["uq"] + h + 1, c("rot_mla"), 96, 7)
                if step % 4 == 0 and step // 4 < MLA_HEADS:
                    pe.wait_ge(roped, 7 + step // 4)
                    pe.wait_ge(key_rope, step // 4 + 1)

            attention("mla", beside_mla)
            linear("oout", lambda i, k: (need_split("lru" if k >= 4 else "mattn", k % 4),
                                         splits["lru" if k >= 4 else "mattn", k % 4])[1])
            mlp(1)

            head("zin", "mix2", "final", after_down=True)
            norm_spread("final")
            norm_spread("mix2")
            def at_zin(n):
                if n == 8:
                    pe.wait_ge(silu_made, 1)
                    for t in range(TT):
                        mm = pe.transpose(bank[0][:, 32 * t:32 * (t + 1)], z2(17)[0:32, P * t:P * (t + 1)],
                                          ident[0:32, 0:32])
                    mm.then_inc(gates_turned, 1)
                if 11 <= n < 16:
                    pe.wait_ge(gates_ready, 1)
                    i = (14, 16, 27, 28, 29)[n - 11]
                    turn_values([(z2(i), TILE0["zin"] + ZIN.index(i) + 1)])
                if n == 20:
                    pe.wait_ge(hid_made, 1)
                    pe.matmul(bank[2][:, 0:32], g("w2k", 0, P), hid[:, 0, :], start=True, stop=True).then_inc(cmp_full, 1)
                    pe.wait_ge(hid_made, 2)
                    pe.matmul(bank[3][0:32, 0:P], hid[:, 1, :], g("w2v", 0, P), start=True, stop=True).then_inc(cmp_full, 1)

            def compress(i):
                b, kv = SUB0[f"cmp{i}"] // SUBS, i // 4
                pe.wait_ge(lo_made, b + 1)
                for k in range(SUBS):
                    pos = SUBS * (i % 4) + k
                    half, at = divmod(pos, CMP_STRIDE)
                    need_split("cmp", 2 * kv + half)
                    last = pos == CMP_BLOCK - 1
                    both = opE[:, :, 2 * kv + half, at:at + 31 * CMP_STRIDE + 1:CMP_STRIDE]
                    pe.matmul(bank[2 + kv][:, 0:64].rearrange("p (a b) -> p a b", a=2), w_hi[:, b % RING, P * k:P * (k + 1)],
                              both, start=pos == 0, stop=last, skip_group_check=True)
                    mm = pe.matmul(bank[2 + kv][:, 0:32], w_lo[:, b % RING, P * k:P * (k + 1)], both[:, 0, :],
                                   start=False, stop=last, skip_group_check=True)
                mm.then_inc(block_used, 1)

            linear("zin", split_operand("mix2"), headed=HEAD)
            for i in range(8):
                linear(f"zin_by{i}", split_operand("mix2"), after=lambda _, i=i: at_zin(6 + i))
                compress(i)
            linear("zin_rest", split_operand("mix2"), after=lambda i: at_zin(14 + i))
            pe.wait_ge(cmp_ready, 2)
            pe.wait_ge(v_tok, 10)
            pe.wait_ge(z_ready, TILE0["out2"])
            attention("last")

            def out2_operand(i, k):
                name, j = ("conv2", k) if k < 2 else ("nsa", k - 2) if k < 5 else ("dil", k - 5)
                need_split(name, j)
                return splits[name, j]

            def out2_head(i, ks):
                t, b = TILE0["out2"] + i, SUB0["out2"] // SUBS + i
                if ks[0] == 0:
                    pe.wait_ge(lo_made, b + 1)
                for k in ks:
                    mm = product(bank[4 + t % 4][:, :], b % RING, k, *out2_operand(i, k), k == 0, k == KT - 1)
                if ks[-1] == KT - 1:
                    mm.then_inc(acc_full, 1)

            out2_head(0, range(3))
            pe.wait_ge(lse_ready, 1)
            for gi in range(3):
                for t in range(TT):
                    r = DILATIONS[gi]
                    per = r // TT if r > TT else 1
                    out = (bank[gi][:, P * t:P * (t + 1)] if r == 1 else
                           dilate(bank[gi][:, :], r)[:, per * t:per * (t + 1), :])
                    mm = pe.matmul(out, tmp[:, gi, P * t:P * (t + 1)],
                                   ident if r == 1 else ident.rearrange("p (r a) -> p r a", r=per), start=True, stop=True)
                mm.then_inc(lse_full, 1)
            out2_head(0, range(3, 5))
            for i in range(1, HEAD):
                out2_head(i, range(5))
            for i in range(HEAD):
                out2_head(i, range(5, KT))
            linear("out2", out2_operand, headed=HEAD)

            def ple_operand(i, k):
                if i % 2 == 0:
                    need_split("ple", k)
                    return splits["ple", k]
                pe.wait_ge(mlp_lo, 2 * FF // P + 2) if i == 1 and k == 0 else None
                return mlp_op[:, 0, k, :], mlp_op[:, 1, k, :]

            linear("ple", ple_operand, subs=lambda i: 2 if i % 2 else 8)
            norm_sums("out")
            norm_spread("out")

        @block.scalar
        def _(act):
            prepared = [0]

            def prepare(n):
                while prepared[0] <= min(n, NBLOCKS - 1):
                    b = prepared[0]
                    act.wait_ge(raw_in[b % RING], 16 * (b // RING + 1))
                    if b >= RING:
                        what, count = BLOCK_END[b - RING]
                        act.wait_ge(acc_full if what == "tile" else block_used, count)
                    nc.scalar.activation(w_hi[:, b % RING, :], raw[:, b % RING, :], ACT.Copy).then_inc(hi_made, 1)
                    prepared[0] += 1

            def prepare_stage(name):
                i = [s[0] for s in STAGES].index(name)
                end = SUB0[STAGES[i + 1][0]] if i + 1 < len(STAGES) else NBLOCKS * SUBS
                prepare(end // SUBS - 1 + RING - 1)

            def hi_of(name, i, src, scale=1.0):
                nc.scalar.activation(splits[name, i][0], src, ACT.Copy, scale=scale).then_inc(split_hi, 1)

            def square(name, m, src, scale=1.0):
                q = SQ0[name] + m
                if q >= 2:
                    act.wait_ge(sq_used, q - 1)
                nc.scalar.activation(tmp[:, 4 + q % 2, :], src, ACT.Square, scale=scale).then_inc(sq_ready, 1)

            def root(name, n):
                nc.scalar.activation(unread[:, NORM[name]:NORM[name] + 1], c("ones"), ACT.Sqrt)
                order = [n for n, _ in NORMS if n != "mix2"]
                act.wait_ge(sums_full, order.index(name) + 1)
                nc.scalar.activation(std[:, NORM[name], :], bank[2 if name == "ckv" else 0][:, 0:TT], ACT.Sqrt, bias=c("eps"),
                                     scale=1.0 / n).then_inc(std_ready, 1)

            def norm(name, gain, ready, next_stage, stage=None):
                for m in range(KT):
                    if stage:
                        prepare(SUB0[stage] // SUBS + m + RING - 1)
                    ready(m)
                    hi_of(name, m, x[:, m, :], g(gain, m))
                    square(name, m, x[:, m, :])
                prepare(SUB0[next_stage] // SUBS + HEAD)
                if name == "even":
                    act.wait_ge(con_in, 16)
                root(name, D)

            def rows(stage):
                return lambda m: act.wait_ge(z_ready, TILE0[stage] + m + 1)

            def attention(family, evacuate, beside=lambda step: None):
                units, u0 = FAMILY[family], UNIT0[family]
                n = len(units)
                for step in range(n + VALUE_LAG + 1):
                    beside(step)
                    if step < n:
                        u, gu = units[step], u0 + step
                        act.wait_ge(masked, gu + 1)
                        if u["sink"] is not None:
                            act.wait_ge(sink_put, gu + 1)
                        if step >= 4:
                            act.wait_ge(pt_full, gu - 3)
                        w = u["n"] + (u["sink"] is not None)
                        nc.scalar.activation(probs(step, w), tmp[:, step % 2, 0:w], ACT.Exp,
                                             bias=negm[:, step:step + 1], scale=-1.0,
                                             accum_out=den[:, step:step + 1]).then_inc(exp_done, 1)
                    i = step - TURN_LAG
                    if 0 <= i < n:
                        u, gu = units[i], u0 + i
                        act.wait_ge(pt_full, gu + 1)
                        if i >= 2:
                            act.wait_ge(pv_done, gu - 1)
                        w, m = (u["n"] + P - 1) // P * P, min(P, u["n"])
                        nc.scalar.activation(tmp[0:m, 4 + i % 2, 0:w], bank[4 + i % 2][0:m, 0:w],
                                             ACT.Copy).then_inc(pt_ready, 1)
                    for k in groups_after(family, step):
                        evacuate(k)

            def group_done(family, k):
                act.wait_ge(pv_done, UNIT0[family] + last_of(family, k) + 1)

            def mlp(layer):
                t0, b0 = TILE0[f"up{layer}"], SUB0[f"up{layer}"] // SUBS
                arena0 = 16 * ((layer + 1) % 2)
                used0 = BLOCK_END[b0 + FF // P][1] - 1
                def ahead(i, j, base, first=False):
                    b = base + j + RING - 1
                    act.wait_ge(raw_in[b % RING], 16 * i + 16 * (b // RING + 1))
                    if base == b0 or first:
                        act.wait_ge(acc_full, RING * i + (TILE0[f"up{layer}"] + base - b0 + j))
                    else:
                        act.wait_ge(block_used, RING * i + (used0 + j))
                    nc.scalar.activation(w_hi[:, b % RING, :], raw[:, b % RING, :], ACT.Copy).then_inc(hi_made, 1)

                def up(i, j, prepared_ahead=False):
                    if not prepared_ahead:
                        ahead(i, j, b0)
                    t = RING * i + (t0 + j)
                    act.wait_ge(acc_full, t + 1)
                    act.wait_ge(z_ready, t - 1)
                    nc.scalar.activation(tmp[:, j % 2, :], bank[4 + (t0 + j) % 4][:, :], ACT.Relu).then_inc(relu_made, 1)

                for j in range(RING):
                    up(0, j, j == 0)
                with act.Fori(1, FF // P // RING - 1) as i:
                    for j in range(RING):
                        up(i, j)

                b1, t1, k0 = b0 + FF // P, t0 + FF // P, layer * FF // P
                src = arena[:, arena0:arena0 + FF // P, :].rearrange("p a b -> p (a b)")
                for k in range(2):
                    act.wait_ge(z_ready, t0 + k + 1)
                    nc.scalar.activation(mlp_op[:, 0, k, :], src[:, SEQ * k:SEQ * (k + 1)], ACT.Copy).then_inc(mlp_hi, 1)
                for j in range(RING):
                    up(FF // P // RING - 1, j)

                def down(i, j):
                    ahead(i, j, b1)
                    act.wait_ge(z_ready, t1)
                    nc.scalar.activation(mlp_op[:, 0, (j + 1) % 2, :], src[:, bass.ds(SEQ * RING * i + SEQ * (j + 1), SEQ)],
                                         ACT.Copy).then_inc(mlp_hi, 1)

                for j in range(RING):
                    if j == 0:
                        ahead(0, 0, b1, True)
                    else:
                        down(0, j)
                with act.Fori(1, FF // P // RING - 1) as i:
                    for j in range(RING):
                        down(i, j)
                for j in range(RING):
                    if j < RING - 1:
                        down(FF // P // RING - 1, j)
                    else:
                        ahead(FF // P // RING - 1, j, b1)
                prepared[0] = b1 + FF // P + RING - 1

            act.dma_start(par[:, :], params).then_inc(par_in, 16)
            act.wait_ge(par_in, 16)

            def arrived(m):
                if m < RING - 1:
                    prepare(m)
                act.wait_ge(x_in[m], 16)
                if m == 0:
                    for i in range(4, KT):
                        act.dma_start(x[:, i, :], x_t[P * i:P * (i + 1), :]).then_inc(x_in[i], 16)
                if m == 3:
                    act.dma_start(con[:, :], consts).then_inc(con_in, 16)
                    act.dma_start(rope[:, :, :], ropes[0]).then_inc(rope_in, 16)
                    act.dma_start(arena[:, 29:33, :], invcnt).then_inc(inv_in, 16)

            norm("even", "g_even", arrived, "ein")
            nc.scalar.activation(small[:, 0, :], g("lam", 0, 8), ACT.Abs).then_inc(lam_act, 1)
            act.wait_ge(lam_act, 1)
            nc.scalar.activation(small[:, 1, :], small[:, 0, :], ACT.Exp, scale=-1.0).then_inc(lam_act, 1)
            for i in range(4):
                prepare(HEAD + RING - 1 + max(i - 1, 0))
                act.wait_ge(src_ready, i + 1)
                hi_of("pool", i, z0(14 + i))
            prepare_stage("ein")
            prepare_stage("pool")
            for i in range(4):
                act.wait_ge(z_ready, TILE0["pool"] + i + 1)
                hi_of("pooled", i, z0(10 + i))

            def even_out(k):
                if k == 0:
                    act.wait_ge(acc_full, TILE0["pool"] + 4)
                group_done("even", k)
                hi_of("eattn", k, bank[(GROUP0["even"] + k) % 2][:, :])

            attention("even", even_out)
            act.dma_start(rope[:, :, :], ropes[1]).then_inc(rope_in, 16)
            norm("mlp0", "g_mlp0", rows("eout"), "up0", "eout")
            mlp(0)

            norm("odd", "g_odd", rows("down0"), "oin")
            b = SUB0["oin"] // SUBS
            half = len(LRU_UNITS) // 2

            def xc_hi(part):
                for i in (2 * part, 2 * part + 1):
                    act.wait_ge(src_ready, 4 + i + 1)
                    if part:
                        act.wait_ge(acc_full, TILE0["oin_b"])
                    hi_of("xc", i, z1(28 + i))

            def gates_of(part):
                t0 = TILE0["lru_b" if part else "lru_a"]
                act.wait_ge(z_ready, t0)
                for i in range(2 * half):
                    act.wait_ge(acc_full, t0 + i + 1)
                    u, kind = LRU_UNITS[half * part + i // 2], i % 2
                    nc.scalar.activation(gate_tile(kind, u), bank[4 + (t0 + i) % 4][:, :], ACT.Sigmoid,
                                         bias=g("gate_b", gate(kind, u))).then_inc(z_ready, 1)

            def decays_of(part):
                for i in range(half):
                    u = LRU_UNITS[half * part + i]
                    act.wait_ge(z_ready, TILE0["lru_b" if part else "lru_a"] + 2 * half)
                    nc.scalar.activation(decay_tmp(u), gate_tile(0, u), ACT.Exp,
                                         scale=small[:, 14, u:u + 1]).then_inc(decay_made, 1)
                    nc.scalar.activation(gate_tile(0, u), gate_tile(0, u), ACT.Tanh,
                                         scale=small[:, 15, u:u + 1]).then_inc(decay_made, 1)
                    if i == 1:
                        prepare(b + (14 if part else 11))

            def betas_of(part):
                for i in range(half * part, half * (part + 1)):
                    act.wait_ge(beta_sq, i + 1)
                    u = LRU_UNITS[i]
                    nc.scalar.activation(gate_tile(0, u), gate_tile(0, u), ACT.Sqrt, scale=-1.0).then_inc(beta_made, 1)

            act.wait_ge(sp_made, 2)
            prepare(b + 6)
            xc_hi(0)
            prepare(b + 9)
            gates_of(0)
            prepare(b + 10)
            xc_hi(1)
            decays_of(0)
            prepare(b + 12)
            gates_of(1)
            prepare(b + 13)
            betas_of(0)
            decays_of(1)
            for m in range(2):
                act.wait_ge(z_ready, TILE0["oin_c"] + m + 1)
                square("cq", m, z1(m))
                hi_of("cq", m, z1(m), g("g_cq", m))
                prepare(b + 15 + m)
            act.wait_ge(z_ready, TILE0["oin_c"] + 3)
            square("ckv", 0, z1(2))
            root("cq", 2 * P)
            root("ckv", P)
            prepare(b + 17)
            betas_of(1)
            act.wait_ge(acc_full, TILE0["oin_c"] + 4)
            act.wait_ge(ckv_scaled, 1)
            hi_of("ckv", 0, z1(2))
            for j in range(4):
                nc.scalar.activation(z1(8 + j), z1(8 + j), ACT.Gelu_apprx_tanh).then_inc(gelu_made, 1)
            prepare_stage("uq")
            act.wait_ge(roped, 6)
            act.wait_ge(z_ready, TILE0["ukn"])
            for h in range(MLA_HEADS):
                t = TILE0["ukn"] + h
                act.wait_ge(acc_full, t + 1)
                nc.scalar.activation(mla_k[h][0:64, :], bank[4 + t % 4][0:64, :], ACT.Copy).then_inc(z_ready, 1)
                nc.scalar.activation(mla_k[h][64:96, :], z1(3)[64:96, :], ACT.Copy).then_inc(key_rope, 1)
                if h == 3:
                    prepare_stage("ukn")
            prepare_stage("uv")
            for i in range(4):
                act.wait_ge(acc_full, TILE0["uv"] + i + 1)
                nc.scalar.activation(mla_v[i], bank[4 + (TILE0["uv"] + i) % 4][:, :], ACT.Copy).then_inc(z_ready, 1)
            for i in range(4):
                act.wait_ge(turned, 2 + i)
                nc.scalar.activation(mla_v[i], bank[(1 + i) % 2][:, :], ACT.Copy).then_inc(v_tok, 1)

            def beside_mla(step):
                if 9 <= step < 13:
                    i = step - 9
                    act.wait_ge(src_ready, 8 + i + 1)
                    hi_of("lru", i, z1(8 + i))

            def mla_out(k):
                group_done("mla", k)
                hi_of("mattn", k, bank[(GROUP0["mla"] + k) % 2][:, :])

            attention("mla", mla_out, beside_mla)
            norm("mlp1", "g_mlp1", rows("oout"), "up1", "oout")
            mlp(1)

            act.wait_ge(src_ready, 13)
            for m in range(KT):
                act.wait_ge(z_ready, TILE0["down1"] + m + 1)
                hi_of("mix2", m, x[:, m, :], small[:, 12, m:m + 1])
                square("final", 2 * m, x[:, m, :])
                square("final", 2 * m + 1, x[:, m, :], g("g_final", m))
            prepare(SUB0["zin"] // SUBS + HEAD)
            root("final", D)
            act.wait_ge(src_ready, 14)
            nc.scalar.activation(std[:, NORM["mix2"], :], small[:, 11, 0:TT], ACT.Sqrt, bias=c("eps"),
                                 scale=1.0 / D).then_inc(std_ready, 1)
            block0 = SUB0["zin"] // SUBS
            for n in range(33):
                prepare(block0 + n + min(max(n - 6, 0), 8) + RING - 1)
                if n == 3:
                    for i in range(4):
                        act.wait_ge(src_ready, 14 + i + 1)
                        hi_of("cmp", i, tmp[:, i, :])
                if n == 7:
                    act.wait_ge(z_ready, TILE0["zin"] + ZIN.index(17) + 1)
                    nc.scalar.activation(z2(17)[0:32, :], z2(17)[0:32, :], ACT.Sigmoid).then_inc(silu_made, 1)
                if n == 17:
                    for i in range(2):
                        act.wait_ge(hid_in, i + 1)
                        nc.scalar.activation(hid[:, 2 + i, :], hid[:, i, :], ACT.Sigmoid).then_inc(hid_sig, 1)
                for i in {20: (6, 7), 26: (18, 19, 20, 30, 31, 32)}.get(n, ()):
                    act.wait_ge(z_ready, TILE0["zin"] + ZIN.index(i) + 1)
                    nc.scalar.activation(z2(i), z2(i), ACT.Silu).then_inc(silu_made, 1)
            for i in range(2):
                act.wait_ge(src_ready, 18 + i + 1)
                act.wait_ge(acc_full, TILE0["zin"] + 33)
                hi_of("conv2", i, z2(4 + i))

            def last_out(k):
                if k < NSA_R:
                    act.wait_ge(o_out, k + 1)
                    hi_of("nsa", k, z2(18 + k))

            attention("last", last_out)
            first = 3 * TT * 2 * NSA_R
            nc.scalar.activation(rden[:, 0:24], den[:, first:first + 24], ACT.Ln).then_inc(log_den, 1)
            for gi in range(3):
                act.wait_ge(ls_max, gi + 1)
                nc.scalar.activation(z2(24 + gi), z2(24 + gi), ACT.Exp).then_inc(lse_exp, 1)
            act.wait_ge(ls_max, 4)
            nc.scalar.activation(tmp[:, 5, :], tmp[:, 4, :], ACT.Ln).then_inc(lse_exp, 1)
            act.wait_ge(lse_exp, 4)
            nc.scalar.activation(tmp[:, 5, :], tmp[:, 5, :], ACT.Exp, scale=-1.0).then_inc(lse_exp, 1)
            for gi in range(3):
                act.wait_ge(src_ready, 20 + gi + 1)
                hi_of("dil", gi, z2(30 + gi))
            act.dma_start(arena[:, 24:26, :], p_t.rearrange("(m p) n -> p m n", p=P)).then_inc(p_in, 16)
            act.wait_ge(p_in, 16)
            for k in range(2):
                nc.scalar.activation(mlp_op[:, 0, k, :], arena[:, 24 + k, :], ACT.Copy).then_inc(mlp_hi, 1)
            for m in range(KT):
                prepare(SUB0["out2"] // SUBS + m + RING - 1)
                act.wait_ge(z_ready, TILE0["out2"] + m + 1)
                hi_of("ple", m, x[:, m, :])
            for m in range(KT):
                prepare((SUB0["ple"] + 10 * m + 9) // SUBS + RING - 1)
                act.wait_ge(z_ready, TILE0["ple"] + 2 * m + 1)
                nc.scalar.activation(tmp[:, m % 2, :], tmp[:, m % 2, :], ACT.Sigmoid).then_inc(ple_sig, 1)
                act.wait_ge(z_ready, TILE0["ple"] + 2 * m + 2)
                square("out", m, x[:, m, :])
            root("out", D)

        @block.vector
        def _(dve):
            steps = [0]

            def mark(ins):
                ins.then_inc(vstep, 1)
                steps[0] += 1
                return steps[0]

            def step(ins):
                dve.wait_ge(vstep, mark(ins))

            TTn, TS, STT = nc.vector.tensor_tensor, nc.vector.tensor_scalar, nc.vector.scalar_tensor_tensor

            def lo_of(name, i, src, scale=None):
                e = SPLIT0[name] + i
                dve.wait_ge(split_hi, e + 1)
                hi, lo = splits[name, i]
                if scale is None:
                    return TTn(lo, src, hi.bitcast(F32), ALU.subtract).then_inc(split_lo, 1)
                return STT(lo, src, scale, hi.bitcast(F32), ALU.mult, ALU.subtract).then_inc(split_lo, 1)

            def spread(name, slot=0, then=None, gain=None):
                k = NORM[name]
                dve.wait_ge(std_ready, k + 1)
                if gain is None:
                    nc.vector.reciprocal(rtok[:, k, :], std[:, k, :]).then_inc(rtok_ready, 1)
                else:
                    step(nc.vector.reciprocal(small[:, 9, 0:TT], std[:, k, :]))
                    TTn(rtok[:, k, :], small[:, 9, 0:TT], gain, ALU.mult).then_inc(rtok_ready, 1)
                if then:
                    dve.wait_ge(rtok_ready, k + 1)
                    then()
                dve.wait_ge(rms_full, k + 1)
                nc.vector.tensor_copy(rms[:, slot, :], bank[3 if name == "ckv" else 1][:, :]).then_inc(rms_ready, 1)
                dve.wait_ge(rms_ready, k + 1)

            def add_square(name, m):
                q = SQ0[name] + m
                dve.wait_ge(sq_ready, q + 1)
                total, new = square_sum(name, m), tmp[:, 4 + q % 2, :]
                if m < (2 if name == "final" else 1):
                    nc.vector.tensor_copy(total, new).then_inc(sq_used, 1)
                else:
                    dve.wait_ge(sq_used, q)
                    TTn(total, total, new, ALU.add).then_inc(sq_used, 1)

            def norm(name, gain, ready=None, taken_from=None):
                ahead = 2 if taken_from and taken_from.startswith("down") else 0
                for step_ in range(KT + ahead):
                    if taken_from and step_ < KT:
                        residual_tile(taken_from, step_)
                    m = step_ - ahead
                    if m < 0:
                        continue
                    if ready:
                        ready(m)
                    if name == "final":
                        lo_of("mix2", m, x[:, m, :], gain[:, m:m + 1])
                        add_square(name, 2 * m)
                        add_square(name, 2 * m + 1)
                    else:
                        lo_of(name, m, x[:, m, :], g(gain, m))
                        add_square(name, m)
                if name != "final":
                    spread(name)

            def taken(name, i):
                t = TILE0[name] + i
                dve.wait_ge(acc_full, t + 1)
                return bank[4 + t % 4]

            def scaled(name, i, out, slot=0, m=P):
                src = taken(name, i)
                TTn(out[0:m, :], src[0:m, :], rms[0:m, slot, :], ALU.mult).then_inc(z_ready, 1)

            def residual_tile(name, m):
                src = taken(name, m)
                if name.startswith("down"):
                    src = down_bank(int(name[-1]), m)
                TTn(x[:, m, :], src[:, :], x[:, m, :], ALU.add).then_inc(z_ready, 1)

            def rotate(n, tile, m, b, scratch):
                dve.wait_ge(rot_full, n + 1)
                if n:
                    dve.wait_ge(roped, n)
                one, two = (t[0:m, :] for t in scratch)
                mark(TTn(one, tile[0:m, :], rope[0:m, 0, :], ALU.mult))
                step(TTn(two, bank[b][0:m, :], rope[0:m, 1, :], ALU.mult))
                TTn(tile[0:m, :], one, two, ALU.add).then_inc(roped, 1)

            values = [0]

            def turn_values(tiles):
                for tile in tiles:
                    values[0] += 1
                    dve.wait_ge(turned, values[0])
                    nc.vector.tensor_copy(tile, bank[(values[0] - 1) % 2][:, :]).then_inc(v_tok, 1)

            def attention(family, evacuate, beside=lambda step: None):
                units, u0 = FAMILY[family], UNIT0[family]
                n = len(units)
                for s in range(n + VALUE_LAG + 1):
                    beside(s)
                    i = s - NORM_LAG
                    if 0 <= i < n:
                        dve.wait_ge(exp_done, u0 + i + 1)
                        inverted = mark(nc.vector.reciprocal(rden[:, i:i + 1], den[:, i:i + 1]))
                    if s < n:
                        u, gu = units[s], u0 + s
                        if s >= 2:
                            dve.wait_ge(exp_done, gu - 1)
                        if u["sink"] is not None:
                            col = small[:, 13, u["sink"]:u["sink"] + 1]
                            nc.vector.tensor_copy(tmp[:, s % 2, u["n"]:u["n"] + 1], col).then_inc(sink_put, 1)
                        dve.wait_ge(s_full, gu + 1)
                        nc.vector.tensor_tensor_reduce(
                            tmp[:, s % 2, 0:u["n"]], bank[SCORE_BANKS[family][s % len(SCORE_BANKS[family])]][:, 0:u["n"]], u["mask"], -u["scale"],
                            3e38 if u["sink"] is None else col, ALU.add, ALU.min, negm[:, s:s + 1]).then_inc(masked, 1)
                    if 0 <= i < n:
                        u = units[i]
                        dve.wait_ge(vstep, inverted)
                        pr = probs(i, u["n"])
                        if u["gate"] is None:
                            TS(pr, pr, rden[:, i:i + 1], None, ALU.mult).then_inc(p_ready, 1)
                        else:
                            TS(pr, pr, rden[:, i:i + 1], u["gate"], ALU.mult, ALU.mult).then_inc(p_ready, 1)
                    for k in groups_after(family, s):
                        evacuate(k)

            def group_bank(family, k):
                dve.wait_ge(pv_done, UNIT0[family] + last_of(family, k) + 1)
                return bank[(GROUP0[family] + k) % 2]

            def mlp(layer):
                t0 = TILE0[f"up{layer}"]
                arena0 = 16 * ((layer + 1) % 2)
                u = arena[:, arena0:arena0 + FF // P, :].rearrange("p a b -> p (a b)")
                step(TTn(rms[:, 1, :], rms[:, 0, :], rms[:, 0, :], ALU.mult))
                v0 = steps[0]

                def up(i, j):
                    dve.wait_ge(relu_made, RING * i + (layer * FF // P + j + 1))
                    TTn(tmp[:, j % 2, :], tmp[:, j % 2, :], rms[:, 1, :], ALU.mult).then_inc(vstep, 1)
                    dve.wait_ge(vstep, RING * i + (v0 + j + 1))
                    TTn(u[:, bass.ds(SEQ * RING * i + SEQ * j, SEQ)], bank[4 + (t0 + j) % 4][:, :], tmp[:, j % 2, :],
                        ALU.mult).then_inc(z_ready, 1)

                def low_part(i, j):
                    dve.wait_ge(mlp_hi, RING * i + (layer * FF // P + j + 1))
                    TTn(mlp_op[:, 1, j % 2, :], u[:, bass.ds(SEQ * RING * i + SEQ * j, SEQ)],
                        mlp_op[:, 0, j % 2, :].bitcast(F32), ALU.subtract).then_inc(mlp_lo, 1)

                with dve.Fori(0, FF // P // RING - 1) as i:
                    for j in range(RING):
                        up(i, j)
                for j in range(2):
                    low_part(0, j)
                for j in range(RING):
                    up(FF // P // RING - 1, j)
                steps[0] += FF // P
                for j in range(2, RING):
                    low_part(0, j)
                with dve.Fori(1, FF // P // RING) as i:
                    for j in range(RING):
                        low_part(i, j)

            def cut_conv(out, src, taps, w, bias, done=None):
                at = [i for i, s in enumerate(taps) if s == 0][0]
                step(TS(out, src, w(at), bias, ALU.mult, ALU.add))
                others = [i for i, s in enumerate(taps) if s]
                for i in others:
                    a, b = max(0, -taps[i]), SEQ - max(0, taps[i])
                    ins = STT(out[:, a:b], src[:, a + taps[i]:b + taps[i]], w(i), out[:, a:b], ALU.mult, ALU.add)
                    if done is not None and i == others[-1]:
                        ins.then_inc(done, 1)
                    else:
                        step(ins)

            def log_decay():
                dve.wait_ge(lam_act, 2)
                step(TS(small[:, 2, :], small[:, 1, :], 2.0, None, ALU.add))
                step(nc.vector.reciprocal(small[:, 3, :], small[:, 2, :]))
                step(TTn(small[:, 4, :], small[:, 3, :], small[:, 1, :], ALU.mult))
                step(TTn(small[:, 5, :], small[:, 4, :], small[:, 4, :], ALU.mult))
                terms = 10
                step(TS(small[:, 6, :], small[:, 5, :], 1.0 / (2 * terms + 1), 1.0 / (2 * terms - 1), ALU.mult, ALU.add))
                for k in range(terms - 2, -1, -1):
                    step(TTn(small[:, 6, :], small[:, 6, :], small[:, 5, :], ALU.mult))
                    step(TS(small[:, 6, :], small[:, 6, :], 1.0 / (2 * k + 1), None, ALU.add))
                step(TTn(small[:, 7, :], small[:, 6, :], small[:, 4, :], ALU.mult))
                step(TS(small[:, 8, :], g("lam", 0, 8), -1.0, 0.0, ALU.mult, ALU.max))
                step(STT(small[:, 9, :], small[:, 7, :], 2.0, small[:, 8, :], ALU.mult, ALU.add))
                TS(small[:, 14, :], small[:, 9, :], -LRU_C, None, ALU.mult).then_inc(sp_made, 1)
                TS(small[:, 15, :], small[:, 9, :], -LRU_C / 2, None, ALU.mult).then_inc(sp_made, 1)

            dve.wait_ge(par_in, 16)
            TS(small[:, 13, :], g("sink", 0, 8), -1.0, None, ALU.mult)

            norm("even", "g_even", lambda m: dve.wait_ge(x_in[m], 16))
            log_decay()
            wide = [tmp[:, 2 * i:2 * i + 2, :].rearrange("p a b -> p (a b)") for i in range(2)]

            def pool(grp):
                u = z0(6 + grp)
                dve.wait_ge(z_ready, TILE0["ein"] + EIN.index(6 + grp) + 1)
                if grp:
                    dve.wait_ge(src_ready, grp)
                step(nc.vector.memset(wide[0][:, 0:8], 0.0))
                step(nc.vector.memset(wide[0][:, SEQ + 8:SEQ + 16], 0.0))
                step(nc.vector.tensor_copy(wide[0][:, 8:SEQ + 8], u))
                step(TTn(wide[1][:, 1:SEQ + 16], wide[0][:, 0:SEQ + 15], wide[0][:, 1:SEQ + 16], ALU.add))
                a, lo, hi = 1, 1, SEQ + 16
                for k in range(grp):
                    h = 1 << k
                    lo, hi = lo + h, hi - h
                    step(TTn(wide[1 - a][:, lo:hi], wide[a][:, lo - h:hi - h], wide[a][:, lo + h:hi + h], ALU.add))
                    a = 1 - a
                total = wide[a][:, 8:SEQ + 8]
                step(TTn(total, total, arena[:, 29 + grp, :], ALU.mult))
                TTn(z0(14 + grp), total, u, ALU.subtract).then_inc(src_ready, 1)

            def rotate_even(n):
                rotate(n, z0(EVEN_ROTATED[n]), P, 2 + n % 2 if n < 3 else 7, (more[:, 2, :], more[:, 3, :]))

            dve.wait_ge(inv_in, 16)
            dve.wait_ge(rope_in, 16)
            for n, i in enumerate(EIN):
                scaled("ein", n, z0(i))
                if 1 <= n <= 4:
                    pool(n - 1)
                if n == 5:
                    for i in range(4):
                        lo_of("pool", i, z0(14 + i))
                if n == 6:
                    rotate_even(0)
                if n == 7:
                    turn_values([z0(5)])
                if n == 8:
                    rotate_even(1)
                    rotate_even(2)
            for i in range(4):
                src = taken("pool", i)
                TS(z0(10 + i), src[:, :], g("pool_scale", i), None, ALU.mult).then_inc(z_ready, 1)

            def beside_even(step):
                if step in (2, 10):
                    rotate_even(3 + step // 8)
                if step in (3, 4, 5, 6):
                    lo_of("pooled", step - 3, z0(10 + step - 3))

            def even_out(k):
                src = group_bank("even", k)
                lo_of("eattn", k, src[:, :])

            dve.wait_ge(src_ready, 4)
            attention("even", even_out, beside_even)
            norm("mlp0", "g_mlp0", taken_from="eout")
            mlp(0)

            norm("odd", "g_odd", taken_from="down0")
            def conv(j):
                dve.wait_ge(z_ready, TILE0["oin"] + j + 1)
                cut_conv(z1(28 + j), z1(4 + j), (-2, -1, 0, 1), lambda i: g("conv_w", 4 * i + j), g("conv_b", j),
                         src_ready)

            def lru_decay(pos):
                u = LRU_UNITS[pos]
                dve.wait_ge(decay_made, 2 * pos + 2)
                e, r = decay_tmp(u), gate_tile(0, u)
                step(STT(r, e, 1.0, r, ALU.add, ALU.mult))
                STT(r, e, 1.0, r, ALU.add, ALU.mult).then_inc(beta_sq, 1)

            def states(u):
                return decay_tmp(u) if u < 4 else gate_tile(1, u)

            def lru_scan(pos):
                u = LRU_UNITS[pos]
                ig = gate_tile(1, u)
                step(TTn(ig, ig, z1(28 + u % 4), ALU.mult))
                dve.wait_ge(beta_made, pos + 1)
                step(TTn(ig, ig, gate_tile(0, u), ALU.mult))
                back = slice(None, None, -1) if u >= 4 else slice(None)
                ins = nc.vector.tensor_tensor_scan(states(u)[:, back], decay_tmp(u)[:, back], ig[:, back], 0.0,
                                                   ALU.mult, ALU.add)
                step(ins)

            def lru_sum(j):
                step(TTn(decay_tmp(j), decay_tmp(j), states(4 + j), ALU.add))

            def lru_gate(j):
                dve.wait_ge(gelu_made, j + 1)
                TTn(z1(8 + j), z1(8 + j), decay_tmp(j), ALU.mult).then_inc(src_ready, 1)

            for j in range(2):
                scaled("oin", j, z1(OIN[j]))
                conv(j)
            scaled("oin", 2, z1(OIN[2]))
            for j in range(2):
                lo_of("xc", j, z1(28 + j))
            scaled("oin", 3, z1(OIN[3]))
            conv(2)
            scaled("oin", 4, z1(OIN[4]))
            conv(3)
            scaled("oin", 5, z1(OIN[5]))
            for j in range(2, 4):
                lo_of("xc", j, z1(28 + j))
            dve.wait_ge(z_ready, TILE0["oin_b"])
            for i in range(2):
                scaled("oin_b", i, z1(OIN[6 + i]))
                lru_decay(2 * i)
                lru_decay(2 * i + 1)
            dve.wait_ge(z_ready, TILE0["oin_c"])
            for i in range(2):
                lru_scan(2 * i)
                lru_scan(2 * i + 1)
                scaled("oin_c", i, z1(OIN[8 + i]))
                lru_sum(i)
            lru_decay(4)
            lru_decay(5)
            for m in range(2):
                add_square("cq", m)
                lo_of("cq", m, z1(m), g("g_cq", m))
            scaled("oin_c", 2, z1(OIN[10]))
            lru_decay(6)
            lru_decay(7)
            add_square("ckv", 0)
            scaled("oin_c", 3, z1(OIN[11]))
            spread("cq", 1)
            spread("ckv", 2)
            STT(z1(2), z1(2), g("g_ckv"), rms[:, 2, :], ALU.mult, ALU.mult).then_inc(ckv_scaled, 1)
            dve.wait_ge(rope_in, 32)
            dve.wait_ge(z_ready, TILE0["oin_c"] + 4)
            rotate(5, z1(3), 96, 2, (tmp[:, 0, :], tmp[:, 1, :]))
            for h in range(MLA_HEADS):
                scaled("uq", h, mla_q[h], 1, 96)
                if h == 1:
                    lo_of("ckv", 0, z1(2))
                if h in (3, 5):
                    lru_scan(h // 2 * 2 + 3)
            for h in range(2):
                rotate(6 + h, mla_q[h], 96, 3 - h, (more[:, 2, :], more[:, 3, :]))

            def beside_mla(step):
                if step in (3, 7):
                    lru_scan(4 if step == 3 else 6)
                    lru_sum(2 + step // 4)
                if step in (1, 2, 5, 9):
                    lru_gate((1, 2, 5, 9).index(step))
                h = (step - 2) // 4 + 2
                if step % 4 == 2 and h < MLA_HEADS:
                    rotate(6 + h, mla_q[h], 96, 7, (more[:, 2, :], more[:, 3, :]))
                if 9 <= step < 13:
                    lo_of("lru", step - 9, z1(8 + step - 9))

            def mla_out(k):
                src = group_bank("mla", k)
                lo_of("mattn", k, src[:, :])

            attention("mla", mla_out, beside_mla)
            TTn(small[:, 12, :], g("g_final", 0, 8), g("g_mix2", 0, 8), ALU.mult).then_inc(src_ready, 1)
            values[0] += 4
            norm("mlp1", "g_mlp1", taken_from="oout")
            mlp(1)

            def second_norm():
                first = rtok[:, NORM["final"], :]
                step(TTn(small[:, 11, 4:8], first, first, ALU.mult))
                TTn(small[:, 11, 0:TT], small[:, 11, 4:8], bank[0][:, TT:2 * TT], ALU.mult).then_inc(src_ready, 1)

            norm("final", small[:, 12, :], taken_from="down1")
            spread("final", 1, then=second_norm)
            spread("mix2", gain=rtok[:, NORM["final"], :])
            def code_positions():
                for i in range(4):
                    kv, half = i // 2, i % 2
                    code = g("pe", CMP_BLOCK * kv + CMP_STRIDE * half, CMP_STRIDE).rearrange("p (o i) -> p o i", o=1)
                    n = SEQ // CMP_STRIDE - half
                    if half:
                        step(nc.vector.memset(tmp[:, i, CMP_STRIDE * n:], 0.0))
                    TTn(tmp[:, i, 0:CMP_STRIDE * n].rearrange("p (n i) -> p n i", i=CMP_STRIDE),
                        z2(11 + kv)[:, CMP_STRIDE * half:].rearrange("p (n i) -> p n i", i=CMP_STRIDE),
                        code.broadcast_to([P, n, CMP_STRIDE]), ALU.add).then_inc(src_ready, 1)
                for i in range(4):
                    lo_of("cmp", i, tmp[:, i, :])

            def gated_conv(j):
                step(TTn(z2(2 + j), z2(2 + j), z2(4 + j), ALU.mult))
                cut_conv(z2(4 + j), z2(2 + j), (-2, -1, 0), lambda i: g("conv2_w", 2 * i + j), g("conv2_b", j))
                step(TTn(z2(4 + j), z2(4 + j), z2(j), ALU.mult))

            for n, i in enumerate(ZIN):
                if i == 18:
                    dve.wait_ge(block_used, BLOCK_END[SUB0["cmp7"] // SUBS][1])
                gi = (i - 21) % 3
                if 21 <= i < 30 and gi:
                    src = taken("zin", n)
                    r = DILATIONS[gi]
                    TTn(residues(z2(i), r), dilate(src[:, :], r), dilate(rms[:, 0, :], r), ALU.mult).then_inc(z_ready, 1)
                else:
                    scaled("zin", n, z2(i))
                if n == 2:
                    dve.wait_ge(z_ready, TILE0["zin"] + 2)
                    code_positions()
                if HEAD < n <= HEAD + KT:
                    m = n - HEAD - 1
                    STT(x[:, m, :], x[:, m, :], g("g_final", m), rms[:, 1, :], ALU.mult, ALU.mult)
                if n == 9:
                    dve.wait_ge(gates_turned, 1)
                    step(nc.vector.tensor_copy(gates[:, :], bank[0][:, 0:TT * 32]))
                    TS(gates[:, 0:18:3], gates[:, 0:18:3], c("late"), None, ALU.mult).then_inc(gates_ready, 1)
                if 12 <= n < 17:
                    turn_values([z2((14, 16, 27, 28, 29)[n - 12])])
                if n == 15:
                    for kv in range(2):
                        dve.wait_ge(block_used, BLOCK_END[SUB0[f"cmp{4 * kv + 3}"] // SUBS][1])
                        step(nc.vector.tensor_copy(hid[:, kv, :], bank[2 + kv][:, 0:32]))
                        TTn(hid[:, kv, :], hid[:, kv, :], bank[2 + kv][:, 32:64], ALU.add).then_inc(hid_in, 1)
                if n in (17, 18):
                    dve.wait_ge(z_ready, TILE0["zin"] + 16)
                    gated_conv(n - 17)
                if n == 19:
                    for kv in range(2):
                        dve.wait_ge(hid_sig, kv + 1)
                        TTn(hid[:, kv, :], hid[:, kv, :], hid[:, 2 + kv, :], ALU.mult).then_inc(hid_made, 1)
                if n == 21:
                    dve.wait_ge(cmp_full, 1)
                    nc.vector.tensor_copy(cmpk[:, :], bank[2][:, 0:32]).then_inc(cmp_ready, 1)
                    dve.wait_ge(cmp_full, 2)
                    nc.vector.tensor_copy(cmpv[:, :], bank[3][0:32, 0:P]).then_inc(cmp_ready, 1)
                if n == 22:
                    for j in range(2):
                        dve.wait_ge(silu_made, 2 + j)
                        TTn(z2(4 + j), z2(4 + j), z2(6 + j), ALU.mult).then_inc(src_ready, 1)
            for j in range(2):
                lo_of("conv2", j, z2(4 + j))
            dve.wait_ge(silu_made, 9)

            def last_out(k):
                src = group_bank("last", k)
                if k < NSA_R:
                    TTn(z2(18 + k), src[:, :], z2(18 + k), ALU.mult).then_inc(o_out, 1)
                    lo_of("nsa", k, z2(18 + k))
                else:
                    r = DILATIONS[k - NSA_R]
                    TTn(dilate(z2(21 + k - NSA_R), r), residues(src[:, :], r), dilate(z2(30 + k - NSA_R), r),
                        ALU.mult).then_inc(o_out, 1)

            attention("last", last_out)
            dve.wait_ge(log_den, 1)
            first = 3 * TT * 2 * NSA_R
            step(TTn(rden[:, 24:48], rden[:, 0:24], negm[:, first:first + 24], ALU.subtract))
            nc.vector.tensor_copy(tmp[:, 0:3, :].rearrange("p a (b e) -> p (a b) e", e=64),
                                  rden[:, 24:48].rearrange("p (n o) -> p n o", o=1).broadcast_to([P, 24, 64])).then_inc(lse_ready, 1)
            dve.wait_ge(lse_full, 2)
            step(nc.vector.tensor_copy(tmp[:, 3, :], bank[0][:, :]))
            step(TTn(tmp[:, 3, :], tmp[:, 3, :], bank[1][:, :], ALU.max))
            dve.wait_ge(lse_full, 3)
            step(TTn(tmp[:, 3, :], tmp[:, 3, :], bank[2][:, :], ALU.max))
            for gi in range(3):
                TTn(z2(24 + gi), bank[gi][:, :], tmp[:, 3, :], ALU.subtract).then_inc(ls_max, 1)
            dve.wait_ge(lse_exp, 2)
            step(TTn(tmp[:, 4, :], z2(24), z2(25), ALU.add))
            dve.wait_ge(lse_exp, 3)
            TTn(tmp[:, 4, :], tmp[:, 4, :], z2(26), ALU.add).then_inc(ls_max, 1)
            for gi in range(3):
                mark(TTn(z2(24 + gi), z2(24 + gi), z2(21 + gi), ALU.mult))
            dve.wait_ge(lse_exp, 5)
            dve.wait_ge(vstep, steps[0])
            for gi in range(3):
                TTn(z2(30 + gi), z2(24 + gi), tmp[:, 5, :], ALU.mult).then_inc(src_ready, 1)
            for gi in range(3):
                lo_of("dil", gi, z2(30 + gi))
            for k in range(2):
                dve.wait_ge(mlp_hi, 2 * FF // P + k + 1)
                TTn(mlp_op[:, 1, k, :], arena[:, 24 + k, :], mlp_op[:, 0, k, :].bitcast(F32), ALU.subtract).then_inc(mlp_lo, 1)
            for m in range(KT):
                residual_tile("out2", m)
                lo_of("ple", m, x[:, m, :])
            for m in range(KT):
                src = taken("ple", 2 * m)
                nc.vector.tensor_copy(tmp[:, m % 2, :], src[:, :]).then_inc(z_ready, 1)
                src = taken("ple", 2 * m + 1)
                dve.wait_ge(ple_sig, m + 1)
                step(TTn(tmp[:, 2, :], src[:, :], tmp[:, m % 2, :], ALU.mult))
                TTn(x[:, m, :], x[:, m, :], tmp[:, 2, :], ALU.add).then_inc(z_ready, 1)
                if m:
                    add_square("out", m - 1)
            add_square("out", KT - 1)
            k = NORM["out"]
            dve.wait_ge(std_ready, k + 1)
            nc.vector.reciprocal(rtok[:, k, :], std[:, k, :]).then_inc(rtok_ready, 1)
            dve.wait_ge(rms_full, k + 1)
            for m in range(KT):
                STT(arena[:, m, :], x[:, m, :], g("g_out", m), bank[1][:, :], ALU.mult, ALU.mult).then_inc(y_ready, 1)


def sub_blocks(w, cols=None):
    k, _ = w.shape
    if cols is not None:
        wide = np.zeros((k, len(cols)), w.dtype)
        there = np.asarray(cols) >= 0
        wide[:, there] = w[:, np.asarray(cols)[there]]
        w = wide
    m = w.shape[1]
    if m % P:
        w = np.concatenate([w, np.zeros((k, P - m % P), w.dtype)], axis=1)
    return w.reshape(k // P, P, -1, P).transpose(2, 0, 1, 3)


def pair_diagonal(w):
    n, a, b = w.shape
    out = np.zeros((n, 2 * a, 2 * b), w.dtype)
    out[:, :a, :b] = w
    out[:, a:, b:] = w
    return out


def padded(blocks):
    blocks = blocks.reshape(-1, P, P)
    short = -len(blocks) % SUBS
    return np.concatenate([blocks, np.zeros((short, P, P), blocks.dtype)]) if short else blocks


def heads(n_pairs, stride, offset=0, dh=64):
    return [offset + dh * (j + stride * s) + i for j in range(n_pairs) for s in range(2) for i in range(dh)]


def weight_stream(a):
    span = lambda lo, n: list(range(lo, lo + n))
    out = []
    ein = heads(4, 4) + span(512, 768)
    out.append(padded(sub_blocks(a["e_w_in"][0], ein)[EIN]))
    out.append(padded(a["e_w_pool"][0]))
    rows = heads(4, 4) + span(512, 512)
    out.append(padded(sub_blocks(a["e_w_out"][0][rows])))

    def mlp(layer):
        out.append(padded(sub_blocks(a["w_mlp1"][layer])))
        out.append(padded(sub_blocks(a["w_mlp2"][layer]).transpose(1, 0, 2, 3)))

    mlp(0)
    oin = span(0, 384) + [-1] * 64 + span(384, 32) + [-1] * 32 + span(416, 1024)
    oin = sub_blocks(a["o_w_in"][0], oin)[OIN]
    gates = np.stack([a["o_lru_wa"][0], a["o_lru_wx"][0]], axis=1)
    lru = np.zeros((2, 2, 4, P, P), gates.dtype)
    lru[:, :, :, :64, :64] = gates[:, :, 0::2]
    lru[:, :, :, 64:, 64:] = gates[:, :, 1::2]
    lru = np.stack([lru[u // 4, kind, u % 4] for u in LRU_UNITS for kind in range(2)])
    out += [padded(part) for part in (oin[:6], lru[:8], oin[6:8], lru[8:], oin[8:])]
    uq = [96 * h + i if i < 96 else -1 for h in range(MLA_HEADS) for i in range(P)]
    out.append(padded(sub_blocks(a["o_w_uq"][0], uq)))
    ukn = [P * h + i if i < 64 else -1 for h in range(MLA_HEADS) for i in range(P)]
    out.append(padded(sub_blocks(a["o_w_ukv"][0], ukn)))
    uv = [P * h + 64 + i for h in range(MLA_HEADS) for i in range(64)]
    out.append(padded(sub_blocks(a["o_w_ukv"][0], uv)))
    out.append(padded(sub_blocks(a["o_w_out"][0])))
    mlp(1)
    q0 = 1024
    g0 = q0 + 384 + 6 * 128
    zin = (span(0, 1024) + heads(3, 3, q0) + span(q0 + 384, 768) + span(g0, 18) + [-1] * 110
           + heads(3, 3, g0 + 18) + span(g0 + 18 + 384, 4 * 384))
    tiles = sub_blocks(a["w_in_2"][0], zin)[ZIN]
    out.append(padded(tiles[:6]))
    compression = np.concatenate([pair_diagonal(a["cmp_w1_2"][0, kv].reshape(CMP_BLOCK, HD, HD)) for kv in range(2)])
    for i in range(8):
        out += [padded(tiles[6 + i]), padded(compression[SUBS * i:SUBS * (i + 1)])]
    out.append(padded(tiles[14:]))
    rows = span(0, 256) + heads(3, 3, 256) + span(640, 384)
    out.append(padded(sub_blocks(a["w_out_2"][0][rows])))
    gate, proj = sub_blocks(a["w_ple_gate_2"][0]), sub_blocks(a["w_ple_proj_2"][0])
    out.append(padded(np.concatenate([gate, proj], axis=1)))
    stream = np.concatenate(out)
    assert len(stream) == NBLOCKS * SUBS
    return np.ascontiguousarray(stream.reshape(NBLOCKS, SUBS, P, P).transpose(0, 2, 1, 3)).reshape(NBLOCKS, P, D)


def small_params(a):
    tiles = lambda v: v.reshape(-1, P).T
    pe = a["cmp_pe_2"][0].transpose(2, 0, 1).reshape(HD, 2 * CMP_BLOCK)
    w2 = pair_diagonal(a["cmp_w2_2"][0])
    bias = np.stack([a["o_lru_ba"][0], a["o_lru_bx"][0]], axis=1)
    parts = dict(g_even=tiles(a["e_norm_mix"][0]), g_mlp0=tiles(a["norm_mlp"][0]), g_odd=tiles(a["o_norm_mix"][0]),
                 g_mlp1=tiles(a["norm_mlp"][1]), g_final=tiles(a["final_norm"]), g_mix2=tiles(a["norm_mix_2"][0]),
                 g_out=tiles(a["norm_final_2"]), g_cq=tiles(a["o_g_cq"][0]), g_ckv=tiles(a["o_g_ckv"][0]),
                 pool_scale=tiles(a["e_pool_scale"][0]), conv_w=tiles(a["o_conv_w"][0]), conv_b=tiles(a["o_conv_b"][0]),
                 gate_b=tiles(bias), lam=tiles(a["o_lru_lambda"][0]), conv2_w=tiles(a["conv_w_2"][0]),
                 conv2_b=tiles(a["conv_b_2"][0]), pe=np.concatenate([pe, pe]),
                 sink=np.broadcast_to(a["e_sink"][0], (P, 8)), w2k=w2[0], w2v=w2[1])
    return np.ascontiguousarray(np.concatenate([parts[n].reshape(P, w) for n, w in PARAM_COLS], axis=1))


def small_consts():
    p = np.arange(P)[:, None]
    mask = lambda ok: np.where(ok, 0.0, NEG)
    c = np.arange(640)[None]
    band = np.arange(384)[None]
    near = np.arange(256)[None]
    b = np.arange(P)[None]
    tok = (np.arange(TT) * P)[None, :, None] + p[:, :, None]
    n = np.arange(32)[None, None, :]
    rot = np.zeros((2, P, P))
    for first, half, which in ((0, 32, 0), (64, 32, 0), (64, 16, 1)):
        for i in range(half):
            rot[which, first + half + i, first + i] = -1.0
            rot[which, first + i, first + half + i] = 1.0
    parts = dict(causal=mask(c - 512 <= p), band=mask(np.abs(band - P - p) <= 128),
                 near=mask((p + P - near >= 0) & (p + P - near <= 128)),
                 blocks=mask((p // 32 == b // 32) & (b <= p)),
                 cmpmask=mask(CMP_STRIDE * n + CMP_BLOCK - 1 <= tok).reshape(P, TT * 32),
                 ident=np.eye(P), rot_even=rot[0], rot_mla=rot[1], late=(p >= CMP_BLOCK - 1) * 1.0,
                 ones=np.ones((P, 1)), eps=np.full((P, 1), EPS))
    return np.concatenate([parts[k].reshape(P, w) for k, w in CONST_COLS], axis=1).astype(np.float32)


def rope_tables():
    out = np.zeros((2, P, 2, SEQ), np.float32)
    out[1, :64, 0] = 1.0
    for layer, first, half, n in ((0, 0, 32, 4), (1, 64, 16, 2)):
        inv = np.float32(10000.0) ** (-np.arange(half, dtype=np.float32) / np.float32(half))
        ang = np.arange(SEQ, dtype=np.float32)[None] * inv[:, None]
        for j in range(n):
            out[layer, first + half * j:first + half * (j + 1), 0] = np.cos(ang)
            out[layer, first + half * j:first + half * (j + 1), 1] = np.sin(ang)
    return out


def window_counts():
    t = np.arange(SEQ)
    rows = [1.0 / (np.clip(t + w // 2, 0, SEQ) - np.clip(t - w // 2, 0, SEQ)) for w in (2, 4, 8, 16)]
    return np.ascontiguousarray(np.broadcast_to(np.stack(rows)[None], (P, 4, SEQ))).astype(np.float32)


def kernel(**inputs):
    import concourse.bacc as bacc
    from concourse.bass_utils import run_bass_kernel_spmd

    a = {k: np.asarray(v) for k, v in inputs.items()}
    arrays = dict(x_t=np.ascontiguousarray(a["x"][0].T), stream=weight_stream(a), params=small_params(a),
                  consts=small_consts(), ropes=rope_tables(), invcnt=window_counts(),
                  p_t=np.ascontiguousarray(a["p_2"][0, 0].T))
    nc = bacc.Bacc("TRN2", target_bir_lowering=False, num_devices=1)
    args = {n: nc.dram_tensor(n + "_dram", v.shape, mybir.dt.from_np(v.dtype), kind="ExternalInput").ap()
            for n, v in arrays.items()}
    out = nc.dram_tensor("out_t_dram", (D, SEQ), F32, kind="ExternalOutput").ap()
    program(nc, out_t=out, **args)
    r = run_bass_kernel_spmd(nc, [{n + "_dram": v for n, v in arrays.items()}], core_ids=[0])
    return np.ascontiguousarray(r.results[0]["out_t_dram"].T)[None]
```
